# Optimizing a Trainium2 kernel written in Bass

```python
import jax, jax.numpy as jnp
from jax import lax
import numpy as np
import math

D_MODEL = 2048
BATCH = 1
SEQ = 256
DEPTH = 1

D_MIX = D_MODEL
D_SSD = D_MIX // 2
SSD_HEAD_DIM = 64
SSD_HEADS = D_SSD // SSD_HEAD_DIM
SSD_GROUPS = 2
SSD_HEADS_PER_GROUP = SSD_HEADS // SSD_GROUPS
SSD_STATE = 128
SSD_CONV = 5
SSD_CHUNK = 128
SSD_CONV_DIM = D_SSD + 2 * SSD_GROUPS * SSD_STATE
D_POOL = D_MIX - D_SSD
POOL_WINDOWS = (2, 4, 8, 16)
POOL_GROUPS = len(POOL_WINDOWS)
POOL_GROUP_DIM = D_POOL // POOL_GROUPS
D_IN_PROJ = D_SSD + SSD_CONV_DIM + 2 * SSD_HEADS + D_POOL
D_FF = 5632
FFN_CONV = 3
D_PLE = 256
EPS = 1e-6


F32 = jnp.float32

def rmsnorm(x, g):
    xf = x.astype(F32)
    y = xf * lax.rsqrt(jnp.mean(xf * xf, axis=-1, keepdims=True) + EPS)
    return (y * g.astype(F32)).astype(x.dtype)

def dwconv_centred(u, w, bias):
    k = w.shape[0]
    L = u.shape[1]
    half = k // 2
    up = jnp.pad(u, ((0, 0), (half, half), (0, 0)))
    wf = w.astype(u.dtype)
    y = up[:, 0:L] * wf[0]
    for j in range(1, k):
        y = y + up[:, j:j + L] * wf[j]
    return y + bias.astype(u.dtype)

def ssd_scan(xs, dt, a, bm, cm):
    b, L, g, e, pdim = xs.shape
    n = bm.shape[-1]
    c = L // SSD_CHUNK
    q = SSD_CHUNK
    xdt = (xs.astype(F32) * dt[..., None]).reshape(b, c, q, g, e, pdim)
    da = jnp.moveaxis((dt * a).reshape(b, c, q, g, e), 2, -1)
    acum = jnp.cumsum(da, axis=-1)
    bmc = bm.astype(F32).reshape(b, c, q, g, n)
    cmc = cm.astype(F32).reshape(b, c, q, g, n)
    causal = jnp.tril(jnp.ones((q, q), dtype=bool))
    seg = acum[..., :, None] - acum[..., None, :]
    decay = jnp.exp(jnp.where(causal, seg, -jnp.inf))
    cb = jnp.einsum("bclgn,bcsgn->bcgls", cmc, bmc)
    y_diag = jnp.einsum("bcgls,bcgels,bcsgep->bclgep", cb, decay, xdt)
    decay_to_end = jnp.exp(acum[..., -1:] - acum)
    states = jnp.einsum("bclgn,bcgel,bclgep->bcgepn", bmc, decay_to_end, xdt)
    chunk_decay = jnp.exp(acum[..., -1])

    def step(h, inp):
        s, d = inp
        return h * d[..., None, None] + s, h

    h0 = jnp.zeros((b, g, e, pdim, n), F32)
    _, h_in = lax.scan(step, h0, (jnp.moveaxis(states, 1, 0), jnp.moveaxis(chunk_decay, 1, 0)))
    h_in = jnp.moveaxis(h_in, 0, 1)
    y_off = jnp.einsum("bclgn,bcgepn,bcgel->bclgep", cmc, h_in, jnp.exp(acum))
    return (y_diag + y_off).reshape(b, L, g, e, pdim)

def ssd_mixer(z, xbc, dt_raw, conv_w, conv_b, dt_bias, a_log, d_skip, norm_w):
    b, L, _ = z.shape
    G, E = SSD_GROUPS, SSD_HEADS_PER_GROUP
    xbc = jax.nn.silu(dwconv_centred(xbc, conv_w, conv_b))
    xs, bm, cm = jnp.split(xbc, [D_SSD, D_SSD + G * SSD_STATE], axis=-1)
    xs = xs.reshape(b, L, G, E, SSD_HEAD_DIM)
    bm = bm.reshape(b, L, G, SSD_STATE)
    cm = cm.reshape(b, L, G, SSD_STATE)
    dt = jax.nn.softplus(dt_raw.astype(F32).reshape(b, L, 2, SSD_HEADS) + dt_bias.astype(F32))
    dt = dt.reshape(b, L, 2, G, E)
    a = (-jnp.exp(a_log.astype(F32))).reshape(2, G, E)
    flip = lambda t: jnp.flip(t, axis=1)
    y_fwd = ssd_scan(xs, dt[:, :, 0], a[0], bm, cm)
    y_bwd = flip(ssd_scan(flip(xs), flip(dt[:, :, 1]), a[1], flip(bm), flip(cm)))
    y = y_fwd + y_bwd + xs.astype(F32) * d_skip.astype(F32).reshape(G, E)[:, :, None]
    y = y.reshape(b, L, D_SSD) * jax.nn.silu(z.astype(F32))
    y = y.reshape(b, L, G, D_SSD // G)
    y = y * lax.rsqrt(jnp.mean(y * y, axis=-1, keepdims=True) + EPS)
    return (y.reshape(b, L, D_SSD) * norm_w.astype(F32)).astype(z.dtype)

def pool_mixer(u, w, scale):
    b, L, _ = u.shape
    uf = u.astype(F32).reshape(b, L, POOL_GROUPS, POOL_GROUP_DIM)
    cs = jnp.concatenate([jnp.zeros((b, 1, POOL_GROUPS, POOL_GROUP_DIM), F32),
                          jnp.cumsum(uf, axis=1)], axis=1)
    t = jnp.arange(L)
    means = []
    for gi, k in enumerate(POOL_WINDOWS):
        lo = jnp.clip(t - k // 2, 0, L)
        hi = jnp.clip(t + (k - k // 2), 0, L)
        csg = cs[:, :, gi]
        cnt = (hi - lo).astype(F32)[None, :, None]
        means.append((csg[:, hi] - csg[:, lo]) / cnt)
    mixed = jnp.stack(means, axis=2) - uf
    y = jnp.einsum("blgc,gcd->blgd", mixed, w.astype(F32))
    return (y.reshape(b, L, D_POOL) * scale.astype(F32)).astype(u.dtype)

def conv_glu(hn, w_up, conv_w, conv_b, w_down):
    up = hn @ w_up
    gate, val = jnp.split(up, 2, axis=-1)
    gate = dwconv_centred(gate, conv_w, conv_b)
    return (jax.nn.gelu(gate, approximate=True) * val) @ w_down

def first_inputs(seed: int = 0) -> dict:
    key = jax.random.key(seed)
    ks = jax.random.split(key, 24)
    nrm = lambda k, shape, s: jax.random.normal(k, shape, F32) * s
    gain = lambda k: 1.0 + 0.02 * jax.random.normal(k, (DEPTH, D_MODEL), F32)
    dt0 = jnp.exp(jax.random.uniform(ks[6], (DEPTH, 2, SSD_HEADS), F32,
                                     np.log(1e-3).astype(np.float32), np.log(1e-1).astype(np.float32)))
    dt_bias = dt0 + jnp.log(-jnp.expm1(-dt0))
    return {
        "x": jax.random.normal(ks[0], (BATCH, SEQ, D_MODEL), F32),
        "p": jax.random.normal(ks[1], (DEPTH, BATCH, SEQ, D_PLE), F32),
        "mix_norm_pre": gain(ks[2]),
        "mix_norm_post": gain(ks[3]),
        "w_in": nrm(ks[4], (DEPTH, D_MODEL, D_IN_PROJ), D_MODEL ** -0.5),
        "ssd_conv_w": nrm(ks[5], (DEPTH, SSD_CONV, SSD_CONV_DIM), SSD_CONV ** -0.5),
        "ssd_conv_b": nrm(ks[7], (DEPTH, SSD_CONV_DIM), 0.02),
        "ssd_dt_bias": dt_bias,
        "ssd_a_log": jnp.log(jax.random.uniform(ks[8], (DEPTH, 2, SSD_HEADS), F32, 1.0, 16.0)),
        "ssd_d": 1.0 + 0.1 * jax.random.normal(ks[9], (DEPTH, SSD_HEADS), F32),
        "ssd_norm": 1.0 + 0.02 * jax.random.normal(ks[10], (DEPTH, D_SSD), F32),
        "pool_w": nrm(ks[11], (DEPTH, POOL_GROUPS, POOL_GROUP_DIM, POOL_GROUP_DIM), POOL_GROUP_DIM ** -0.5),
        "pool_scale": 1.0 + 0.1 * jax.random.normal(ks[12], (DEPTH, D_POOL), F32),
        "w_out": nrm(ks[13], (DEPTH, D_MIX, D_MODEL), D_MIX ** -0.5),
        "ffn_norm_pre": gain(ks[14]),
        "ffn_norm_post": gain(ks[15]),
        "w_ffn_up": nrm(ks[16], (DEPTH, D_MODEL, 2 * D_FF), D_MODEL ** -0.5),
        "ffn_conv_w": nrm(ks[17], (DEPTH, FFN_CONV, D_FF), FFN_CONV ** -0.5),
        "ffn_conv_b": nrm(ks[18], (DEPTH, D_FF), 0.02),
        "w_ffn_down": nrm(ks[19], (DEPTH, D_FF, D_MODEL), D_FF ** -0.5),
        "ple_norm_pre": gain(ks[20]),
        "w_ple_gate": nrm(ks[21], (DEPTH, D_MODEL, D_MODEL), D_MODEL ** -0.5),
        "w_ple": nrm(ks[22], (DEPTH, D_PLE, D_MODEL), D_PLE ** -0.5),
        "ple_norm_post": gain(ks[23]),
    }

def first_block(x, p, mix_norm_pre, mix_norm_post, w_in, ssd_conv_w, ssd_conv_b, ssd_dt_bias,
              ssd_a_log, ssd_d, ssd_norm, pool_w, pool_scale, w_out, ffn_norm_pre, ffn_norm_post,
              w_ffn_up, ffn_conv_w, ffn_conv_b, w_ffn_down, ple_norm_pre, w_ple_gate, w_ple,
              ple_norm_post):
    h = x
    split_at = [D_SSD, D_SSD + SSD_CONV_DIM, D_SSD + SSD_CONV_DIM + 2 * SSD_HEADS]
    for i in range(DEPTH):
        hn = rmsnorm(h, mix_norm_pre[i])
        proj = hn @ w_in[i]
        z, xbc, dt_raw, u = jnp.split(proj, split_at, axis=-1)
        y_ssd = ssd_mixer(z, xbc, dt_raw, ssd_conv_w[i], ssd_conv_b[i], ssd_dt_bias[i],
                          ssd_a_log[i], ssd_d[i], ssd_norm[i])
        y_pool = pool_mixer(u, pool_w[i], pool_scale[i])
        mix = jnp.concatenate([y_ssd, y_pool], axis=-1) @ w_out[i]
        h = h + rmsnorm(mix, mix_norm_post[i])
        hn = rmsnorm(h, ffn_norm_pre[i])
        ff = conv_glu(hn, w_ffn_up[i], ffn_conv_w[i], ffn_conv_b[i], w_ffn_down[i])
        h = h + rmsnorm(ff, ffn_norm_post[i])
        gate = jax.nn.sigmoid(rmsnorm(h, ple_norm_pre[i]) @ w_ple_gate[i])
        h = h + rmsnorm(gate * (p[i] @ w_ple[i]), ple_norm_post[i])
    return h


CTX_LEN = 256
GRID_W = 64
Q_BLOCK = 128
ROPE_THETA = 10000.0
ADA_CHUNKS = 6

A_HEADS = 16
A_KV_HEADS = 4
A_HEAD_DIM = 128
B_HEADS = 8
B_HEAD_DIM = 64
B_V_DIM = 2 * B_HEAD_DIM

A_Q = A_HEADS * A_HEAD_DIM
A_KV = A_KV_HEADS * A_HEAD_DIM
B_QK = B_HEADS * 2 * B_HEAD_DIM
B_V = B_HEADS * B_V_DIM
KV_WIDTH = 2 * A_KV + B_QK + B_V
IN_WIDTH = KV_WIDTH + A_Q + B_QK + 2 * D_MODEL

D_FF_2 = -(-8 * D_MODEL // (3 * 256)) * 256


def rms_norm(x, g):
    xf = x.astype(jnp.float32)
    y = xf * lax.rsqrt(jnp.mean(xf * xf, axis=-1, keepdims=True) + EPS)
    return (y * g.astype(jnp.float32)).astype(x.dtype)

def modulate(h, shift, scale):
    return h * (1 + scale) + shift

def adaln(cond, w_ada, b_ada):
    return jnp.split(jax.nn.silu(cond) @ w_ada + b_ada, ADA_CHUNKS, axis=-1)

def axial_rope(rows, head_dim):
    n_freq = head_dim // 4
    freqs = ROPE_THETA ** (-jnp.arange(n_freq, dtype=jnp.float32) / n_freq)
    row = jnp.repeat(jnp.arange(rows, dtype=jnp.float32), GRID_W)
    col = jnp.tile(jnp.arange(GRID_W, dtype=jnp.float32), rows)
    ang = jnp.concatenate([row[:, None] * freqs, col[:, None] * freqs], axis=-1)
    return jnp.cos(ang), jnp.sin(ang)

def apply_rope(x, cos, sin):
    half = x.shape[-1] // 2
    shape = (cos.shape[0],) + (1,) * (x.ndim - 3) + (half,)
    cos = cos.reshape(shape).astype(x.dtype)
    sin = sin.reshape(shape).astype(x.dtype)
    x1, x2 = x[..., :half], x[..., half:]
    return jnp.concatenate([x1 * cos - x2 * sin, x2 * cos + x1 * sin], axis=-1)

def split_kv(p_kv, k_norm_a, k_norm_b):
    b, n = p_kv.shape[:2]
    k_a, v_a, k_b, v_b = jnp.split(p_kv, [A_KV, 2 * A_KV, 2 * A_KV + B_QK], axis=-1)
    k_a = rms_norm(k_a.reshape(b, n, A_KV_HEADS, A_HEAD_DIM), k_norm_a)
    v_a = v_a.reshape(b, n, A_KV_HEADS, A_HEAD_DIM)
    k_b = rms_norm(k_b.reshape(b, n, B_HEADS, 2, B_HEAD_DIM), k_norm_b)
    v_b = v_b.reshape(b, n, B_HEADS, B_V_DIM)
    return k_a, v_a, k_b, v_b

def split_qg(p_qg, q_norm_a, q_norm_b):
    b, n = p_qg.shape[:2]
    q_a, q_b, g_a, g_b = jnp.split(p_qg, [A_Q, A_Q + B_QK, A_Q + B_QK + D_MODEL], axis=-1)
    q_a = rms_norm(q_a.reshape(b, n, A_HEADS, A_HEAD_DIM), q_norm_a)
    q_b = rms_norm(q_b.reshape(b, n, B_HEADS, 2, B_HEAD_DIM), q_norm_b)
    return q_a, q_b, g_a, g_b

def gqa(q, k, v):
    b, n, hq, d = q.shape
    hkv = k.shape[2]
    qg = q.reshape(b, n, hkv, hq // hkv, d)
    s = jnp.einsum('bnkgd,bmkd->bkgnm', qg, k).astype(jnp.float32) * (d ** -0.5)
    p = jax.nn.softmax(s, axis=-1).astype(v.dtype)
    o = jnp.einsum('bkgnm,bmkd->bnkgd', p, v)
    return o.reshape(b, n, hq * d)

def diff_attn(q, k, v, lam, lam_init, subln_g):
    b, n, h, _, dh = q.shape
    s = jnp.einsum('bnhid,bmhid->bhinm', q, k).astype(jnp.float32) * (dh ** -0.5)
    p = jax.nn.softmax(s, axis=-1)
    a = (p[:, :, 0] - lam * p[:, :, 1]).astype(v.dtype)
    o = jnp.einsum('bhnm,bmhe->bnhe', a, v)
    o = rms_norm(o, subln_g) * (1 - lam_init)
    return o.reshape(b, n, h * B_V_DIM)

def sweep_query_blocks(attn_fn, q):
    b, s = q.shape[:2]
    nblk = s // Q_BLOCK
    qb = jnp.moveaxis(q.reshape((b, nblk, Q_BLOCK) + q.shape[2:]), 1, 0)
    o = lax.map(attn_fn, qb)
    return jnp.moveaxis(o, 0, 1).reshape(b, s, o.shape[-1])

def merge_branches(o_a, o_b, g_a, g_b, w_br_a, w_br_b, w_out):
    merged = jax.nn.sigmoid(g_a) * (o_a @ w_br_a) + jax.nn.sigmoid(g_b) * (o_b @ w_br_b)
    return merged @ w_out

def swiglu_sublayer(x, shift, scale, gate, norm_g, w_ff_gate, w_ff_up, w_ff_down):
    h = modulate(rms_norm(x, norm_g), shift, scale)
    return x + gate * ((jax.nn.silu(h @ w_ff_gate) * (h @ w_ff_up)) @ w_ff_down)

def second_inputs(seed: int = 0) -> dict:
    key = jax.random.key(seed)
    ks = jax.random.split(key, 24)
    f32 = jnp.float32
    L = DEPTH

    def w(k, shape, fan_in, s=1.0):
        return jax.random.normal(k, shape, f32) * (s * fan_in ** -0.5)

    def gain(k, shape):
        return 1.0 + 0.05 * jax.random.normal(k, shape, f32)

    return {
        'x': jax.random.normal(ks[0], (BATCH, SEQ, D_MODEL), f32),
        'c': jax.random.normal(ks[1], (BATCH, D_MODEL), f32),
        'ctx': jax.random.normal(ks[2], (BATCH, CTX_LEN, D_MODEL), f32),
        'c_ctx': jax.random.normal(ks[3], (D_MODEL,), f32),
        'w_ada': w(ks[4], (L, D_MODEL, ADA_CHUNKS * D_MODEL), D_MODEL, 0.5),
        'b_ada': 0.02 * jax.random.normal(ks[5], (L, ADA_CHUNKS * D_MODEL), f32),
        'norm1_g': gain(ks[6], (L, D_MODEL)),
        'w_in': w(ks[7], (L, D_MODEL, IN_WIDTH), D_MODEL),
        'q_norm_a': gain(ks[8], (L, A_HEAD_DIM)),
        'k_norm_a': gain(ks[9], (L, A_HEAD_DIM)),
        'q_norm_b': gain(ks[10], (L, B_HEAD_DIM)),
        'k_norm_b': gain(ks[11], (L, B_HEAD_DIM)),
        'lam_q1': 0.1 * jax.random.normal(ks[12], (L, B_HEAD_DIM), f32),
        'lam_k1': 0.1 * jax.random.normal(ks[13], (L, B_HEAD_DIM), f32),
        'lam_q2': 0.1 * jax.random.normal(ks[14], (L, B_HEAD_DIM), f32),
        'lam_k2': 0.1 * jax.random.normal(ks[15], (L, B_HEAD_DIM), f32),
        'subln_g': gain(ks[16], (L, B_V_DIM)),
        'w_br_a': w(ks[17], (L, A_Q, D_MODEL), A_Q),
        'w_br_b': w(ks[18], (L, B_V, D_MODEL), B_V),
        'w_out': w(ks[19], (L, D_MODEL, D_MODEL), D_MODEL),
        'norm2_g': gain(ks[20], (L, D_MODEL)),
        'w_ff_gate': w(ks[21], (L, D_MODEL, D_FF_2), D_MODEL),
        'w_ff_up': w(ks[22], (L, D_MODEL, D_FF_2), D_MODEL),
        'w_ff_down': w(ks[23], (L, D_FF_2, D_MODEL), D_FF_2),
    }

def second_block(x, c, ctx, c_ctx, w_ada, b_ada, norm1_g, w_in, q_norm_a, k_norm_a, q_norm_b, k_norm_b,
              lam_q1, lam_k1, lam_q2, lam_k2, subln_g, w_br_a, w_br_b, w_out, norm2_g,
              w_ff_gate, w_ff_up, w_ff_down):
    rows = x.shape[1] // GRID_W
    cos_a, sin_a = axial_rope(rows, A_HEAD_DIM)
    cos_b, sin_b = axial_rope(rows, B_HEAD_DIM)

    for l in range(DEPTH):
        last = l == DEPTH - 1
        lam_init = 0.8 - 0.6 * math.exp(-0.3 * l)
        lam = (jnp.exp(jnp.sum(lam_q1[l].astype(jnp.float32) * lam_k1[l].astype(jnp.float32)))
               - jnp.exp(jnp.sum(lam_q2[l].astype(jnp.float32) * lam_k2[l].astype(jnp.float32)))
               + lam_init)
        m_lat = [m[:, None, :] for m in adaln(c, w_ada[l], b_ada[l])]
        m_ctx = adaln(c_ctx, w_ada[l], b_ada[l])
        w_in_l = w_in[l]

        hc = modulate(rms_norm(ctx, norm1_g[l]), m_ctx[0], m_ctx[1])
        pc = hc @ (w_in_l[:, :KV_WIDTH] if last else w_in_l)
        ka_c, va_c, kb_c, vb_c = split_kv(pc[..., :KV_WIDTH], k_norm_a[l], k_norm_b[l])

        h = modulate(rms_norm(x, norm1_g[l]), m_lat[0], m_lat[1])
        p = h @ w_in_l
        ka, va, kb, vb = split_kv(p[..., :KV_WIDTH], k_norm_a[l], k_norm_b[l])
        qa, qb, ga, gb = split_qg(p[..., KV_WIDTH:], q_norm_a[l], q_norm_b[l])
        qa = apply_rope(qa, cos_a, sin_a)
        ka = apply_rope(ka, cos_a, sin_a)
        qb = apply_rope(qb, cos_b, sin_b)
        kb = apply_rope(kb, cos_b, sin_b)

        ka_all = jnp.concatenate([ka_c, ka], axis=1)
        va_all = jnp.concatenate([va_c, va], axis=1)
        kb_all = jnp.concatenate([kb_c, kb], axis=1)
        vb_all = jnp.concatenate([vb_c, vb], axis=1)
        sg = subln_g[l]
        oa = sweep_query_blocks(lambda qblk: gqa(qblk, ka_all, va_all), qa)
        ob = sweep_query_blocks(lambda qblk: diff_attn(qblk, kb_all, vb_all, lam, lam_init, sg), qb)
        x_new = x + m_lat[2] * merge_branches(oa, ob, ga, gb, w_br_a[l], w_br_b[l], w_out[l])
        x_new = swiglu_sublayer(x_new, m_lat[3], m_lat[4], m_lat[5], norm2_g[l],
                                w_ff_gate[l], w_ff_up[l], w_ff_down[l])

        if not last:
            qa_c, qb_c, ga_c, gb_c = split_qg(pc[..., KV_WIDTH:], q_norm_a[l], q_norm_b[l])
            oa_c = gqa(qa_c, ka_c, va_c)
            ob_c = diff_attn(qb_c, kb_c, vb_c, lam, lam_init, sg)
            ctx = ctx + m_ctx[2] * merge_branches(oa_c, ob_c, ga_c, gb_c, w_br_a[l], w_br_b[l], w_out[l])
            ctx = swiglu_sublayer(ctx, m_ctx[3], m_ctx[4], m_ctx[5], norm2_g[l],
                                  w_ff_gate[l], w_ff_up[l], w_ff_down[l])
        x = x_new
    return x


def setup_inputs(seed=0):
    out = dict(first_inputs(seed))
    for name, value in second_inputs(seed + 1).items():
        if name != "x":
            out[name + "_2"] = value
    return out


def reference(
    x, p, mix_norm_pre, mix_norm_post, w_in, ssd_conv_w, ssd_conv_b, ssd_dt_bias, ssd_a_log,
    ssd_d, ssd_norm, pool_w, pool_scale, w_out, ffn_norm_pre, ffn_norm_post, w_ffn_up,
    ffn_conv_w, ffn_conv_b, w_ffn_down, ple_norm_pre, w_ple_gate, w_ple, ple_norm_post, c_2,
    ctx_2, c_ctx_2, w_ada_2, b_ada_2, norm1_g_2, w_in_2, q_norm_a_2, k_norm_a_2, q_norm_b_2,
    k_norm_b_2, lam_q1_2, lam_k1_2, lam_q2_2, lam_k2_2, subln_g_2, w_br_a_2, w_br_b_2, w_out_2,
    norm2_g_2, w_ff_gate_2, w_ff_up_2, w_ff_down_2,
):
    x = first_block(
        x, p, mix_norm_pre, mix_norm_post, w_in, ssd_conv_w, ssd_conv_b, ssd_dt_bias, ssd_a_log,
        ssd_d, ssd_norm, pool_w, pool_scale, w_out, ffn_norm_pre, ffn_norm_post, w_ffn_up,
        ffn_conv_w, ffn_conv_b, w_ffn_down, ple_norm_pre, w_ple_gate, w_ple, ple_norm_post,
    )
    return second_block(
        x, c_2, ctx_2, c_ctx_2, w_ada_2, b_ada_2, norm1_g_2, w_in_2, q_norm_a_2, k_norm_a_2,
        q_norm_b_2, k_norm_b_2, lam_q1_2, lam_k1_2, lam_q2_2, lam_k2_2, subln_g_2, w_br_a_2,
        w_br_b_2, w_out_2, norm2_g_2, w_ff_gate_2, w_ff_up_2, w_ff_down_2,
    )


_drawn_inputs = setup_inputs


def setup_inputs(seed=0):
    import zlib

    import numpy as np

    out = dict(_drawn_inputs(seed))
    spreads = {}
    factors = {'mix_norm_pre': 2.873,
     'mix_norm_post': 4.014,
     'ssd_conv_b': 3.487,
     'ssd_norm': 5.435,
     'ffn_norm_pre': 3.765,
     'ffn_norm_post': 5.338,
     'ffn_conv_b': 5.509,
     'ple_norm_pre': 8.0,
     'ple_norm_post': 5.733,
     'ctx_2': 3.539,
     'b_ada_2': 5.281,
     'norm1_g_2': 8.0,
     'q_norm_a_2': 8.0,
     'k_norm_a_2': 8.0,
     'q_norm_b_2': 8.0,
     'k_norm_b_2': 8.0,
     'lam_q1_2': 8.0,
     'lam_k1_2': 7.566,
     'lam_q2_2': 8.0,
     'lam_k2_2': 8.0,
     'subln_g_2': 41.892,
     'norm2_g_2': 7.599,
     'ssd_d': 8.0}
    for name, (base, spread) in spreads.items():
        noise = np.random.default_rng([zlib.crc32(name.encode()), seed]).standard_normal(out[name].shape)
        drawn = base * np.exp(spread * noise) if base else spread * noise
        out[name] = __import__('jax').numpy.asarray(drawn.astype(out[name].dtype))
    for name, factor in factors.items():
        out[name] = (out[name] * factor).astype(out[name].dtype)
    return out
```

```python
from contextlib import ExitStack

import numpy as np

import concourse.bass as bass
from concourse import mybir

F32 = mybir.dt.float32
F32R = mybir.dt.float32r
ALU = mybir.AluOpType
ACT = mybir.ActivationFunctionType
AX = mybir.AxisListType

P = 128
L = 256
D = 2048
KT = D // P
DFF = 5632
FT = DFF // P
RING = 4
GC = 512
NF = GC // P
EPS = 1e-6
SSD_H = 16
LAM_INIT = 0.2

PARAM_ROWS = {
    "mix_pre": 0, "mix_post": 16, "ffn_pre": 32, "ffn_post": 48, "ple_pre": 64, "ple_post": 80,
    "norm1": 96, "norm2": 112,
    "ssd_conv_w": 128, "ssd_conv_b": 188, "ssd_norm": 200, "pool_scale": 208, "ssd_d": 216,
    "b_ada": 256, "q_norm_a": 352, "k_norm_a": 353, "q_norm_b": 354, "k_norm_b": 355, "subln": 356,
    "ffn_w0": 384, "ffn_w1": 428, "c": 472, "c_ctx": 488,
    "ffn_w2": 512, "ffn_b": 556,
}
PARAM_USED = [128, 88, 101, 120, 88]
N_PARAM_LOADS = 33

CONST = {}
_at = 0
for _name, _n in (("ident", 128), ("ones", 128), ("half", 128), ("rot_a", 128), ("rot_b", 128),
                  ("upto", 128), ("from", 128), ("cos_a", 256), ("sin_a", 256), ("cos_b", 256),
                  ("sin_b", 256)):
    CONST[_name] = (_at, _n)
    _at += _n
NCONST = _at


def constant_tables():
    c = np.zeros((P, NCONST), np.float32)
    i, j = np.arange(P)[:, None], np.arange(P)[None, :]

    def put(name, a):
        at, n = CONST[name]
        c[:, at:at + n] = a

    put("ident", i == j)
    put("ones", 1.0)
    put("half", i // 64 == j // 64)
    for name, sub in (("rot_a", 128), ("rot_b", 64)):
        half = sub // 2
        put(name, np.where((j % sub < half) & (i == j + half), -1.0, 0.0)
            + np.where((j % sub >= half) & (i == j - half), 1.0, 0.0))
    put("upto", i <= j)
    put("from", i >= j)
    t = np.arange(L)
    for name, hd in (("a", 128), ("b", 64)):
        n = hd // 4
        freqs = (np.float32(10000.0) ** (-np.arange(n, dtype=np.float32) / np.float32(n))).astype(np.float32)
        row, col = (t // 64).astype(np.float32), (t % 64).astype(np.float32)
        ang = np.concatenate([row[:, None] * freqs, col[:, None] * freqs], axis=1).T
        rows = np.arange(P) % (hd // 2)
        put("cos_" + name, np.cos(ang)[rows])
        put("sin_" + name, np.sin(ang)[rows])
    sel = (np.arange(32)[:, None] == (np.arange(32 * P)[None, :] // P)).astype(np.float32)
    inv = np.zeros((4, L), np.float32)
    for g, k in enumerate((2, 4, 8, 16)):
        lo, hi = np.clip(t - k // 2, 0, L), np.clip(t + k - k // 2, 0, L)
        inv[g] = 1.0 / (hi - lo).astype(np.float32)
    return c, sel, inv


class Phase:

    def __init__(self, Us, times, ada, last=None):
        self.Us, self.times, self.ada = Us, times, ada
        order = [("g", j, u) for j, n in enumerate(Us) for u in range(n)]
        body, a = [], 0
        for i, x in enumerate(order):
            body.append(x)
            while a < 8 * ada and (i + 1) * 8 * ada >= (a + 1) * len(order):
                body.append(("a", a // 8, a % 8))
                a += 1
        self.body = body
        assert times == 1 or (len(body) % RING == 0 and len(Us) % 2 == 0)


PHASES = {
    "in": Phase([8] * 7, 1, 0),
    "out": Phase([8, 8], 2, 0),
    "up": Phase([8, 8], 11, 1),
    "down": Phase([22, 22], 2, 3),
    "ple": Phase([1] * 4, 1, 0),
    "gate": Phase([8, 8], 2, 2),
    "kv": Phase([8, 8], 3, 0),
    "q": Phase([8, 8], 3, 1),
    "branch": Phase([8, 8, 8, 4], 4, 0),
    "out2": Phase([8, 8], 2, 0),
    "up2": Phase([8, 8], 11, 0),
    "down2": Phase([22] * 4, 1, 0),
}
_u = _g = _a = 0
for _p in PHASES.values():
    _p.unit0, _p.group0, _p.ada0 = _u, _g, _a
    _u += len(_p.body) * _p.times
    _g += len(_p.Us) * _p.times
    _a += _p.ada * _p.times
UNITS, ADA_GROUPS = _u, _a
assert ADA_GROUPS == 6 * D // GC


class Body:

    def __init__(self, ph, i, rep):
        self.ph, self.i, self.rep = ph, i, rep

    def _of(self, base, per, k):
        if self.i is None:
            return base + self.rep * per + k
        return self.i * per + (base + k)

    def unit(self, k):
        return self._of(self.ph.unit0, len(self.ph.body), k)

    def static_unit(self, k):
        return self.ph.unit0 + self.rep * len(self.ph.body) + k

    def slot(self, k):
        return self.static_unit(k) % RING

    def landed(self, k):
        n = self.static_unit(k) // RING + 1
        return 16 * n if self.i is None else self.i * (16 * len(self.ph.body) // RING) + 16 * n

    def group(self, j):
        return self._of(self.ph.group0, len(self.ph.Us), j)

    def local(self, j):
        return self._of(0, len(self.ph.Us), j)

    def set(self, j):
        return (self.ph.group0 + self.rep * len(self.ph.Us) + j) % 2

    def ada(self, a):
        return self._of(self.ph.ada0, self.ph.ada, a)

    def n(self, per=1, k=0):
        return self._of(0, per, k)


def bodies(eng, name, straight=False):
    ph = PHASES[name]
    if ph.times == 1 or straight:
        for rep in range(ph.times):
            yield Body(ph, None, rep)
    else:
        with eng.Fori(0, ph.times) as i:
            yield Body(ph, i, 0)


class Chain:

    def __init__(self, eng, sem):
        self.eng, self.sem, self.n, self.i, self.per = eng, sem, 0, None, 0

    def mark(self, ins):
        ins.then_inc(self.sem, 1)
        self.n += 1
        return self.n

    def wait(self, n=None):
        n = self.n if n is None else n
        self.eng.wait_ge(self.sem, n if self.i is None else self.i * self.per + n)

    def start(self, b, per):
        self.i, self.per, self.n0 = b.i, per, self.n

    def end(self, b):
        assert self.n - self.n0 == self.per, self.n - self.n0
        if b.i is not None:
            self.n = self.n0 + self.per * b.ph.times
        self.i = None


def build(nc, A, out, tables):
    consts_d, sel_d, inv_d = tables

    def ktiles(w):
        return w[0].rearrange("(t p) n -> p t n", p=P)

    W_IN, W_OUT, W_UP, W_DOWN = (ktiles(A[n]) for n in ("w_in", "w_out", "w_ffn_up", "w_ffn_down"))
    W_GATE, W_PLE, W_ADA, W_IN2 = (ktiles(A[n]) for n in ("w_ple_gate", "w_ple", "w_ada_2", "w_in_2"))
    W_BR_A, W_BR_B, W_OUT2 = (ktiles(A[n]) for n in ("w_br_a_2", "w_br_b_2", "w_out_2"))
    W_G2, W_U2, W_D2 = (ktiles(A[n]) for n in ("w_ff_gate_2", "w_ff_up_2", "w_ff_down_2"))

    with ExitStack() as ctx:
        def sb(name, shape, dt=F32):
            return ctx.enter_context(nc.sbuf_tensor(name, shape, dt))

        def freed(name, shape, dt):
            with nc.sbuf_tensor(name, shape, dt) as t:
                return t

        sems = {}

        def S(name):
            if name not in sems:
                sems[name] = ctx.enter_context(nc.semaphore(name))
            return sems[name]

        raw = sb("w_raw", [P, RING, 2, GC])
        w_hi = sb("w_hi", [P, RING, 2, GC], F32R)
        w_lo = sb("w_lo", [P, RING, 2, GC], F32R)
        H = sb("residual", [P, KT, L])
        XS = freed("x_split", [P, KT, 2, L], F32R)
        XF = sb("region_x", [P, 2 * KT * L])
        NB = FT * 2 * L
        HID = freed("hidden_split", [P, FT, 2, L], F32R)
        CS = freed("ctx_split", [P, KT, 2, L], F32R)
        with nc.sbuf_tensor("pad_o", [P, 8192], F32):
            OS = freed("attn_split", [P, 24, 2, L], F32R)
        with nc.sbuf_tensor("pad_p", [P, 4096], F32):
            PSP = freed("p_split", [P, 2, 2, L], F32R)
        BF = sb("region_b", [P, NB])
        EV = sb("evac", [P, 2, NF, L])
        C = sb("constants", [P, NCONST])
        PRM = sb("params", [P, 5, P])
        MADA = sb("ada", [P, 6 * KT, 2])
        CSP = sb("cond_split", [P, KT, 4], F32R)
        GE = sb("gain_eff", [P, 3, KT])
        SM = sb("small", [P, 512])
        ST = sb("stat", [P, 512])
        PS = ctx.enter_context(nc.psum_tensor("psum", [P, 8, 512], F32))

        def const(name):
            at, n = CONST[name]
            return C[:, at:at + n]

        def prm(name, i=0, n=1):
            at = PARAM_ROWS[name] + i
            return PRM[:, at // P, at % P:at % P + n]

        def prm_dyn(name, i):
            at = PARAM_ROWS[name]
            return PRM[:, at // P, bass.ds(i + at % P, 1)]

        def bf(at, *shape):
            n = int(np.prod(shape))
            v = BF[:, at:at + n]
            if len(shape) == 1:
                return v
            names = "abcd"[:len(shape)]
            return v.rearrange(f"p ({' '.join(names)}) -> p {' '.join(names)}",
                               **{k: s for k, s in zip(names[1:], shape[1:])})

        def xf(at, *shape):
            n = int(np.prod(shape))
            v = XF[:, at:at + n]
            if len(shape) == 1:
                return v
            names = "abcd"[:len(shape)]
            return v.rearrange(f"p ({' '.join(names)}) -> p {' '.join(names)}",
                               **{k: s for k, s in zip(names[1:], shape[1:])})

        def r(ap):
            return ap.bitcast(F32)

        SQ = bf(14336, KT, L)
        Z = bf(18432, KT, L)
        XNAT = bf(0, 2, D)
        PROW = bf(4096, 5, P)
        WDT = bf(4736, KT, 32)
        DROW = bf(5248, P)
        DPAIR = bf(5376, 2)
        XBC = bf(0, 12, L)
        SZ = bf(3072, 8, L)
        UPW = L + 16
        UP = bf(5120, 8, UPW)
        MIXED = bf(7296, 8, L)
        PW = bf(9344, 4, 2, L)
        XDT = bf(11392, 2, 2, SSD_H, 64)
        CBM = bf(15488, 2, 2, 3, P)
        Y = bf(17024, KT, L)
        YSQ = bf(5120, 8, L)
        SEL = xf(0, 32, P)
        MR = xf(4096, 4, 3 * P)
        ER = xf(5632, 4, 3 * P)
        SA, SB = bf(11392, 8, UPW), bf(13568, 8, UPW)
        INV = bf(21120, 4, L)
        OUT1 = bf(0, KT, L)
        OSQ1 = bf(4096, KT, L)
        OUT2 = xf(0, KT, L)
        OSQ2 = xf(4096, KT, L)
        PLE = bf(0, KT, L)
        OUT3 = bf(5120, KT, L)
        OSQ3 = bf(9216, KT, L)
        PNAT = bf(5120, 2, L)
        PTR = bf(5632, 2, L)
        CNAT = bf(0, 2, D)
        CTX = bf(8192, KT, L)
        KV = bf(8192, 24, 2 * L)
        Q = bf(0, 24, L)
        PR = bf(6144, 4, 512)
        PTT = bf(20480, 2, 4, L)
        MG = bf(0, KT, L)
        ONAT = bf(0, 2, D)
        evA, evB = EV[:, 0], EV[:, 1]

        def acc(s):
            return PS[:, 2 * s:2 * s + 2, :].rearrange("p b (h n) -> p (b h) n", h=2)

        def accf(s, f):
            return PS[:, 2 * s + f // 2, (f % 2) * L:(f % 2) * L + L]

        ADA = PS[:, 7, 0:4 * NF].rearrange("p (f v) -> p f v", v=4)

        w_landed = [S(f"w_landed{i}") for i in range(RING)]
        w_rounded, w_split, w_used = S("w_rounded"), S("w_split"), S("w_used")
        evacuated, ada_evacuated = S("evacuated"), S("ada_evacuated")

        def source(name, b, x):
            kind, j, u = x
            k = slice(2 * u, 2 * u + 2)
            if kind == "a":
                return W_ADA[:, k, bass.ds(b.ada(j) * GC, GC)]
            if name == "in":
                col = [1024, 1536, 2048, 2592, 3104, 0, 512][j]
                return W_IN[:, k, col:col + GC]
            if name == "up":
                return W_UP[:, k, bass.ds(b.n(GC, j * DFF), GC)]
            if name == "branch":
                w, c0 = [(W_IN2, 6144), (W_BR_A, 0), (W_IN2, 8192), (W_BR_B, 0)][j]
                return w[:, k, bass.ds(b.n(GC, c0), GC)]
            if name == "up2":
                return (W_G2, W_U2)[j][:, k, bass.ds(b.n(GC, 0), GC)]
            w, c0 = {"out": (W_OUT, 0), "down": (W_DOWN, 0), "ple": (W_PLE, 0), "gate": (W_GATE, 0),
                     "kv": (W_IN2, 0), "q": (W_IN2, 3072), "out2": (W_OUT2, 0),
                     "down2": (W_D2, 0)}[name]
            return w[:, k, bass.ds(b.local(j) * GC + c0, GC)]

        def stream_pe(pe, name, rhs):
            for b in bodies(pe, name):
                for k, x in enumerate(b.ph.body):
                    kind, j, u = x
                    slot = b.slot(k)
                    if u == 0 and kind == "g":
                        pe.wait_ge(evacuated, b.group(j) + 1)
                    if u == 0 and kind == "a":
                        pe.wait_ge(ada_evacuated, b.ada(j) + 1)
                    pe.wait_ge(w_split, b.unit(k) + RING + 1)
                    for t in range(2):
                        kt = 2 * u + t
                        last = kt == 2 * (b.ph.Us[j] if kind == "g" else 8) - 1
                        for f in range(NF):
                            hi = w_hi[:, slot, t, f * P:f * P + P]
                            lo = w_lo[:, slot, t, f * P:f * P + P]
                            if kind == "a":
                                nc.tensor.matmul(ADA[:, f, :], hi, CSP[:, kt, :], start=kt == 0 and f == 0,
                                                 stop=False, skip_group_check=True)
                                mm = nc.tensor.matmul(ADA[:, f, 0:2], lo, CSP[:, kt, 0:2], start=False,
                                                      stop=last, skip_group_check=True)
                                continue
                            to = accf(b.set(j), f)
                            x_hi, x_lo = rhs(j, kt)
                            nc.tensor.matmul(to, hi, x_hi, start=kt == 0 and f % 2 == 0, stop=False,
                                             skip_group_check=True)
                            nc.tensor.matmul(to, hi, x_lo, start=False, stop=False, skip_group_check=True)
                            mm = nc.tensor.matmul(to, lo, x_hi, start=False, stop=last, skip_group_check=True)
                    mm.then_inc(w_used, 1)

        def kv_stream(pe):
            for b in bodies(pe, "kv"):
                for k, (_, j, u) in enumerate(b.ph.body):
                    slot, s = b.slot(k), b.set(j)
                    if u == 0:
                        pe.wait_ge(evacuated, b.group(j) + 1)
                    pe.wait_ge(w_split, b.unit(k) + RING + 1)
                    for t in range(2):
                        kt = 2 * u + t
                        for f in range(NF):
                            hi = w_hi[:, slot, t, f * P:f * P + P]
                            lo = w_lo[:, slot, t, f * P:f * P + P]
                            for i, x in enumerate((XS, CS)):
                                to = PS[:, 4 * s + f, i * L:i * L + L]
                                nc.tensor.matmul(to, hi, x[:, kt, 0], start=kt == 0 and i == 0, stop=False,
                                                 skip_group_check=True)
                                nc.tensor.matmul(to, hi, x[:, kt, 1], start=False, stop=False,
                                                 skip_group_check=True)
                                mm = nc.tensor.matmul(to, lo, x[:, kt, 0], start=False, stop=kt == KT - 1,
                                                      skip_group_check=True)
                    mm.then_inc(w_used, 1)

        def stream_act(act, name, evac, straight=False):
            for b in bodies(act, name, straight):
                for k, x in enumerate(b.ph.body):
                    if b.static_unit(k) + RING < UNITS:
                        slot = b.slot(k)
                        act.wait_ge(w_landed[slot], b.landed(k) + 16)
                        act.wait_ge(w_used, b.unit(k) + RING + 1)
                        nc.scalar.activation(w_hi[:, slot], raw[:, slot], ACT.Copy).then_inc(w_rounded, 1)
                    if x[0] == "g" and x[2] == b.ph.Us[x[1]] - 1:
                        evac(b, x[1], k)

        def stream_dve(dve, name, evac, straight=False):
            for b in bodies(dve, name, straight):
                for k, x in enumerate(b.ph.body):
                    if b.static_unit(k) + RING < UNITS:
                        slot = b.slot(k)
                        dve.wait_ge(w_rounded, b.unit(k) + RING + 1)
                        nc.vector.tensor_tensor(w_lo[:, slot], raw[:, slot], r(w_hi[:, slot]),
                                                ALU.subtract).then_inc(w_split, 1)
                    if x[0] == "g" and x[2] == b.ph.Us[x[1]] - 1:
                        evac(b, x[1], k)
                    if x[0] == "a" and x[2] == 7:
                        dve.wait_ge(w_used, b.unit(k) + RING + 1)
                        nc.vector.tensor_reduce(
                            MADA[:, bass.ds(b.ada(x[1]) * NF, NF), :],
                            ADA.rearrange("p f (h v) -> p f v h", h=2), AX.X, ALU.add
                        ).then_inc(ada_evacuated, 1)

        def group_used(eng, b, k):
            eng.wait_ge(w_used, b.unit(k) + RING + 1)

        def all_evacuated(eng, name):
            ph = PHASES[name]
            eng.wait_ge(evacuated, 2 + ph.group0 + len(ph.Us) * ph.times)

        def squares_act(act, tag, src):
            for q in range(4):
                nc.scalar.activation(SQ[:, 4 * q:4 * q + 4], src[:, 4 * q:4 * q + 4],
                                     ACT.Square).then_inc(S(tag + "_sq"), 1)

        def stat_pe(pe, tag, sq, per):
            for t in range(KT):
                pe.wait_ge(S(tag + "_sq"), t // (KT // per) + 1)
                mm = nc.tensor.matmul(PS[:, 4, 0:L], const("ones"), sq[:, t], start=t == 0, stop=t == KT - 1,
                                      skip_group_check=True)
            mm.then_inc(S(tag + "_stat"), 1)

        def std_act(act, tag):
            act.wait_ge(S(tag + "_stat"), 1)
            nc.scalar.activation(ST[:, 0:L], PS[:, 4, 0:L], ACT.Sqrt, bias=SM[:, 0:1],
                                 scale=1.0 / D).then_inc(S(tag + "_std"), 1)

        def rstd_dve(dve, ch, tag):
            dve.wait_ge(S(tag + "_std"), 1)
            ch.mark(nc.vector.reciprocal(ST[:, 0:L], ST[:, 0:L]))
            ch.wait()

        def pre_act(act, tag, dst, shift=None):
            std_act(act, tag)
            for q in range(4):
                act.wait_ge(S(tag + "_z"), 4 * q + 4)
                if shift is None:
                    nc.scalar.activation(dst[:, 4 * q:4 * q + 4, 0], Z[:, 4 * q:4 * q + 4],
                                         ACT.Copy).then_inc(S(tag + "_hi"), 1)
                else:
                    for t in range(4 * q, 4 * q + 4):
                        ins = nc.scalar.activation(dst[:, t, 0], Z[:, t], ACT.Identity, bias=shift(t))
                    ins.then_inc(S(tag + "_hi"), 1)

        def pre_dve(dve, ch, tag, src, gain, dst, shift=None):
            rstd_dve(dve, ch, tag)
            for t in range(KT):
                nc.vector.scalar_tensor_tensor(Z[:, t], src[:, t], gain(t), ST[:, 0:L], ALU.mult,
                                               ALU.mult).then_inc(S(tag + "_z"), 1)
            for q in range(4):
                dve.wait_ge(S(tag + "_hi"), q + 1)
                dve.wait_ge(S(tag + "_z"), 4 * q + 4)
                if shift is None:
                    ins = nc.vector.tensor_tensor(dst[:, 4 * q:4 * q + 4, 1], Z[:, 4 * q:4 * q + 4],
                                                  r(dst[:, 4 * q:4 * q + 4, 0]), ALU.subtract)
                else:
                    for t in range(4 * q, 4 * q + 4):
                        ins = nc.vector.scalar_tensor_tensor(dst[:, t, 1], Z[:, t], shift(t), r(dst[:, t, 0]),
                                                             ALU.add, ALU.subtract)
                ins.then_inc(S(tag + "_ready"), 1)

        def post_dve(dve, ch, tag, o, gain):
            rstd_dve(dve, ch, tag)
            for t in range(KT):
                ch.mark(nc.vector.scalar_tensor_tensor(Z[:, t], o[:, t], prm(gain, t), ST[:, 0:L], ALU.mult,
                                                       ALU.mult))
            for q in range(4):
                ch.wait(ch.n - 12 + 4 * q)
                ins = nc.vector.tensor_tensor(H[:, 4 * q:4 * q + 4], H[:, 4 * q:4 * q + 4],
                                              Z[:, 4 * q:4 * q + 4], ALU.add)
                ins.then_inc(S(tag + "_added"), 1)

        def split_rhs(xs, at=0):
            return lambda j, k: (xs[:, at + k, 0], xs[:, at + k, 1])

        def copy_evac(o, tag):
            def dve_part(dve):
                def evac(b, j, k):
                    group_used(dve, b, k)
                    nc.vector.tensor_copy(o[:, bass.ds(b.local(j) * NF, NF)], acc(b.set(j))).then_inc(evacuated, 1)
                return evac

            def act_part(act, sq):
                def evac(b, j, k):
                    act.wait_ge(evacuated, b.group(j) + 3)
                    nc.scalar.activation(sq[:, bass.ds(b.local(j) * NF, NF)], o[:, bass.ds(b.local(j) * NF, NF)],
                                         ACT.Square).then_inc(S(tag + "_sq"), 1)
                return evac
            return dve_part, act_part

        out_dve, out_act = copy_evac(OUT1, "mix_post")
        down_dve, down_act = copy_evac(OUT2, "ffn_post")

        block = ctx.enter_context(nc.Block())

        @block.sync
        def _(sp):
            sp.dma_start(C[:, :], consts_d).then_inc(S("consts_landed"), 16)
            for t in range(2):
                sp.dma_start(XNAT[:, t, :], A["x"][0, t * P:(t + 1) * P, :]).then_inc(S("x_landed"), 16)
            rows = {
                "mix_pre": "mix_norm_pre", "mix_post": "mix_norm_post", "ffn_pre": "ffn_norm_pre",
                "ffn_post": "ffn_norm_post", "ple_pre": "ple_norm_pre", "ple_post": "ple_norm_post",
                "norm1": "norm1_g_2", "norm2": "norm2_g_2", "ssd_conv_w": "ssd_conv_w",
                "ssd_conv_b": "ssd_conv_b", "ssd_norm": "ssd_norm", "pool_scale": "pool_scale",
                "b_ada": "b_ada_2", "q_norm_a": "q_norm_a_2", "k_norm_a": "k_norm_a_2",
                "subln": "subln_g_2", "ffn_b": "ffn_conv_b", "c": "c_2",
            }
            n = 0

            def param(at, src):
                nonlocal n
                k = src.shape[0]
                sp.dma_start(PROW[at % P:at % P + k, at // P, :], src).then_inc(S("params_landed"), 16)
                n += 1

            for name, key in rows.items():
                a = A[key][0]
                if len(a.shape) == 2:
                    a = a.rearrange("k (r c) -> (k r) c", c=P)
                else:
                    a = a.rearrange("(r c) -> r c", c=P)
                param(PARAM_ROWS[name], a)
            param(PARAM_ROWS["c_ctx"], A["c_ctx_2"].rearrange("(r c) -> r c", c=P))
            for i, name in enumerate(("ffn_w0", "ffn_w1", "ffn_w2")):
                param(PARAM_ROWS[name], A["ffn_conv_w"][0, i].rearrange("(r c) -> r c", c=P))
            for name, key in (("q_norm_b", "q_norm_b_2"), ("k_norm_b", "k_norm_b_2")):
                at = PARAM_ROWS[name]
                for half in range(2):
                    sp.dma_start(PROW[at % P:at % P + 1, at // P, 64 * half:64 * half + 64],
                                 A[key][0:1, :]).then_inc(S("params_landed"), 16)
                    n += 1
            sp.dma_start(DPAIR[0:8], A["ssd_d"][0].rearrange("(t e) -> t e", e=2)).then_inc(S("params_landed"), 16)
            sp.dma_start(SM[:, 32:64], A["ssd_dt_bias"][0].rearrange("a b -> (a b)").partition_broadcast(P)
                         ).then_inc(S("params_landed"), 16)
            sp.dma_start(SM[:, 64:96], A["ssd_a_log"][0].rearrange("a b -> (a b)").partition_broadcast(P)
                         ).then_inc(S("params_landed"), 16)
            for i, key in enumerate(("lam_q1_2", "lam_k1_2", "lam_q2_2", "lam_k2_2")):
                sp.dma_start(EV[:, 0, 0, 64 * i:64 * i + 64], A[key][0].partition_broadcast(P)
                             ).then_inc(S("params_landed"), 16)
            assert n + 7 == N_PARAM_LOADS
            sp.dma_start(WDT, W_IN[:, :, 2560:2592]).then_inc(S("wdt_landed"), 16)
            sp.dma_start(PW, A["pool_w"][0].rearrange("g (t p) n -> p g t n", p=P)).then_inc(S("poolw_landed"), 16)

            def stream(name):
                for b in bodies(sp, name, straight=name == "branch"):
                    for k, x in enumerate(b.ph.body):
                        sp.wait_ge(w_split, b.unit(k) + 1)
                        sp.dma_start(raw[:, b.slot(k)], source(name, b, x)).then_inc(w_landed[b.slot(k)], 16)

            stream("in")
            stream("out")
            stream("up")
            stream("down")
            stream("ple")
            stream("gate")
            for name in ("kv", "q", "branch", "out2", "up2", "down2"):
                stream(name)
            for t, by in enumerate(("out_copied_dve", "out_copied_act")):
                sp.wait_ge(S(by), 1)
                sp.dma_start(out[0, t * P:(t + 1) * P, :], ONAT[:, t, :]).then_inc(S("stored"), 16)
            sp.wait_ge(S("stored"), 32)

        @block.gpsimd
        def _(pool):
            pool.wait_ge(S("mix_pre_ready"), 4)
            pool.wait_ge(S("dt_projected"), 1)
            for g in range(4):
                pool.dma_start(INV[:, g, :], inv_d[g].partition_broadcast(P)).then_inc(S("inv_landed"), 16)
            pool.wait_ge(w_used, RING + PHASES["out"].unit0)
            pool.dma_start(SEL[0:32], sel_d.rearrange("r (h p) -> r h p", h=32)).then_inc(S("sel_landed"), 16)
            pool.wait_ge(w_used, RING + PHASES["ple"].unit0)
            for t in range(2):
                pool.dma_start(PNAT[:, t, :], A["p"][0, 0, t * P:(t + 1) * P, :]).then_inc(S("p_landed"), 16)
            pool.wait_ge(S("ple_post_added"), 4)
            for t in range(2):
                pool.dma_start(CNAT[:, t, :], A["ctx_2"][0, t * P:(t + 1) * P, :]).then_inc(S("ctx_landed"), 16)

        SSD_STEPS = [(t, e, d) for t in range(8) for e in range(2) for d in range(2)]

        ROUNDS = [("a", h, qb) for h in range(16) for qb in range(2)] + \
                 [("b", h, qb) for h in range(8) for qb in range(2)]
        JOBS, at = [], 0
        for rd in ROUNDS:
            JOBS.append(list(range(at, at + (1 if rd[0] == "a" else 2))))
            at += len(JOBS[-1])
        NJOBS = at

        QK = [(KV[:, j], 2 * L, "k_norm_a", "a") for j in range(4)] + \
             [(KV[:, 8 + j], 2 * L, "k_norm_b", "b") for j in range(8)] + \
             [(Q[:, j], L, "q_norm_a", "a") for j in range(16)] + \
             [(Q[:, 16 + j], L, "q_norm_b", "b") for j in range(8)]
        QK_SQ = PR[:, 0:2]
        QK_ST = [PR[:, 2], PR[:, 3]]
        QK_T = PTT.rearrange("p a b n -> p (a b) n")
        SUBSQ, SUBST = bf(6144, 8, L), bf(20480, 8, L)
        V_TILES = [4, 5, 6, 7] + list(range(16, 24))
        NEGMAX, SUMS, RSUM = SM[:, 96:160], SM[:, 160:224], SM[:, 224:288]

        @block.scalar
        def _(act):
            seen = Chain(act, S("act_chain"))
            for n in range(RING):
                act.wait_ge(w_landed[n], 16)
                nc.scalar.activation(w_hi[:, n], raw[:, n], ACT.Copy).then_inc(w_rounded, 1)
            act.wait_ge(S("params_turned"), 1)
            cond = SM[:, 96:128].rearrange("p (t v) -> p t v", v=2)
            for v, name in enumerate(("c", "c_ctx")):
                seen.mark(nc.scalar.activation(cond[:, :, v], prm(name, 0, KT), ACT.Silu))
            seen.wait()
            nc.scalar.activation(CSP[:, :, 0:2], cond, ACT.Copy).then_inc(S("cond_hi"), 1)
            act.wait_ge(S("lam_sums"), 1)
            nc.scalar.activation(SM[:, 1:3], SM[:, 1:3], ACT.Exp).then_inc(S("lam_exp"), 1)
            act.wait_ge(S("x_turned"), 1)
            nc.scalar.activation(H[:, 8:16], PS[:, 4:8, :].rearrange("p b (h n) -> p (b h) n", h=2),
                                 ACT.Copy).then_inc(S("h_loaded_act"), 1)
            act.wait_ge(S("h_loaded_act"), 1)
            act.wait_ge(S("h_loaded_dve"), 1)
            squares_act(act, "mix_pre", H)
            pre_act(act, "mix_pre", XS)

            def in_evac(b, j, k):
                if j < 3:
                    act.wait_ge(evacuated, b.group(j) + 3)
                    t = slice(4 * j, 4 * j + 4)
                    nc.scalar.activation(XBC[:, t], XBC[:, t], ACT.Silu).then_inc(S("xbc_ready"), 1)
                elif j < 5:
                    group_used(act, b, k)
                    act.wait_ge(S("u_padded"), 1)
                    t = slice(4 * (j - 3), 4 * (j - 3) + 4)
                    nc.scalar.activation(UP[:, t, 8:8 + L], acc(b.set(j)), ACT.Copy).then_inc(S("u_ready"), 1)
                else:
                    group_used(act, b, k)
                    t = slice(4 * (j - 5), 4 * (j - 5) + 4)
                    nc.scalar.activation(SZ[:, t], acc(b.set(j)), ACT.Silu).then_inc(S("z_ready"), 1)
                if j == 0:
                    act.wait_ge(S("dt_biased"), 1)
                    seen.mark(nc.scalar.activation(SM[:, 384:448], SM[:, 128:192], ACT.Abs))
                    seen.wait()
                    nc.scalar.activation(SM[:, 192:256], SM[:, 384:448], ACT.Exp, scale=-1.0)
                    nc.scalar.activation(SM[:, 64:96], SM[:, 64:96], ACT.Exp).then_inc(S("dt_exp"), 1)
                if j == 1:
                    act.wait_ge(S("dt_plus_one"), 1)
                    nc.scalar.activation(SM[:, 320:384], SM[:, 256:320], ACT.Ln).then_inc(S("dt_ln"), 1)

            stream_act(act, "in", in_evac)

            act.wait_ge(S("acum_done"), 1)
            nc.scalar.activation(ST[0:32, :], PS[0:32, 6, :], ACT.Copy).then_inc(S("acum_rows"), 1)
            for n in range(len(SSD_STEPS)):
                act.wait_ge(S("exponent_ready"), n + 1)
                nc.scalar.activation(ER[:, n % 4], ER[:, n % 4], ACT.Exp).then_inc(S("decay_ready"), 1)
            for g in range(2):
                act.wait_ge(S("y_gated"), 4 * g + 4)
                nc.scalar.activation(YSQ[:, 4 * g:4 * g + 4], Y[:, 4 * g:4 * g + 4],
                                     ACT.Square).then_inc(S("y_sq"), 1)
            act.wait_ge(S("y_stat"), 1)
            nc.scalar.activation(ST[:, :], PS[:, 4, :], ACT.Sqrt, bias=SM[:, 0:1],
                                 scale=1.0 / 512).then_inc(S("y_std"), 1)
            for q in (2, 3, 0, 1):
                if q < 2:
                    act.wait_ge(S("y_normed"), 4 * q + 4)
                else:
                    act.wait_ge(S("pool_scaled"), q - 1)
                nc.scalar.activation(XS[:, 4 * q:4 * q + 4, 0], Y[:, 4 * q:4 * q + 4],
                                     ACT.Copy).then_inc(S("mix_hi"), 1)

            stream_act(act, "out", out_act(act, OSQ1))
            std_act(act, "mix_post")
            act.wait_ge(S("mix_post_added"), 4)
            squares_act(act, "ffn_pre", H)
            pre_act(act, "ffn_pre", XS)

            def up_evac(b, j, k):
                if j == 0:
                    act.wait_ge(evacuated, b.group(j) + 3)
                    nc.scalar.activation(evA, evA, ACT.Gelu_apprx_tanh).then_inc(S("gate_gelu"), 1)
                else:
                    act.wait_ge(evacuated, b.group(j) + 3)
                    nc.scalar.activation(HID[:, bass.ds(b.n(NF, 0), NF), 0], evB, ACT.Copy
                                         ).then_inc(S("hidden_hi"), 1)

            stream_act(act, "up", up_evac)
            stream_act(act, "down", down_act(act, OSQ2))
            std_act(act, "ffn_post")
            act.wait_ge(S("p_turned"), 1)
            nc.scalar.activation(PTR.rearrange("p a n -> p (a n)"), PS[:, 5, :], ACT.Copy).then_inc(S("p_copied"), 1)
            act.wait_ge(S("p_copied"), 1)
            nc.scalar.activation(PSP[:, :, 0], PTR, ACT.Copy).then_inc(S("p_hi"), 1)
            act.wait_ge(S("ffn_post_added"), 4)
            squares_act(act, "ple_pre", H)
            pre_act(act, "ple_pre", XS)
            stream_act(act, "ple", lambda b, j, k: None)

            def gate_evac(b, j, k):
                group_used(act, b, k)
                act.wait_ge(evacuated, b.group(j) + 2)
                nc.scalar.activation(evA, acc(b.set(j)), ACT.Sigmoid).then_inc(S("gate_ready"), 1)
                act.wait_ge(evacuated, b.group(j) + 3)
                at = bass.ds(b.local(j) * NF, NF)
                nc.scalar.activation(OSQ3[:, at], OUT3[:, at], ACT.Square).then_inc(S("ple_post_sq"), 1)

            stream_act(act, "gate", gate_evac)
            std_act(act, "ple_post")

            act.wait_ge(S("ple_post_added"), 4)
            squares_act(act, "norm1", H)
            pre_act(act, "norm1", XS, shift=lambda t: MADA[:, t, 0:1])
            act.wait_ge(S("ctx_turned"), 1)
            nc.scalar.activation(CTX[:, 8:16], PS[:, 4:8, :].rearrange("p b (h n) -> p (b h) n", h=2),
                                 ACT.Copy).then_inc(S("ctx_loaded_act"), 1)
            act.wait_ge(S("ctx_loaded_act"), 1)
            act.wait_ge(S("ctx_loaded_dve"), 1)
            squares_act(act, "norm_c", CTX)
            pre_act(act, "norm_c", CS, shift=lambda t: MADA[:, t, 1:2])

            def kv_evac(b, j, k):
                group_used(act, b, k)
                s = b.set(j)
                nc.scalar.activation(KV[:, bass.ds(b.local(j) * NF + 2, 2)], PS[:, 4 * s + 2:4 * s + 4, :],
                                     ACT.Copy).then_inc(S("kv_half"), 1)

            stream_act(act, "kv", kv_evac)
            stream_act(act, "q", lambda b, j, k: None)

            act.wait_ge(evacuated, 2 + PHASES["branch"].group0)
            nq = len(QK)

            def qk_square(i):
                x, n = QK[i][0], QK[i][1]
                if i >= 2:
                    act.wait_ge(S("qk_stat"), i - 1)
                nc.scalar.activation(QK_SQ[:, i % 2, 0:n], x, ACT.Square).then_inc(S("qk_sq"), 1)

            qk_square(0)
            qk_square(1)
            for i in range(nq):
                x, n, _, kind = QK[i]
                act.wait_ge(S("qk_stat"), i + 1)
                if i >= 2:
                    act.wait_ge(S("qk_normed"), i - 1)
                nc.scalar.activation(QK_ST[i % 2][:, 0:n], PS[:, 4 + i % 2, 0:n], ACT.Sqrt, bias=SM[:, 0:1],
                                     scale=1.0 / (128 if kind == "a" else 64)).then_inc(S("qk_std"), 1)
                if i + 2 < nq:
                    qk_square(i + 2)
            for i, j in enumerate(V_TILES):
                act.wait_ge(S("v_turned"), i + 1)
                nc.scalar.activation(KV[:, j], PS[:, i % 4, :], ACT.Copy).then_inc(S("v_ready"), 1)

            def exps(rd):
                for n in JOBS[rd]:
                    act.wait_ge(S("max_ready"), n + 1)
                    if rd >= 2:
                        act.wait_ge(S("p_turn"), rd - 1)
                    nc.scalar.activation(PR[:, n % 4], PS[:, 2 + n % 4, :], ACT.Exp, bias=NEGMAX[:, n:n + 1],
                                         accum_out=SUMS[:, n:n + 1]).then_inc(S("exp_ready"), 1)

            exps(0)
            for rd, (_, h, qb) in enumerate(ROUNDS):
                if rd + 1 < len(ROUNDS):
                    exps(rd + 1)
                act.wait_ge(S("p_turn"), rd + 1)
                if rd >= 4:
                    act.wait_ge(S("pv_done"), rd // 2 - 1)
                nc.scalar.activation(PTT[:, (rd // 2) % 2, :, qb * P:(qb + 1) * P],
                                     PS[:, 6 + rd % 2, :].rearrange("p (c q) -> p c q", c=4),
                                     ACT.Copy).then_inc(S("pt_ready"), 1)
            act.wait_ge(S("o_ready"), 24)
            for q in range(2):
                nc.scalar.activation(SUBSQ[:, 4 * q:4 * q + 4], Q[:, 16 + 4 * q:20 + 4 * q],
                                     ACT.Square).then_inc(S("sub_sq"), 1)
            act.wait_ge(S("sub_stat"), 1)
            nc.scalar.activation(SUBST, PS[:, 2:6, :].rearrange("p b (h n) -> p (b h) n", h=2), ACT.Sqrt,
                                 bias=SM[:, 0:1], scale=1.0 / P).then_inc(S("sub_std"), 1)
            for q in range(6):
                if q == 4:
                    act.wait_ge(S("o_normed"), 8)
                nc.scalar.activation(OS[:, 4 * q:4 * q + 4, 0], Q[:, 4 * q:4 * q + 4],
                                     ACT.Copy).then_inc(S("o_hi"), 1)

            def branch_evac(b, j, k):
                if j % 2 == 0:
                    group_used(act, b, k)
                    act.wait_ge(evacuated, b.group(j) + 2)
                    nc.scalar.activation(evA, acc(b.set(j)), ACT.Sigmoid).then_inc(S("branch_gate"), 1)

            stream_act(act, "branch", branch_evac)
            act.wait_ge(S("merged"), 4)
            for q in range(4):
                nc.scalar.activation(XS[:, 4 * q:4 * q + 4, 0], MG[:, 4 * q:4 * q + 4],
                                     ACT.Copy).then_inc(S("merged_hi"), 1)
            stream_act(act, "out2", lambda b, j, k: None)
            all_evacuated(act, "out2")
            squares_act(act, "norm2", H)
            pre_act(act, "norm2", XS, shift=lambda t: MADA[:, 3 * KT + t, 0:1])

            def up2_evac(b, j, k):
                if j == 0:
                    group_used(act, b, k)
                    act.wait_ge(evacuated, b.group(j) + 2)
                    nc.scalar.activation(evA, acc(b.set(j)), ACT.Silu).then_inc(S("gate2_silu"), 1)
                else:
                    act.wait_ge(evacuated, b.group(j) + 3)
                    nc.scalar.activation(HID[:, bass.ds(b.n(NF, 0), NF), 0], evB, ACT.Copy
                                         ).then_inc(S("hidden2_hi"), 1)

            stream_act(act, "up2", up2_evac)
            stream_act(act, "down2", lambda b, j, k: None)
            act.wait_ge(S("out_turned"), 2)
            nc.scalar.activation(ONAT[:, 1, :], PS[:, 4:8, :].rearrange("p b n -> p (b n)"),
                                 ACT.Copy).then_inc(S("out_copied_act"), 1)

        @block.vector
        def _(dve):
            ch = Chain(dve, S("dve_chain"))
            dve.sem_inc(w_split, RING)
            dve.sem_inc(evacuated, 2)
            dve.sem_inc(ada_evacuated, 1)
            nc.vector.memset(SM[:, 0:1], EPS).then_inc(S("eps_ready"), 1)
            for n in range(RING):
                dve.wait_ge(w_rounded, n + 1)
                nc.vector.tensor_tensor(w_lo[:, n], raw[:, n], r(w_hi[:, n]), ALU.subtract).then_inc(w_split, 1)
            dve.wait_ge(S("params_landed"), 16 * N_PARAM_LOADS)
            nc.vector.tensor_copy(DROW[0:8].rearrange("p (e c) -> p e c", e=2),
                                  DPAIR[0:8].rearrange("p (e o) -> p e o", o=1).to_broadcast([8, 2, 64])
                                  ).then_inc(S("d_rows"), 1)
            for i in range(2):
                ch.mark(nc.vector.tensor_tensor_reduce(
                    SM[:, 320:384], EV[:, 0, 0, 128 * i:128 * i + 64], EV[:, 0, 0, 128 * i + 64:128 * i + 128],
                    1.0, 0.0, ALU.mult, ALU.add, SM[:, 1 + i:2 + i]))
                ch.wait()
            dve.sem_inc(S("lam_sums"), 1)
            dve.wait_ge(S("params_pe"), 1)
            for i, n in enumerate(PARAM_USED):
                nc.vector.tensor_copy(PRM[:, i, 0:n], PS[:, i // 4, (i % 4) * P:(i % 4) * P + n])
            nc.vector.tensor_copy(PRM[:, 1, 88:96], PS[:, 1, P:P + 8]).then_inc(S("params_turned"), 1)
            dve.wait_ge(S("params_turned"), 1)
            for i, (name, g) in enumerate((("q_norm_a", P ** -0.5), ("q_norm_b", 64 ** -0.5),
                                           ("subln", 1 - LAM_INIT))):
                nc.vector.tensor_scalar(SM[:, 4 + i:5 + i], prm(name), g, None, ALU.mult)
            dve.wait_ge(S("x_turned"), 1)
            nc.vector.tensor_copy(H[:, 0:8], PS[:, 0:4, :].rearrange("p b (h n) -> p (b h) n", h=2)
                                  ).then_inc(S("h_loaded_dve"), 1)
            dve.wait_ge(S("cond_hi"), 1)
            nc.vector.tensor_tensor(CSP[:, :, 2:4], SM[:, 96:128].rearrange("p (t v) -> p t v", v=2),
                                    r(CSP[:, :, 0:2]), ALU.subtract).then_inc(S("cond_split"), 1)
            dve.wait_ge(S("lam_exp"), 1)
            ch.mark(nc.vector.tensor_tensor(SM[:, 3:4], SM[:, 2:3], SM[:, 1:2], ALU.subtract))
            ch.wait()
            ch.mark(nc.vector.tensor_scalar(SM[:, 3:4], SM[:, 3:4], -LAM_INIT, None, ALU.add))
            dve.wait_ge(S("h_loaded_act"), 1)
            dve.wait_ge(S("h_loaded_dve"), 1)
            pre_dve(dve, ch, "mix_pre", H, lambda t: prm("mix_pre", t), XS)

            dx = SM[:, 128:192]
            dtv = SM[:, 448:512]
            da = SM[:, 256:320]

            def c32(ap):
                return ap.rearrange("p (c h) -> p c h", c=2)

            def over_chunks(ap):
                return ap.rearrange("p (o h) -> p o h", o=1).to_broadcast([P, 2, 32])

            def conv(x, out, taps, weight, bias, tiles):
                half = taps // 2
                for f in range(tiles):
                    ch.mark(nc.vector.tensor_scalar(out(f), x(f), weight(half, f), bias(f), ALU.mult, ALU.add))
                others = [j for j in range(taps) if j != half]
                for j in others:
                    off = j - half
                    for f in range(tiles):
                        ch.wait(ch.n - tiles + 1 if j != others[-1] else ch.n - tiles + 1 + f)
                        a, z = max(0, -off), L - max(0, off)
                        ins = nc.vector.scalar_tensor_tensor(out(f)[:, a:z], x(f)[:, a + off:z + off],
                                                             weight(j, f), out(f)[:, a:z], ALU.mult, ALU.add)
                        if j != others[-1]:
                            ch.mark(ins)
                ins.then_inc(evacuated, 1)

            def in_evac(b, j, k):
                if j == 0:
                    dve.wait_ge(S("dt_projected"), 1)
                    nc.vector.tensor_tensor(c32(dx), c32(PS[:, 5, 0:64]), over_chunks(SM[:, 32:64]),
                                            ALU.add).then_inc(S("dt_biased"), 1)
                if j == 1:
                    dve.wait_ge(S("dt_exp"), 1)
                    nc.vector.tensor_scalar(SM[:, 256:320], SM[:, 192:256], 1.0, None,
                                            ALU.add).then_inc(S("dt_plus_one"), 1)
                if j == 2:
                    dve.wait_ge(S("dt_ln"), 1)
                    dve.wait_ge(S("dt_plus_one"), 1)
                    e, ln, um1, is0, den = SM[:, 192:256], SM[:, 320:384], SM[:, 384:448], ST[:, 0:64], ST[:, 64:128]
                    for ins in (lambda: nc.vector.tensor_scalar(um1, SM[:, 256:320], -1.0, None, ALU.add),
                                lambda: nc.vector.tensor_scalar(is0, um1, 0.0, None, ALU.is_equal),
                                lambda: nc.vector.tensor_tensor(den, um1, is0, ALU.add),
                                lambda: nc.vector.reciprocal(den, den),
                                lambda: nc.vector.tensor_tensor(ln, ln, e, ALU.mult),
                                lambda: nc.vector.tensor_tensor(ln, ln, den, ALU.mult),
                                lambda: nc.vector.tensor_tensor(is0, is0, e, ALU.mult),
                                lambda: nc.vector.tensor_tensor(ln, ln, is0, ALU.add),
                                lambda: nc.vector.scalar_tensor_tensor(dtv, dx, 0.0, ln, ALU.max, ALU.add)):
                        ch.mark(ins())
                        ch.wait()
                    nc.vector.scalar_tensor_tensor(c32(da), c32(dtv), -1.0, over_chunks(SM[:, 64:96]),
                                                   ALU.mult, ALU.mult).then_inc(S("da_ready"), 1)
                if j < 3:
                    group_used(dve, b, k)
                    conv(lambda f: accf(b.set(j), f), lambda f: XBC[:, 4 * j + f], 5,
                         lambda tap, f: prm("ssd_conv_w", 12 * tap + 4 * j + f),
                         lambda f: prm("ssd_conv_b", 4 * j + f), NF)
                elif j < 5:
                    dve.wait_ge(S("u_ready"), j - 2)
                    dve.sem_inc(evacuated, 1)
                else:
                    dve.wait_ge(S("z_ready"), j - 4)
                    dve.sem_inc(evacuated, 1)
                if j == 2:
                    nc.vector.memset(UP[:, :, 0:8], 0.0)
                    nc.vector.memset(UP[:, :, 8 + L:UPW], 0.0).then_inc(S("u_padded"), 1)
                if j == 4:
                    dve.wait_ge(S("u_padded"), 1)

                    def window(dst, src, t0, reach, a, z):
                        ch.mark(nc.vector.tensor_tensor(dst[:, t0:8, a:z], src[:, t0:8, a - reach[0]:z - reach[0]],
                                                        src[:, t0:8, a + reach[1]:z + reach[1]], ALU.add))
                        ch.wait()
                    window(SA, UP, 0, (1, 0), 1, UPW)
                    window(SB, SA, 2, (1, 1), 2, UPW - 1)
                    nc.vector.tensor_copy(MIXED[:, 0:2], SA[:, 0:2, 8:8 + L])
                    window(SA, SB, 4, (2, 2), 4, UPW - 3)
                    nc.vector.tensor_copy(MIXED[:, 2:4], SB[:, 2:4, 8:8 + L])
                    window(SB, SA, 6, (4, 4), 8, UPW - 7)
                    nc.vector.tensor_copy(MIXED[:, 4:6], SA[:, 4:6, 8:8 + L])
                    ch.mark(nc.vector.tensor_copy(MIXED[:, 6:8], SB[:, 6:8, 8:8 + L]))
                    ch.wait()
                    dve.wait_ge(S("inv_landed"), 64)
                    for g in range(4):
                        m = MIXED[:, 2 * g:2 * g + 2]
                        ch.mark(nc.vector.tensor_tensor(m, m, INV[:, g:g + 1].to_broadcast([P, 2, L]), ALU.mult))
                    ch.wait()
                    nc.vector.tensor_tensor(MIXED, MIXED, UP[:, :, 8:8 + L], ALU.subtract
                                            ).then_inc(S("mixed_ready"), 1)

            stream_dve(dve, "in", in_evac)

            nac = SM[:, 320:384]
            off = SM[:, 384:416]
            dve.wait_ge(S("acum_done"), 1)
            ch.mark(nc.vector.tensor_scalar(nac, PS[:, 5, 64:128], -1.0, None, ALU.mult))
            ch.wait()
            nc.vector.tensor_tensor(off[:, 0:16], PS[:, 5, 128:144], c32(nac)[:, 0, 0:16], ALU.add)
            ch.mark(nc.vector.tensor_tensor(off[:, 16:32], PS[:, 5, 144:160], c32(nac)[:, 1, 16:32], ALU.add))
            dve.wait_ge(S("pool_product"), 1)
            for t in range(8):
                ins = nc.vector.tensor_scalar(Y[:, 8 + t], PS[:, t // 2, (t % 2) * L:(t % 2) * L + L],
                                              prm("pool_scale", t), None, ALU.mult)
                if t % 4 == 3:
                    ins.then_inc(S("pool_scaled"), 1)
            dve.wait_ge(S("xs_turned"), 1)
            for d in range(2):
                for c in range(2):
                    ins = nc.vector.tensor_tensor(
                        XDT[:, d, c],
                        PS[:, 2 * c:2 * c + 2, :].rearrange("p b (h n) -> p (b h) n", n=64),
                        c32(dtv)[:, c, 16 * d:16 * d + 16].rearrange("p (h o) -> p h o", o=1
                                                                     ).to_broadcast([P, 16, 64]), ALU.mult)
            ins.then_inc(S("xdt_ready"), 1)
            dve.wait_ge(S("cb_done"), 1)
            for g in range(2):
                cb = PS[:, 4 if g == 0 else 7, :].rearrange("p (c l) -> p c l", c=2)
                for d, mask in enumerate(("upto", "from")):
                    nc.vector.tensor_tensor(CBM[:, g, d, 0], cb[:, 0, 0:P], const(mask), ALU.mult)
                    nc.vector.tensor_copy(CBM[:, g, d, 1], cb[:, 0, P:L] if d == 0 else cb[:, 1, 0:P])
                    ins = nc.vector.tensor_tensor(CBM[:, g, d, 2], cb[:, 1, P:L], const(mask), ALU.mult)
            ins.then_inc(S("cbm_ready"), 1)
            dve.wait_ge(S("cbm_ready"), 1)
            ch.wait()

            def exponents(n):
                t, e, d = SSD_STEPS[n]
                h = 16 * d + 2 * t + e
                row = PS[:, 4 + n % 2, 0:L]
                dve.wait_ge(S("row_ready"), n + 1)
                for blk, (l0, col) in enumerate(((0, nac[:, h:h + 1]),
                                                 (P if d == 0 else 0, off[:, h:h + 1]),
                                                 (P, nac[:, 32 + h:33 + h]))):
                    ins = nc.vector.tensor_scalar(ER[:, n % 4, blk * P:blk * P + P], row[:, l0:l0 + P], col, 0.0,
                                                  ALU.add, ALU.min)
                ins.then_inc(S("exponent_ready"), 1)

            def gate_y(t):
                dve.wait_ge(S("y_product"), 4 * t + 4)
                ch.mark(nc.vector.scalar_tensor_tensor(Y[:, t], XBC[:, t], prm("ssd_d", t), PS[:, 6 + t % 2, 0:L],
                                                       ALU.mult, ALU.add))
                ch.wait()
                nc.vector.tensor_tensor(Y[:, t], Y[:, t], SZ[:, t], ALU.mult).then_inc(S("y_gated"), 1)

            exponents(0)
            exponents(1)
            for n, (t, e, d) in enumerate(SSD_STEPS):
                if n + 2 < len(SSD_STEPS):
                    exponents(n + 2)
                dve.wait_ge(S("decay_ready"), n + 1)
                if n >= 4:
                    dve.wait_ge(S("y_product"), n - 3)
                nc.vector.tensor_tensor(MR[:, n % 4], ER[:, n % 4], CBM[:, t // 4, d].rearrange("p b l -> p (b l)"),
                                        ALU.mult).then_inc(S("mix_matrix"), 1)
                if n % 4 == 1 and t > 0:
                    gate_y(t - 1)
            gate_y(7)
            dve.wait_ge(S("y_std"), 1)
            ch.mark(nc.vector.reciprocal(ST[:, :], ST[:, :]))
            ch.wait()
            dve.wait_ge(S("y_gated"), 8)
            for t in range(8):
                nc.vector.scalar_tensor_tensor(Y[:, t], Y[:, t], prm("ssd_norm", t),
                                               ST[:, (t // 4) * L:(t // 4) * L + L], ALU.mult, ALU.mult
                                               ).then_inc(S("y_normed"), 1)
            for i, q in enumerate((2, 3, 0, 1)):
                dve.wait_ge(S("mix_hi"), i + 1)
                nc.vector.tensor_tensor(XS[:, 4 * q:4 * q + 4, 1], Y[:, 4 * q:4 * q + 4],
                                        r(XS[:, 4 * q:4 * q + 4, 0]), ALU.subtract).then_inc(S("mix_split"), 1)

            stream_dve(dve, "out", out_dve(dve))
            all_evacuated(dve, "out")
            post_dve(dve, ch, "mix_post", OUT1, "mix_post")
            dve.wait_ge(S("mix_post_added"), 4)
            pre_dve(dve, ch, "ffn_pre", H, lambda t: prm("ffn_pre", t), XS)

            def up_evac(b, j, k):
                group_used(dve, b, k)
                if j == 0:
                    ch.start(b, 8)
                    w = [lambda f: prm_dyn("ffn_w0", b.n(NF, f)), lambda f: prm_dyn("ffn_w1", b.n(NF, f)),
                         lambda f: prm_dyn("ffn_w2", b.n(NF, f))]
                    conv(lambda f: accf(b.set(j), f), lambda f: evA[:, f], 3, lambda tap, f: w[tap](f),
                         lambda f: prm_dyn("ffn_b", b.n(NF, f)), NF)
                    ch.end(b)
                else:
                    dve.wait_ge(S("gate_gelu"), b.n(1, 1))
                    nc.vector.tensor_tensor(evB, acc(b.set(j)), evA, ALU.mult).then_inc(evacuated, 1)
                    dve.wait_ge(S("hidden_hi"), b.n(1, 1))
                    dve.wait_ge(evacuated, b.group(j) + 3)
                    at = bass.ds(b.n(NF, 0), NF)
                    nc.vector.tensor_tensor(HID[:, at, 1], evB, r(HID[:, at, 0]), ALU.subtract
                                            ).then_inc(S("hidden_split"), 1)

            stream_dve(dve, "up", up_evac)
            stream_dve(dve, "down", down_dve(dve))
            all_evacuated(dve, "down")
            post_dve(dve, ch, "ffn_post", OUT2, "ffn_post")
            dve.wait_ge(S("p_hi"), 1)
            nc.vector.tensor_tensor(PSP[:, :, 1], PTR, r(PSP[:, :, 0]), ALU.subtract).then_inc(S("p_split"), 1)
            dve.wait_ge(S("ffn_post_added"), 4)
            pre_dve(dve, ch, "ple_pre", H, lambda t: prm("ple_pre", t), XS)

            def ple_evac(b, j, k):
                group_used(dve, b, k)
                nc.vector.tensor_copy(PLE[:, NF * j:NF * j + NF], acc(b.set(j))).then_inc(evacuated, 1)

            stream_dve(dve, "ple", ple_evac)

            def gate_evac(b, j, k):
                dve.wait_ge(S("gate_ready"), b.local(j) + 1)
                at = bass.ds(b.local(j) * NF, NF)
                nc.vector.tensor_tensor(OUT3[:, at], evA, PLE[:, at], ALU.mult).then_inc(evacuated, 1)

            all_evacuated(dve, "ple")
            stream_dve(dve, "gate", gate_evac)
            all_evacuated(dve, "gate")
            post_dve(dve, ch, "ple_post", OUT3, "ple_post")

            def ada_bias(t0, t1):
                ch.mark(nc.vector.tensor_tensor(
                    MADA[:, t0:t1], MADA[:, t0:t1],
                    prm("b_ada", t0, t1 - t0).rearrange("p (t o) -> p t o", o=1).to_broadcast([P, t1 - t0, 2]),
                    ALU.add))

            def gain_eff(i, m, v, name):
                ch.mark(nc.vector.scalar_tensor_tensor(GE[:, i], MADA[:, m * KT:(m + 1) * KT, v], 1.0,
                                                       prm(name, 0, KT), ALU.add, ALU.mult))

            def ada_done(name):
                ph = PHASES[name]
                dve.wait_ge(ada_evacuated, 1 + ph.ada0 + ph.ada * ph.times)

            ada_done("gate")
            ada_bias(0, 2 * KT)
            ch.wait()
            gain_eff(0, 1, 0, "norm1")
            gain_eff(1, 1, 1, "norm1")
            ch.wait()
            dve.sem_inc(S("mod1_ready"), 1)
            dve.wait_ge(S("ple_post_added"), 4)
            pre_dve(dve, ch, "norm1", H, lambda t: GE[:, 0, t:t + 1], XS, shift=lambda t: MADA[:, t, 0:1])
            dve.wait_ge(S("ctx_turned"), 1)
            nc.vector.tensor_copy(CTX[:, 0:8], PS[:, 0:4, :].rearrange("p b (h n) -> p (b h) n", h=2)
                                  ).then_inc(S("ctx_loaded_dve"), 1)
            dve.wait_ge(S("ctx_loaded_act"), 1)
            dve.wait_ge(S("ctx_loaded_dve"), 1)
            pre_dve(dve, ch, "norm_c", CTX, lambda t: GE[:, 1, t:t + 1], CS, shift=lambda t: MADA[:, t, 1:2])

            def kv_evac(b, j, k):
                group_used(dve, b, k)
                s = b.set(j)
                dve.wait_ge(S("kv_half"), b.local(j) + 1)
                nc.vector.tensor_copy(KV[:, bass.ds(b.local(j) * NF, 2)], PS[:, 4 * s:4 * s + 2, :]
                                      ).then_inc(evacuated, 1)

            def q_evac(b, j, k):
                group_used(dve, b, k)
                nc.vector.tensor_copy(Q[:, bass.ds(b.local(j) * NF, NF)], acc(b.set(j))).then_inc(evacuated, 1)

            stream_dve(dve, "kv", kv_evac)
            stream_dve(dve, "q", q_evac)
            all_evacuated(dve, "q")
            ada_done("q")
            ada_bias(2 * KT, 6 * KT)
            ch.wait()
            gain_eff(2, 4, 0, "norm2")

            gains = {"k_norm_a": prm("k_norm_a"), "k_norm_b": prm("k_norm_b"), "q_norm_a": SM[:, 4:5],
                     "q_norm_b": SM[:, 5:6]}

            def qk_norm(i):
                x, n, g, _ = QK[i]
                dve.wait_ge(S("qk_std"), i + 1)
                ch.mark(nc.vector.reciprocal(QK_ST[i % 2][:, 0:n], QK_ST[i % 2][:, 0:n]))
                ch.wait()
                nc.vector.scalar_tensor_tensor(x, x, gains[g], QK_ST[i % 2][:, 0:n], ALU.mult,
                                               ALU.mult).then_inc(S("qk_normed"), 1)

            def qk_rope(i):
                x, _, _, kind = QK[i]
                t1, t2 = QK_T[:, 2 * (i % 2)], QK_T[:, 2 * (i % 2) + 1]
                dve.wait_ge(S("qk_normed"), i + 1)
                nc.vector.tensor_tensor(t1, x[:, 0:L], const("cos_" + kind), ALU.mult)
                dve.wait_ge(S("qk_turned"), i + 1)
                ch.mark(nc.vector.tensor_tensor(t2, PS[:, 6 + i % 2, 0:L], const("sin_" + kind), ALU.mult))
                ch.wait()
                nc.vector.tensor_tensor(x[:, 0:L], t1, t2, ALU.add).then_inc(S("qk_roped"), 1)

            qk_norm(0)
            for i in range(len(QK)):
                if i + 1 < len(QK):
                    qk_norm(i + 1)
                qk_rope(i)

            def maxima(rd):
                for n in JOBS[rd]:
                    dve.wait_ge(S("scores_ready"), n + 1)
                    nc.vector.tensor_reduce(NEGMAX[:, n:n + 1], PS[:, 2 + n % 4, :], AX.X, ALU.max,
                                            negate=True).then_inc(S("max_ready"), 1)

            def probabilities(rd):
                js = JOBS[rd]
                dve.wait_ge(S("exp_ready"), js[-1] + 1)
                ch.mark(nc.vector.reciprocal(RSUM[:, js[0]:js[-1] + 1], SUMS[:, js[0]:js[-1] + 1]))
                ch.wait()
                p0 = PR[:, js[0] % 4]
                ins = nc.vector.tensor_scalar(p0, p0, RSUM[:, js[0]:js[0] + 1], None, ALU.mult)
                if len(js) == 2:
                    ch.mark(ins)
                    n = js[1]
                    ch.mark(nc.vector.tensor_tensor(RSUM[:, n:n + 1], RSUM[:, n:n + 1], SM[:, 3:4], ALU.mult))
                    ch.wait()
                    ins = nc.vector.scalar_tensor_tensor(p0, PR[:, n % 4], RSUM[:, n:n + 1], p0, ALU.mult, ALU.add)
                ins.then_inc(S("p_ready"), 1)

            def output(hd):
                dve.wait_ge(S("pv_done"), hd + 1)
                nc.vector.tensor_copy(Q[:, hd], PS[:, hd % 2, 0:L]).then_inc(S("o_ready"), 1)

            maxima(0)
            for rd in range(len(ROUNDS)):
                if rd + 1 < len(ROUNDS):
                    maxima(rd + 1)
                probabilities(rd)
                if rd % 2 == 1 and rd >= 3:
                    output(rd // 2 - 1)
            output(23)
            dve.wait_ge(S("sub_std"), 1)
            ch.mark(nc.vector.reciprocal(SUBST, SUBST))
            ch.wait()
            dve.wait_ge(S("o_ready"), 24)
            for i in range(8):
                nc.vector.scalar_tensor_tensor(Q[:, 16 + i], Q[:, 16 + i], SM[:, 6:7], SUBST[:, i], ALU.mult,
                                               ALU.mult).then_inc(S("o_normed"), 1)
            for q in range(6):
                dve.wait_ge(S("o_hi"), q + 1)
                nc.vector.tensor_tensor(OS[:, 4 * q:4 * q + 4, 1], Q[:, 4 * q:4 * q + 4],
                                        r(OS[:, 4 * q:4 * q + 4, 0]), ALU.subtract).then_inc(S("o_split"), 1)

            def branch_evac(b, j, k):
                at = bass.ds(b.n(NF, 0), NF)
                if j % 2 == 0:
                    dve.wait_ge(S("branch_gate"), b.n(2, 1 + j // 2))
                    dve.sem_inc(evacuated, 1)
                elif j == 1:
                    group_used(dve, b, k)
                    nc.vector.tensor_tensor(MG[:, at], acc(b.set(j)), evA, ALU.mult).then_inc(evacuated, 1)
                else:
                    group_used(dve, b, k)
                    nc.vector.tensor_tensor(evB, acc(b.set(j)), evA, ALU.mult).then_inc(evacuated, 1)
                    dve.wait_ge(evacuated, b.group(j) + 3)
                    nc.vector.tensor_tensor(MG[:, at], MG[:, at], evB, ALU.add).then_inc(S("merged"), 1)

            stream_dve(dve, "branch", branch_evac)
            dve.wait_ge(S("merged"), 4)
            for q in range(4):
                dve.wait_ge(S("merged_hi"), q + 1)
                nc.vector.tensor_tensor(XS[:, 4 * q:4 * q + 4, 1], MG[:, 4 * q:4 * q + 4],
                                        r(XS[:, 4 * q:4 * q + 4, 0]), ALU.subtract).then_inc(S("merged_split"), 1)

            def gated_residual(m):
                def evac(b, j, k):
                    group_used(dve, b, k)
                    for f in range(NF):
                        t = bass.ds(b.local(j) * NF + f, 1)
                        h = H[:, t].rearrange("p o n -> p (o n)")
                        ins = nc.vector.scalar_tensor_tensor(
                            h, accf(b.set(j), f), MADA[:, bass.ds(b.local(j) * NF + (m * KT + f), 1), 0], h,
                            ALU.mult, ALU.add)
                    ins.then_inc(evacuated, 1)
                return evac

            stream_dve(dve, "out2", gated_residual(2))
            all_evacuated(dve, "out2")
            pre_dve(dve, ch, "norm2", H, lambda t: GE[:, 2, t:t + 1], XS, shift=lambda t: MADA[:, 3 * KT + t, 0:1])

            def up2_evac(b, j, k):
                if j == 0:
                    dve.wait_ge(S("gate2_silu"), b.n(1, 1))
                    dve.sem_inc(evacuated, 1)
                else:
                    group_used(dve, b, k)
                    nc.vector.tensor_tensor(evB, acc(b.set(j)), evA, ALU.mult).then_inc(evacuated, 1)
                    dve.wait_ge(S("hidden2_hi"), b.n(1, 1))
                    dve.wait_ge(evacuated, b.group(j) + 3)
                    at = bass.ds(b.n(NF, 0), NF)
                    nc.vector.tensor_tensor(HID[:, at, 1], evB, r(HID[:, at, 0]), ALU.subtract
                                            ).then_inc(S("hidden2_split"), 1)

            stream_dve(dve, "up2", up2_evac)
            stream_dve(dve, "down2", gated_residual(5))
            dve.wait_ge(S("out_turned"), 1)
            nc.vector.tensor_copy(ONAT[:, 0, :], PS[:, 0:4, :].rearrange("p b n -> p (b n)")
                                  ).then_inc(S("out_copied_dve"), 1)

        @block.tensor
        def _(pe):
            pe.sem_inc(w_used, RING)
            ident = const("ident")
            pe.wait_ge(S("consts_landed"), 16)
            pe.wait_ge(S("params_landed"), 16 * N_PARAM_LOADS)
            for i, n in enumerate(PARAM_USED):
                nc.tensor.transpose(PS[:, i // 4, (i % 4) * P:(i % 4) * P + n], PROW[0:n, i, :], ident[0:n, 0:n])
            pe.wait_ge(S("d_rows"), 1)
            nc.tensor.transpose(PS[:, 1, P:P + 8], DROW[0:8], ident[0:8, 0:8]).then_inc(S("params_pe"), 1)

            def turn(src, done):
                for t in range(KT):
                    for c in range(2):
                        ins = nc.tensor.transpose(PS[:, t // 2, (t % 2) * L + c * P:(t % 2) * L + c * P + P],
                                                  src[:, c, t * P:t * P + P], ident)
                ins.then_inc(S(done), 1)

            pe.wait_ge(S("params_turned"), 1)
            pe.wait_ge(S("x_landed"), 32)
            turn(XNAT, "x_turned")
            pe.wait_ge(S("h_loaded_act"), 1)
            pe.wait_ge(S("h_loaded_dve"), 1)
            stat_pe(pe, "mix_pre", SQ, 4)
            pe.wait_ge(S("wdt_landed"), 16)
            pe.wait_ge(S("mix_pre_z"), 16)
            for c in range(2):
                for t in range(KT):
                    mm = nc.tensor.matmul(PS[:, 5, 32 * c:32 * c + 32], Z[:, t, c * P:c * P + P], WDT[:, t],
                                          start=c == 0 and t == 0, stop=t == KT - 1, skip_group_check=True)
            mm.then_inc(S("dt_projected"), 1)
            pe.wait_ge(S("mix_pre_ready"), 4)
            stream_pe(pe, "in", split_rhs(XS))

            da = SM[:, 256:320].rearrange("p (c h) -> p c h", c=2)
            pe.wait_ge(S("da_ready"), 1)
            for c in range(2):
                for d, tri in enumerate(("upto", "from")):
                    nc.tensor.matmul(PS[:, 5, 64 + 32 * c + 16 * d:80 + 32 * c + 16 * d], const(tri),
                                     da[:, c, 16 * d:16 * d + 16], start=c == 0 and d == 0, stop=True,
                                     skip_group_check=True)
            for d in range(2):
                nc.tensor.matmul(PS[:, 5, 128 + 16 * d:144 + 16 * d], const("ones"), da[:, d, 16 * d:16 * d + 16],
                                 start=False, stop=True, skip_group_check=True)
            for d, tri in enumerate(("upto", "from")):
                for c in range(2):
                    mm = nc.tensor.matmul(PS[0:32, 6, d * L + c * P:d * L + c * P + P], da[:, c], const(tri),
                                          start=c == 0 and d == 0, stop=True, skip_group_check=True)
            mm.then_inc(S("acum_done"), 1)
            all_evacuated(pe, "in")
            pe.wait_ge(S("mixed_ready"), 1)
            pe.wait_ge(S("poolw_landed"), 16)
            for g in range(4):
                for f in range(2):
                    for t in range(2):
                        mm = nc.tensor.matmul(PS[:, g, f * L:f * L + L], PW[:, g, t, f * P:f * P + P],
                                              MIXED[:, 2 * g + t], start=f == 0 and t == 0, stop=t == 1,
                                              skip_group_check=True)
            mm.then_inc(S("pool_product"), 1)
            pe.wait_ge(S("xbc_ready"), 3)
            for g in range(2):
                for c in range(2):
                    mm = nc.tensor.matmul(PS[:, 4 if g == 0 else 7, c * L:c * L + L],
                                          XBC[:, 8 + g, c * P:c * P + P], XBC[:, 10 + g], start=c == 0, stop=True,
                                          skip_group_check=True)
            mm.then_inc(S("cb_done"), 1)
            pe.wait_ge(S("pool_scaled"), 2)
            for c in range(2):
                for t in range(8):
                    ins = nc.tensor.transpose(PS[:, 2 * c + t // 4, (t % 4) * P:(t % 4) * P + P],
                                              XBC[:, t, c * P:c * P + P], ident)
            ins.then_inc(S("xs_turned"), 1)
            pe.wait_ge(S("sel_landed"), 16)
            pe.wait_ge(S("acum_rows"), 1)
            pe.wait_ge(S("cbm_ready"), 1)
            pe.wait_ge(S("xdt_ready"), 1)

            def row(n):
                t, e, d = SSD_STEPS[n]
                if n >= 2:
                    pe.wait_ge(S("exponent_ready"), n - 1)
                nc.tensor.matmul(PS[:, 4 + n % 2, 0:L], SEL[0:32, 16 * d + 2 * t + e], ST[0:32, d * L:d * L + L],
                                 start=True, stop=True, skip_group_check=True).then_inc(S("row_ready"), 1)

            row(0)
            row(1)
            for n, (t, e, d) in enumerate(SSD_STEPS):
                if n + 2 < len(SSD_STEPS):
                    row(n + 2)
                if n % 4 == 0 and t >= 2:
                    pe.wait_ge(S("y_gated"), t - 1)
                pe.wait_ge(S("mix_matrix"), n + 1)
                to = PS[64 * e:64 * e + 64, 6 + t % 2, 0:L]
                m = MR[:, n % 4]
                h = 2 * t + e
                if d == 0:
                    nc.tensor.matmul(to, XDT[:, 0, 0, h], m[:, 0:L], start=True, stop=False,
                                     skip_group_check=True)
                    mm = nc.tensor.matmul(to[:, P:L], XDT[:, 0, 1, h], m[:, L:L + P], start=False, stop=False,
                                          skip_group_check=True)
                else:
                    nc.tensor.matmul(to[:, 0:P], XDT[:, 1, 0, h], m[:, 0:P], start=False, stop=False,
                                     skip_group_check=True)
                    mm = nc.tensor.matmul(to, XDT[:, 1, 1, h], m[:, P:L + P], start=False, stop=True,
                                          skip_group_check=True)
                mm.then_inc(S("y_product"), 1)
            for t in range(8):
                pe.wait_ge(S("y_sq"), t // 4 + 1)
                mm = nc.tensor.matmul(PS[:, 4, (t // 4) * L:(t // 4) * L + L], const("ones"), YSQ[:, t],
                                      start=t == 0, stop=t % 4 == 3, skip_group_check=True)
            mm.then_inc(S("y_stat"), 1)

            pe.wait_ge(S("mix_split"), 4)
            stream_pe(pe, "out", split_rhs(XS))
            stat_pe(pe, "mix_post", OSQ1, 4)
            stat_pe(pe, "ffn_pre", SQ, 4)
            pe.wait_ge(S("cond_split"), 1)
            pe.wait_ge(S("ffn_pre_ready"), 4)
            stream_pe(pe, "up", split_rhs(XS))
            pe.wait_ge(S("hidden_split"), PHASES["up"].times)
            stream_pe(pe, "down", split_rhs(HID))
            stat_pe(pe, "ffn_post", OSQ2, 4)
            pe.wait_ge(S("p_landed"), 32)
            for t in range(2):
                for c in range(2):
                    ins = nc.tensor.transpose(PS[:, 5, t * L + c * P:t * L + c * P + P], PNAT[:, c, t * P:t * P + P],
                                              ident)
            ins.then_inc(S("p_turned"), 1)
            stat_pe(pe, "ple_pre", SQ, 4)
            pe.wait_ge(S("p_split"), 1)
            stream_pe(pe, "ple", split_rhs(PSP))
            pe.wait_ge(S("ple_pre_ready"), 4)
            stream_pe(pe, "gate", split_rhs(XS))
            stat_pe(pe, "ple_post", OSQ3, 4)
            stat_pe(pe, "norm1", SQ, 4)
            pe.wait_ge(S("norm1_std"), 1)
            all_evacuated(pe, "gate")
            pe.wait_ge(ada_evacuated, 1 + PHASES["kv"].ada0)
            pe.wait_ge(S("ctx_landed"), 32)
            turn(CNAT, "ctx_turned")
            pe.wait_ge(S("ctx_loaded_act"), 1)
            pe.wait_ge(S("ctx_loaded_dve"), 1)
            stat_pe(pe, "norm_c", SQ, 4)
            pe.wait_ge(S("norm1_ready"), 4)
            pe.wait_ge(S("norm_c_ready"), 4)
            kv_stream(pe)
            all_evacuated(pe, "kv")
            stream_pe(pe, "q", split_rhs(XS))

            all_evacuated(pe, "q")

            def qk_stat(i):
                n, kind = QK[i][1], QK[i][3]
                pe.wait_ge(S("qk_sq"), i + 1)
                if i >= 2:
                    pe.wait_ge(S("qk_std"), i - 1)
                nc.tensor.matmul(PS[:, 4 + i % 2, 0:n], const("ones" if kind == "a" else "half"),
                                 QK_SQ[:, i % 2, 0:n], start=True, stop=True,
                                 skip_group_check=True).then_inc(S("qk_stat"), 1)

            qk_stat(0)
            for i in range(len(QK)):
                if i + 1 < len(QK):
                    qk_stat(i + 1)
                pe.wait_ge(S("qk_normed"), i + 1)
                if i >= 2:
                    pe.wait_ge(S("qk_roped"), i - 1)
                nc.tensor.matmul(PS[:, 6 + i % 2, 0:L], const("rot_" + QK[i][3]), QK[i][0][:, 0:L], start=True,
                                 stop=True, skip_group_check=True).then_inc(S("qk_turned"), 1)
            for i, j in enumerate(V_TILES):
                if i >= 4:
                    pe.wait_ge(S("v_ready"), i - 3)
                for c in range(4):
                    ins = nc.tensor.transpose(PS[:, i % 4, c * P:c * P + P], KV[:, j, c * P:c * P + P], ident)
                ins.then_inc(S("v_turned"), 1)
            pe.wait_ge(S("qk_roped"), len(QK))
            pe.wait_ge(S("v_ready"), len(V_TILES))

            def scores(rd):
                br, h, qb = ROUNDS[rd]
                for i, n in enumerate(JOBS[rd]):
                    if n >= 4:
                        pe.wait_ge(S("exp_ready"), n - 3)
                    if br == "a":
                        q, k = Q[:, h, qb * P:qb * P + P], KV[:, h // 4]
                    else:
                        rows = slice(64 * i, 64 * i + 64)
                        q, k = Q[rows, 16 + h, qb * P:qb * P + P], KV[rows, 8 + h]
                    nc.tensor.matmul(PS[:, 2 + n % 4, :], q, k, start=True, stop=True,
                                     skip_group_check=True).then_inc(S("scores_ready"), 1)

            def values(hd):
                j = 4 + hd // 4 if hd < 16 else hd
                pe.wait_ge(S("pt_ready"), 2 * hd + 2)
                if hd >= 2:
                    pe.wait_ge(S("o_ready"), hd - 1)
                for c in range(4):
                    mm = nc.tensor.matmul(PS[:, hd % 2, 0:L], KV[:, j, c * P:c * P + P], PTT[:, hd % 2, c],
                                          start=c == 0, stop=c == 3, skip_group_check=True)
                mm.then_inc(S("pv_done"), 1)

            scores(0)
            scores(1)
            for rd in range(len(ROUNDS)):
                if rd + 2 < len(ROUNDS):
                    scores(rd + 2)
                pe.wait_ge(S("p_ready"), rd + 1)
                if rd >= 2:
                    pe.wait_ge(S("pt_ready"), rd - 1)
                for c in range(4):
                    ins = nc.tensor.transpose(PS[:, 6 + rd % 2, c * P:c * P + P],
                                              PR[:, JOBS[rd][0] % 4, c * P:c * P + P], ident)
                ins.then_inc(S("p_turn"), 1)
                if rd % 2 == 0 and rd >= 2:
                    values(rd // 2 - 1)
            values(23)
            for i in range(8):
                pe.wait_ge(S("sub_sq"), i // 4 + 1)
                mm = nc.tensor.matmul(PS[:, 2 + i // 2, (i % 2) * L:(i % 2) * L + L], const("ones"), SUBSQ[:, i],
                                      start=i % 2 == 0, stop=True, skip_group_check=True)
            mm.then_inc(S("sub_stat"), 1)
            pe.wait_ge(S("sub_std"), 1)
            pe.wait_ge(S("o_split"), 6)
            branch_rhs = [split_rhs(XS), split_rhs(OS), split_rhs(XS), split_rhs(OS, KT)]
            stream_pe(pe, "branch", lambda j, k: branch_rhs[j](j, k))
            pe.wait_ge(S("merged_split"), 4)
            stream_pe(pe, "out2", split_rhs(XS))
            stat_pe(pe, "norm2", SQ, 4)
            pe.wait_ge(S("norm2_ready"), 4)
            stream_pe(pe, "up2", split_rhs(XS))
            pe.wait_ge(S("hidden2_split"), PHASES["up2"].times)
            stream_pe(pe, "down2", split_rhs(HID))
            all_evacuated(pe, "down2")
            for c in range(2):
                for t in range(KT):
                    ins = nc.tensor.transpose(PS[:, 4 * c + t // 4, (t % 4) * P:(t % 4) * P + P],
                                              H[:, t, c * P:c * P + P], ident)
                ins.then_inc(S("out_turned"), 1)


NAMES = [
    "x", "p", "mix_norm_pre", "mix_norm_post", "w_in", "ssd_conv_w", "ssd_conv_b", "ssd_dt_bias",
    "ssd_a_log", "ssd_d", "ssd_norm", "pool_w", "pool_scale", "w_out", "ffn_norm_pre",
    "ffn_norm_post", "w_ffn_up", "ffn_conv_w", "ffn_conv_b", "w_ffn_down", "ple_norm_pre",
    "w_ple_gate", "w_ple", "ple_norm_post", "c_2", "ctx_2", "c_ctx_2", "w_ada_2", "b_ada_2",
    "norm1_g_2", "w_in_2", "q_norm_a_2", "k_norm_a_2", "q_norm_b_2", "k_norm_b_2", "lam_q1_2",
    "lam_k1_2", "lam_q2_2", "lam_k2_2", "subln_g_2", "w_br_a_2", "w_br_b_2", "w_out_2",
    "norm2_g_2", "w_ff_gate_2", "w_ff_up_2", "w_ff_down_2",
]


def kernel(**inputs):
    import concourse.bacc as bacc
    from concourse.bass_utils import run_bass_kernel_spmd

    nc = bacc.Bacc("TRN2", target_bir_lowering=False, num_devices=1)
    arrays, aps = {}, {}
    for name in NAMES:
        a = np.ascontiguousarray(inputs[name])
        arrays[f"in_{name}"] = a
        aps[name] = nc.dram_tensor(f"in_{name}", a.shape, F32, kind="ExternalInput").ap()
    tables = []
    for name, a in zip(("constants", "selectors", "inverse_counts"), constant_tables()):
        arrays[f"in_{name}"] = a
        tables.append(nc.dram_tensor(f"in_{name}", a.shape, F32, kind="ExternalInput").ap())
    out = nc.dram_tensor("out", (1, L, D), F32, kind="ExternalOutput").ap()
    build(nc, aps, out, tables)
    got = run_bass_kernel_spmd(nc, [arrays], core_ids=[0])
    return got.results[0]["out"]
```

```python
from contextlib import ExitStack

import numpy as np

import concourse.bass as bass
from concourse import mybir

F32 = mybir.dt.float32
F32R = mybir.dt.float32r
ALU = mybir.AluOpType
ACT = mybir.ActivationFunctionType
AX = mybir.AxisListType

P = 128
L = 256
D = 2048
KT = D // P
DFF = 5632
FT = DFF // P
RING = 4
GC = 512
NF = GC // P
EPS = 1e-6
SSD_H = 16
LAM_INIT = 0.2

PARAM_ROWS = {
    "mix_pre": 0, "mix_post": 16, "ffn_pre": 32, "ffn_post": 48, "ple_pre": 64, "ple_post": 80,
    "norm1": 96, "norm2": 112,
    "ssd_conv_w": 128, "ssd_conv_b": 188, "ssd_norm": 200, "pool_scale": 208, "ssd_d": 216,
    "b_ada": 256, "q_norm_a": 352, "k_norm_a": 353, "q_norm_b": 354, "k_norm_b": 355, "subln": 356,
    "ffn_w0": 384, "ffn_w1": 428, "c": 472, "c_ctx": 488,
    "ffn_w2": 512, "ffn_b": 556,
}
PARAM_USED = [128, 88, 101, 120, 88]
N_PARAM_LOADS = 33

CONST = {}
_at = 0
for _name, _n in (("ident", 128), ("ones", 128), ("half", 128), ("rot_a", 128), ("rot_b", 128),
                  ("upto", 128), ("from", 128), ("cos_a", 256), ("sin_a", 256), ("cos_b", 256),
                  ("sin_b", 256)):
    CONST[_name] = (_at, _n)
    _at += _n
NCONST = _at


def constant_tables():
    c = np.zeros((P, NCONST), np.float32)
    i, j = np.arange(P)[:, None], np.arange(P)[None, :]

    def put(name, a):
        at, n = CONST[name]
        c[:, at:at + n] = a

    put("ident", i == j)
    put("ones", 1.0)
    put("half", i // 64 == j // 64)
    for name, sub in (("rot_a", 128), ("rot_b", 64)):
        half = sub // 2
        put(name, np.where((j % sub < half) & (i == j + half), -1.0, 0.0)
            + np.where((j % sub >= half) & (i == j - half), 1.0, 0.0))
    put("upto", i <= j)
    put("from", i >= j)
    t = np.arange(L)
    for name, hd in (("a", 128), ("b", 64)):
        n = hd // 4
        freqs = (np.float32(10000.0) ** (-np.arange(n, dtype=np.float32) / np.float32(n))).astype(np.float32)
        row, col = (t // 64).astype(np.float32), (t % 64).astype(np.float32)
        ang = np.concatenate([row[:, None] * freqs, col[:, None] * freqs], axis=1).T
        rows = np.arange(P) % (hd // 2)
        put("cos_" + name, np.cos(ang)[rows])
        put("sin_" + name, np.sin(ang)[rows])
    sel = (np.arange(32)[:, None] == (np.arange(32 * P)[None, :] // P)).astype(np.float32)
    inv = np.zeros((4, L), np.float32)
    for g, k in enumerate((2, 4, 8, 16)):
        lo, hi = np.clip(t - k // 2, 0, L), np.clip(t + k - k // 2, 0, L)
        inv[g] = 1.0 / (hi - lo).astype(np.float32)
    return c, sel, inv


class Phase:

    def __init__(self, Us, times, ada_cols=(0,)):
        self.Us, self.times, self.ada_cols = Us, times, ada_cols
        ada = self.ada = len(ada_cols) if times == 1 else ada_cols[1]
        self.units = [(j, u) for j, n in enumerate(Us) for u in range(n)]
        n = len(self.units)
        self.body, self.at, self.after = [], [], [[] for _ in range(n)]
        a = 0
        for i, x in enumerate(self.units):
            self.at.append(len(self.body))
            self.body.append(("g",) + x)
            while a < 8 * ada and (i - RING + 1) * 8 * ada >= (a + 1) * (n - RING):
                self.after[i].append((len(self.body), a // 8, a % 8))
                self.body.append(("a", a // 8, a % 8))
                a += 1
        self.done = [max(n - RING for n, xs in enumerate(self.after) for x in xs if x[1:] == (i, 7))
                     for i in range(ada)]
        assert times == 1 or (n % RING == 0 and len(self.body) % RING == 0 and len(Us) % 2 == 0)


PHASES = {
    "in": Phase([8] * 7, 1, ()),
    "out": Phase([8] * 4, 1, (0, 1, 23)),
    "up": Phase([8, 8], 11, (8, 1)),
    "down": Phase([22, 22], 2, (2, 2)),
    "ple": Phase([1] * 4, 1, ()),
    "gate": Phase([8, 8], 2, (6, 1)),
    "kv": Phase([8, 8], 3, (0, 0)),
    "q": Phase([8, 8], 3, (0, 0)),
    "branch": Phase([8, 8, 8, 4], 4, (19, 1)),
    "out2": Phase([8, 8], 2, (0, 0)),
    "up2": Phase([8, 8], 11, (0, 0)),
    "down2": Phase([22] * 4, 1, ()),
}
_u = _n = _g = _a = 0
for _p in PHASES.values():
    _p.load0, _p.unit0, _p.group0, _p.ada0 = _u, _n, _g, _a
    _u += len(_p.body) * _p.times
    _n += len(_p.units) * _p.times
    _g += len(_p.Us) * _p.times
    _a += _p.ada * _p.times
UNITS, ADA_GROUPS = _n, _a
assert ADA_GROUPS == 6 * D // GC


class Body:

    def __init__(self, ph, i, rep):
        self.ph, self.i, self.rep = ph, i, rep

    def _of(self, base, per, k):
        if self.i is None:
            return base + self.rep * per + k
        return self.i * per + (base + k)

    def load(self, k):
        return self._of(self.ph.load0, len(self.ph.body), k)

    def unit(self, n):
        return self._of(self.ph.unit0, len(self.ph.units), n)

    def is_last(self, n):
        return self.ph.unit0 + self.rep * len(self.ph.units) + n + RING >= UNITS

    def ahead(self, n):
        n += RING
        return self.ph.at[n] if n < len(self.ph.units) else len(self.ph.body) + n - len(self.ph.units)

    def static_load(self, k):
        return self.ph.load0 + self.rep * len(self.ph.body) + k

    def raw_slot(self, k):
        return self.static_load(k) % RING

    def slot(self, n):
        return (self.ph.unit0 + self.rep * len(self.ph.units) + n) % RING

    def landed(self, k):
        n = self.static_load(k) // RING + 1
        return 16 * n if self.i is None else self.i * (16 * len(self.ph.body) // RING) + 16 * n

    def group(self, j):
        return self._of(self.ph.group0, len(self.ph.Us), j)

    def local(self, j):
        return self._of(0, len(self.ph.Us), j)

    def set(self, j):
        return (self.ph.group0 + self.rep * len(self.ph.Us) + j) % 2

    def ada(self, a):
        return self._of(self.ph.ada0, self.ph.ada, a)

    def ada_col(self, a):
        if self.ph.times == 1:
            return self.ph.ada_cols[a]
        return self._of(self.ph.ada_cols[0], self.ph.ada, a)

    def n(self, per=1, k=0):
        return self._of(0, per, k)


def bodies(eng, name, straight=False):
    ph = PHASES[name]
    if ph.times == 1 or straight or name in ("kv", "q"):
        for rep in range(ph.times):
            yield Body(ph, None, rep)
    else:
        with eng.Fori(0, ph.times) as i:
            yield Body(ph, i, 0)


class Chain:

    def __init__(self, eng, sem):
        self.eng, self.sem, self.n, self.i, self.per = eng, sem, 0, None, 0

    def mark(self, ins):
        ins.then_inc(self.sem, 1)
        self.n += 1
        return self.n

    def wait(self, n=None):
        n = self.n if n is None else n
        self.eng.wait_ge(self.sem, n if self.i is None else self.i * self.per + n)

    def start(self, b, per):
        self.i, self.per, self.n0 = b.i, per, self.n

    def end(self, b):
        assert self.n - self.n0 == self.per, self.n - self.n0
        if b.i is not None:
            self.n = self.n0 + self.per * b.ph.times
        self.i = None


def build(nc, A, out, tables):
    consts_d, sel_d, inv_d = tables

    def ktiles(w):
        return w[0].rearrange("(t p) n -> p t n", p=P)

    W_IN, W_OUT, W_UP, W_DOWN = (ktiles(A[n]) for n in ("w_in", "w_out", "w_ffn_up", "w_ffn_down"))
    W_GATE, W_PLE, W_ADA, W_IN2 = (ktiles(A[n]) for n in ("w_ple_gate", "w_ple", "w_ada_2", "w_in_2"))
    W_BR_A, W_BR_B, W_OUT2 = (ktiles(A[n]) for n in ("w_br_a_2", "w_br_b_2", "w_out_2"))
    W_G2, W_U2, W_D2 = (ktiles(A[n]) for n in ("w_ff_gate_2", "w_ff_up_2", "w_ff_down_2"))

    with ExitStack() as ctx:
        def sb(name, shape, dt=F32):
            return ctx.enter_context(nc.sbuf_tensor(name, shape, dt))

        def freed(name, shape, dt):
            with nc.sbuf_tensor(name, shape, dt) as t:
                return t

        sems = {}

        def S(name):
            if name not in sems:
                sems[name] = ctx.enter_context(nc.semaphore(name))
            return sems[name]

        raw = sb("w_raw", [P, RING, 2, GC])
        w_hi = sb("w_hi", [P, RING, 2, GC], F32R)
        w_lo = sb("w_lo", [P, RING, 2, GC], F32R)
        H = sb("residual", [P, KT, L])
        XS = freed("x_split", [P, KT, 2, L], F32R)
        XF = sb("region_x", [P, 2 * KT * L])
        NB = FT * 2 * L
        HID = freed("hidden_split", [P, FT, 2, L], F32R)
        CS = freed("ctx_split", [P, KT, 2, L], F32R)
        with nc.sbuf_tensor("pad_o", [P, 8192], F32):
            OS = freed("attn_split", [P, 24, 2, L], F32R)
        with nc.sbuf_tensor("pad_p", [P, 4096], F32):
            PSP = freed("p_split", [P, 2, 2, L], F32R)
        BF = sb("region_b", [P, NB])
        EV = sb("evac", [P, 2, NF, L])
        C = sb("constants", [P, NCONST])
        PRM = sb("params", [P, 5, P])
        MADA = sb("ada", [P, 6 * KT, 2])
        COND = sb("conditions", [P, KT, 2])
        GE = sb("gain_eff", [P, 3, KT])
        SM = sb("small", [P, 608])
        ST = sb("stat", [P, 512])
        PS = ctx.enter_context(nc.psum_tensor("psum", [P, 8, 512], F32))

        def const(name):
            at, n = CONST[name]
            return C[:, at:at + n]

        def prm(name, i=0, n=1):
            at = PARAM_ROWS[name] + i
            return PRM[:, at // P, at % P:at % P + n]

        def prm_dyn(name, i):
            at = PARAM_ROWS[name]
            return PRM[:, at // P, bass.ds(i + at % P, 1)]

        def bf(at, *shape):
            n = int(np.prod(shape))
            v = BF[:, at:at + n]
            if len(shape) == 1:
                return v
            names = "abcd"[:len(shape)]
            return v.rearrange(f"p ({' '.join(names)}) -> p {' '.join(names)}",
                               **{k: s for k, s in zip(names[1:], shape[1:])})

        def xf(at, *shape):
            n = int(np.prod(shape))
            v = XF[:, at:at + n]
            if len(shape) == 1:
                return v
            names = "abcd"[:len(shape)]
            return v.rearrange(f"p ({' '.join(names)}) -> p {' '.join(names)}",
                               **{k: s for k, s in zip(names[1:], shape[1:])})

        def r(ap):
            return ap.bitcast(F32)

        SQ = bf(14336, KT, L)
        Z = bf(18432, KT, L)
        XNAT = bf(0, 2, D)
        PROW = bf(4096, 5, P)
        WDT = bf(4736, KT, 32)
        DROW = bf(5248, P)
        DPAIR = bf(5376, 2)
        XBC = bf(0, 12, L)
        SZ = bf(3072, 8, L)
        UPW = L + 16
        UP = bf(5120, 8, UPW)
        MIXED = bf(7296, 8, L)
        PW = bf(9344, 4, 2, L)
        XDT = bf(11392, 2, 2, SSD_H, 64)
        CBM = bf(15488, 2, 2, 3, P)
        Y = bf(17024, KT, L)
        YSQ = bf(5120, 8, L)
        SEL = xf(0, 32, P)
        MR = xf(4096, 4, 3 * P)
        ER = xf(5632, 4, 3 * P)
        SA, SB = bf(11392, 8, UPW), bf(13568, 8, UPW)
        INV = bf(21120, 4, L)
        OUT1 = bf(0, KT, L)
        OSQ1 = bf(4096, KT, L)
        OUT2 = xf(0, KT, L)
        OSQ2 = xf(4096, KT, L)
        PLE = bf(0, KT, L)
        OUT3 = bf(5120, KT, L)
        OSQ3 = bf(9216, KT, L)
        PNAT = bf(5120, 2, L)
        PTR = bf(5632, 2, L)
        CNAT = bf(0, 2, D)
        CTX = bf(8192, KT, L)
        KV = bf(8192, 24, 2 * L)
        Q = bf(0, 24, L)
        PR = bf(6144, 4, 512)
        PTT = bf(20480, 2, 4, L)
        MG = bf(0, KT, L)
        ONAT = bf(0, 2, D)
        evA, evB = EV[:, 0], EV[:, 1]

        def acc(s):
            return PS[:, 2 * s:2 * s + 2, :].rearrange("p b (h n) -> p (b h) n", h=2)

        def accf(s, f):
            return PS[:, 2 * s + f // 2, (f % 2) * L:(f % 2) * L + L]

        ADA = PS[:, 5, 0:2 * NF].rearrange("p (f v) -> p f v", v=2)
        ADA_SUM = ST[:, 0:GC], SM[:, 96:96 + GC]

        w_landed = [S(f"w_landed{i}") for i in range(RING)]
        w_rounded, w_split, w_used = S("w_rounded"), S("w_split"), S("w_used")
        evacuated, ada_evacuated = S("evacuated"), S("ada_evacuated")
        ada_half, ada_copied, ada_reduced = S("ada_half"), S("ada_copied"), S("ada_reduced")
        norm_sq, norm_stat, norm_std, norm_z, norm_hi, norm_ready, norm_added = (
            S("norm_" + kind) for kind in ("sq", "stat", "std", "z", "hi", "ready", "added"))
        norms = ("mix_pre", "mix_post", "ffn_pre", "ffn_post", "ple_pre", "ple_post", "norm1", "norm_c", "norm2")

        def so_far(tag, kind, n):
            before = norms[:norms.index(tag)]
            posts = sum(t.endswith("_post") for t in before)
            per, times = {"sq": (4, len(before)), "stat": (1, len(before)), "std": (1, len(before)),
                          "z": (16, len(before) - posts), "hi": (4, len(before) - posts),
                          "ready": (4, len(before) - posts), "added": (4, posts)}[kind]
            return per * times + n

        prev_ada = {}
        for name, ph in PHASES.items():
            at = [k for k, x in enumerate(ph.body) if x[0] == "a"]
            prev_ada[name] = dict(zip(at[1:], at[:-1]))

        def source(name, b, x):
            kind, j, u = x
            k = slice(2 * u, 2 * u + 2)
            if kind == "a":
                return W_ADA[:, k, bass.ds(b.ada_col(j) * GC, GC)]
            if name == "in":
                col = [1024, 1536, 2048, 2592, 3104, 0, 512][j]
                return W_IN[:, k, col:col + GC]
            if name == "up":
                return W_UP[:, k, bass.ds(b.n(GC, j * DFF), GC)]
            if name == "branch":
                w, c0 = [(W_IN2, 6144), (W_BR_A, 0), (W_IN2, 8192), (W_BR_B, 0)][j]
                return w[:, k, bass.ds(b.n(GC, c0), GC)]
            if name == "up2":
                return (W_G2, W_U2)[j][:, k, bass.ds(b.n(GC, 0), GC)]
            w, c0 = {"out": (W_OUT, 0), "down": (W_DOWN, 0), "ple": (W_PLE, 0), "gate": (W_GATE, 0),
                     "kv": (W_IN2, 0), "q": (W_IN2, 3072), "out2": (W_OUT2, 0),
                     "down2": (W_D2, 0)}[name]
            return w[:, k, bass.ds(b.local(j) * GC + c0, GC)]

        def stream_pe(pe, name, rhs, of=None, first=None, late=None):
            for b in bodies(pe, name):
                for n, (j, u) in enumerate(b.ph.units):
                    slot = b.slot(n)
                    if u == 0:
                        pe.wait_ge(evacuated, b.group(j) + 1)
                        if first is not None:
                            first(j)
                    if of is not None and j == 0 and u % 2 == 0:
                        pe.wait_ge(norm_ready, so_far(of, "ready", u // 2 + 1))
                    pe.wait_ge(w_split, b.load(b.ph.at[n]) + RING + 1)
                    for t in range(2):
                        kt = 2 * u + t
                        last = kt == 2 * b.ph.Us[j] - 1
                        for f in range(NF):
                            hi = w_hi[:, slot, t, f * P:f * P + P]
                            lo = w_lo[:, slot, t, f * P:f * P + P]
                            to = accf(b.set(j), f)
                            x_hi, x_lo = rhs(j, kt)
                            nc.tensor.matmul(to, hi, x_hi, start=kt == 0 and f % 2 == 0, stop=False,
                                             skip_group_check=True)
                            nc.tensor.matmul(to, hi, x_lo, start=False, stop=False, skip_group_check=True)
                            mm = nc.tensor.matmul(to, lo, x_hi, start=False, stop=last, skip_group_check=True)
                    mm.then_inc(w_used, 1)
                    for i, at in enumerate(b.ph.done):
                        if n == at + 2:
                            pe.wait_ge(ada_copied, b.ada(i) + 1)
                            pe.wait_ge(ada_evacuated, b.ada(i) + 1)
                            for v in range(ada_conditions(name, i)):
                                for f in range(NF):
                                    mm = nc.tensor.matmul(ADA[:, f, v:v + 1], ADA_SUM[v][:, f * P:f * P + P],
                                                          const("ones")[:, 0:1], start=f == 0 and v == 0,
                                                          stop=True, skip_group_check=True)
                            mm.then_inc(ada_reduced, 1)
                    if late is not None:
                        late(b, j, u)

        def kv_stream(pe, late):
            for b in bodies(pe, "kv"):
                for n, (j, u) in enumerate(b.ph.units):
                    slot = b.slot(n)
                    if u % 2 == 0 and j == 0:
                        pe.wait_ge(norm_ready, so_far("norm1", "ready", u // 2 + 1))
                        pe.wait_ge(norm_ready, so_far("norm_c", "ready", u // 2 + 1))
                    if u == 0:
                        pe.wait_ge(evacuated, b.group(j) + 2)
                    pe.wait_ge(w_split, b.load(b.ph.at[n]) + RING + 1)
                    for t in range(2):
                        kt = 2 * u + t
                        for f in range(NF):
                            if kt == 0 and f == 2:
                                pe.wait_ge(S("kv_half"), b.local(j) + 1)
                            hi = w_hi[:, slot, t, f * P:f * P + P]
                            lo = w_lo[:, slot, t, f * P:f * P + P]
                            for i, x in enumerate((XS, CS)):
                                to = PS[:, f, i * L:i * L + L]
                                nc.tensor.matmul(to, hi, x[:, kt, 0], start=kt == 0 and i == 0, stop=False,
                                                 skip_group_check=True)
                                nc.tensor.matmul(to, hi, x[:, kt, 1], start=False, stop=False,
                                                 skip_group_check=True)
                                mm = nc.tensor.matmul(to, lo, x[:, kt, 0], start=False, stop=kt == KT - 1,
                                                      skip_group_check=True)
                    mm.then_inc(w_used, 1)
                    late(b, j, u)

        def stream_act(act, name, evac, late=None, evac_first=False):
            for b in bodies(act, name):
                for n, (j, u) in enumerate(b.ph.units):
                    if evac_first and u == b.ph.Us[j] - 1:
                        evac(b, j, n)
                    if not b.is_last(n):
                        k = b.ahead(n)
                        act.wait_ge(w_landed[b.raw_slot(k)], b.landed(k))
                        act.wait_ge(w_used, b.unit(n) + RING + 1)
                        nc.scalar.activation(w_hi[:, b.slot(n)], raw[:, b.raw_slot(k)],
                                             ACT.Copy).then_inc(w_rounded, 1)
                    if not evac_first and u == b.ph.Us[j] - 1:
                        evac(b, j, n)
                    if late is not None:
                        late(b, j, u)

        def ada_conditions(name, i):
            cols = PHASES[name].ada_cols
            return 2 if cols[i if PHASES[name].times == 1 else 0] < 2 * D // GC else 1

        def ada_unit(dve, b, name, k, i, u):
            slot, nv = b.raw_slot(k), ada_conditions(name, i)
            dve.wait_ge(w_landed[slot], b.landed(k))
            for t in range(2):
                if u == 0 and t == 0:
                    if b.i is not None or b.ada(i) > 0:
                        dve.wait_ge(ada_copied, b.ada(i))
                elif t == 0:
                    dve.wait_ge(w_split, b.load(prev_ada[name][k]) + RING + 1)
                else:
                    dve.wait_ge(ada_half, b.ada(i) * 8 + (u + 1))
                for v in range(nv):
                    acc_v, c = PS[:, 6 + v, :], COND[:, 2 * u + t, v:v + 1]
                    if u == 0 and t == 0:
                        ins = nc.vector.tensor_scalar(acc_v, raw[:, slot, t], c, None, ALU.mult)
                    else:
                        ins = nc.vector.scalar_tensor_tensor(acc_v, raw[:, slot, t], c, acc_v, ALU.mult, ALU.add)
                ins.then_inc(ada_half if t == 0 else w_split, 1)
            if u == 7:
                dve.wait_ge(w_split, b.load(k) + RING + 1)
                for v in range(nv):
                    ins = nc.vector.tensor_copy(ADA_SUM[v], PS[:, 6 + v, :])
                ins.then_inc(ada_copied, 1)

        def stream_dve(dve, name, evac, late=None, evac_first=False):
            for b in bodies(dve, name):
                for n, (j, u) in enumerate(b.ph.units):
                    if evac_first and u == b.ph.Us[j] - 1:
                        evac(b, j, n)
                    if not b.is_last(n):
                        slot, k = b.slot(n), b.ahead(n)
                        dve.wait_ge(w_rounded, b.unit(n) + RING + 1)
                        nc.vector.tensor_tensor(w_lo[:, slot], raw[:, b.raw_slot(k)], r(w_hi[:, slot]),
                                                ALU.subtract).then_inc(w_split, 1)
                    if n + RING < len(b.ph.units):
                        for k, i, au in b.ph.after[n + RING]:
                            ada_unit(dve, b, name, k, i, au)
                    if not evac_first and u == b.ph.Us[j] - 1:
                        evac(b, j, n)
                    for i, at in enumerate(b.ph.done):
                        if n == at + 3:
                            nv = ada_conditions(name, i)
                            dve.wait_ge(ada_reduced, b.ada(i) + 1)
                            nc.vector.tensor_copy(MADA[:, bass.ds(b.ada_col(i) * NF, NF), 0:nv],
                                                  ADA[:, :, 0:nv]).then_inc(ada_evacuated, 1)
                    if late is not None:
                        late(b, j, u)

        def first_tap(act, x, out, weight, bias):
            for f in range(NF):
                nc.scalar.activation(out(f), x(f), ACT.Identity, bias=bias(f), scale=weight(f)
                                     ).then_inc(S("first_tap"), 1)

        def group_used(eng, b, k):
            eng.wait_ge(w_used, b.unit(k) + RING + 1)

        def all_evacuated(eng, name):
            ph = PHASES[name]
            eng.wait_ge(evacuated, 2 + ph.group0 + len(ph.Us) * ph.times)

        def squares_act(act, tag, src, added=None):
            for q in range(4):
                if added is not None:
                    act.wait_ge(norm_added, so_far(added, "added", q + 1))
                nc.scalar.activation(SQ[:, 4 * q:4 * q + 4], src[:, 4 * q:4 * q + 4],
                                     ACT.Square).then_inc(norm_sq, 1)

        def stat_pe(pe, tag, sq, per):
            for t in range(KT):
                pe.wait_ge(norm_sq, so_far(tag, "sq", t // (KT // per) + 1))
                mm = nc.tensor.matmul(PS[:, 4, 0:L], const("ones"), sq[:, t], start=t == 0, stop=t == KT - 1,
                                      skip_group_check=True)
            mm.then_inc(norm_stat, 1)

        def std_act(act, tag):
            act.wait_ge(norm_stat, so_far(tag, "stat", 1))
            nc.scalar.activation(ST[:, 0:L], PS[:, 4, 0:L], ACT.Sqrt, bias=SM[:, 0:1],
                                 scale=1.0 / D).then_inc(norm_std, 1)

        def rstd_dve(dve, ch, tag):
            dve.wait_ge(norm_std, so_far(tag, "std", 1))
            ch.mark(nc.vector.reciprocal(ST[:, 0:L], ST[:, 0:L]))
            ch.wait()

        def pre_act(act, tag, dst, shift=None):
            std_act(act, tag)
            for q in range(4):
                act.wait_ge(norm_z, so_far(tag, "z", 4 * q + 4))
                if shift is None:
                    nc.scalar.activation(dst[:, 4 * q:4 * q + 4, 0], Z[:, 4 * q:4 * q + 4],
                                         ACT.Copy).then_inc(norm_hi, 1)
                else:
                    for t in range(4 * q, 4 * q + 4):
                        ins = nc.scalar.activation(dst[:, t, 0], Z[:, t], ACT.Identity, bias=shift(t))
                    ins.then_inc(norm_hi, 1)

        def pre_dve(dve, ch, tag, src, gain, dst, shift=None):
            rstd_dve(dve, ch, tag)

            def scaled(q):
                for t in range(4 * q, 4 * q + 4):
                    nc.vector.scalar_tensor_tensor(Z[:, t], src[:, t], gain(t), ST[:, 0:L], ALU.mult,
                                                   ALU.mult).then_inc(norm_z, 1)

            def rest(q):
                dve.wait_ge(norm_hi, so_far(tag, "hi", q + 1))
                dve.wait_ge(norm_z, so_far(tag, "z", 4 * q + 4))
                if shift is None:
                    ins = nc.vector.tensor_tensor(dst[:, 4 * q:4 * q + 4, 1], Z[:, 4 * q:4 * q + 4],
                                                  r(dst[:, 4 * q:4 * q + 4, 0]), ALU.subtract)
                else:
                    for t in range(4 * q, 4 * q + 4):
                        ins = nc.vector.scalar_tensor_tensor(dst[:, t, 1], Z[:, t], shift(t), r(dst[:, t, 0]),
                                                             ALU.add, ALU.subtract)
                ins.then_inc(norm_ready, 1)

            scaled(0)
            for q in range(4):
                if q < 3:
                    scaled(q + 1)
                rest(q)

        def post_dve(dve, ch, tag, o, gain):
            rstd_dve(dve, ch, tag)

            def scaled(q):
                for t in range(4 * q, 4 * q + 4):
                    ch.mark(nc.vector.scalar_tensor_tensor(Z[:, t], o[:, t], prm(gain, t), ST[:, 0:L], ALU.mult,
                                                           ALU.mult))

            scaled(0)
            for q in range(4):
                if q < 3:
                    scaled(q + 1)
                ch.wait(ch.n - (4 if q < 3 else 0))
                nc.vector.tensor_tensor(H[:, 4 * q:4 * q + 4], H[:, 4 * q:4 * q + 4], Z[:, 4 * q:4 * q + 4],
                                        ALU.add).then_inc(norm_added, 1)

        def split_rhs(xs, at=0):
            return lambda j, k: (xs[:, at + k, 0], xs[:, at + k, 1])

        def copy_evac(o, tag):
            def dve_part(dve):
                def evac(b, j, k):
                    group_used(dve, b, k)
                    nc.vector.tensor_copy(o[:, bass.ds(b.local(j) * NF, NF)], acc(b.set(j))).then_inc(evacuated, 1)
                return evac

            def act_part(act, sq):
                def evac(b, j, k):
                    act.wait_ge(evacuated, b.group(j) + 3)
                    nc.scalar.activation(sq[:, bass.ds(b.local(j) * NF, NF)], o[:, bass.ds(b.local(j) * NF, NF)],
                                         ACT.Square).then_inc(norm_sq, 1)
                return evac
            return dve_part, act_part

        out_dve, out_act = copy_evac(OUT1, "mix_post")
        down_dve, down_act = copy_evac(OUT2, "ffn_post")

        IN_TAPS = 3 * NF

        block = ctx.enter_context(nc.Block())

        @block.sync
        def _(sp):
            sp.dma_start(C[:, :], consts_d).then_inc(S("consts_landed"), 16)
            for t in range(2):
                sp.dma_start(XNAT[:, t, :], A["x"][0, t * P:(t + 1) * P, :]).then_inc(S("x_landed"), 16)
            rows = {
                "mix_pre": "mix_norm_pre", "mix_post": "mix_norm_post", "ffn_pre": "ffn_norm_pre",
                "ffn_post": "ffn_norm_post", "ple_pre": "ple_norm_pre", "ple_post": "ple_norm_post",
                "norm1": "norm1_g_2", "norm2": "norm2_g_2", "ssd_conv_w": "ssd_conv_w",
                "ssd_conv_b": "ssd_conv_b", "ssd_norm": "ssd_norm", "pool_scale": "pool_scale",
                "b_ada": "b_ada_2", "q_norm_a": "q_norm_a_2", "k_norm_a": "k_norm_a_2",
                "subln": "subln_g_2", "ffn_b": "ffn_conv_b", "c": "c_2",
            }
            n = 0

            def param(at, src):
                nonlocal n
                k = src.shape[0]
                sp.dma_start(PROW[at % P:at % P + k, at // P, :], src).then_inc(S("params_landed"), 16)
                n += 1

            for name, key in rows.items():
                a = A[key][0]
                if len(a.shape) == 2:
                    a = a.rearrange("k (r c) -> (k r) c", c=P)
                else:
                    a = a.rearrange("(r c) -> r c", c=P)
                param(PARAM_ROWS[name], a)
            param(PARAM_ROWS["c_ctx"], A["c_ctx_2"].rearrange("(r c) -> r c", c=P))
            for i, name in enumerate(("ffn_w0", "ffn_w1", "ffn_w2")):
                param(PARAM_ROWS[name], A["ffn_conv_w"][0, i].rearrange("(r c) -> r c", c=P))
            for name, key in (("q_norm_b", "q_norm_b_2"), ("k_norm_b", "k_norm_b_2")):
                at = PARAM_ROWS[name]
                for half in range(2):
                    sp.dma_start(PROW[at % P:at % P + 1, at // P, 64 * half:64 * half + 64],
                                 A[key][0:1, :]).then_inc(S("params_landed"), 16)
                    n += 1
            sp.dma_start(DPAIR[0:8], A["ssd_d"][0].rearrange("(t e) -> t e", e=2)).then_inc(S("params_landed"), 16)
            sp.dma_start(SM[:, 32:64], A["ssd_dt_bias"][0].rearrange("a b -> (a b)").partition_broadcast(P)
                         ).then_inc(S("params_landed"), 16)
            sp.dma_start(SM[:, 64:96], A["ssd_a_log"][0].rearrange("a b -> (a b)").partition_broadcast(P)
                         ).then_inc(S("params_landed"), 16)
            for i, key in enumerate(("lam_q1_2", "lam_k1_2", "lam_q2_2", "lam_k2_2")):
                sp.dma_start(EV[:, 0, 0, 64 * i:64 * i + 64], A[key][0].partition_broadcast(P)
                             ).then_inc(S("params_landed"), 16)
            assert n + 7 == N_PARAM_LOADS
            sp.dma_start(WDT, W_IN[:, :, 2560:2592]).then_inc(S("wdt_landed"), 16)
            sp.dma_start(PW, A["pool_w"][0].rearrange("g (t p) n -> p g t n", p=P)).then_inc(S("poolw_landed"), 16)

            def stream(name):
                for b in bodies(sp, name, straight=name == "branch"):
                    for k, x in enumerate(b.ph.body):
                        slot = b.raw_slot(k)
                        sp.wait_ge(w_split, b.load(k) + 1)
                        sp.dma_start(raw[:, slot], source(name, b, x)).then_inc(w_landed[slot], 16)

            stream("in")
            stream("out")
            stream("up")
            stream("down")
            stream("ple")
            stream("gate")
            for name in ("kv", "q", "branch", "out2", "up2", "down2"):
                stream(name)
            for t, by in enumerate(("out_copied_dve", "out_copied_act")):
                sp.wait_ge(S(by), 1)
                sp.dma_start(out[0, t * P:(t + 1) * P, :], ONAT[:, t, :]).then_inc(S("stored"), 16)
            sp.wait_ge(S("stored"), 32)

        @block.gpsimd
        def _(pool):
            pool.wait_ge(norm_ready, so_far("mix_pre", "ready", 4))
            pool.wait_ge(S("dt_projected"), 1)
            for g in range(4):
                pool.dma_start(INV[:, g, :], inv_d[g].partition_broadcast(P)).then_inc(S("inv_landed"), 16)
            pool.wait_ge(w_used, RING + PHASES["out"].unit0)
            pool.dma_start(SEL[0:32], sel_d.rearrange("r (h p) -> r h p", h=32)).then_inc(S("sel_landed"), 16)
            pool.wait_ge(w_used, RING + PHASES["ple"].unit0)
            for t in range(2):
                pool.dma_start(PNAT[:, t, :], A["p"][0, 0, t * P:(t + 1) * P, :]).then_inc(S("p_landed"), 16)
            pool.wait_ge(norm_added, so_far("ple_post", "added", 4))
            for t in range(2):
                pool.dma_start(CNAT[:, t, :], A["ctx_2"][0, t * P:(t + 1) * P, :]).then_inc(S("ctx_landed"), 16)

        SSD_STEPS = [(t, e, d) for t in range(8) for e in range(2) for d in range(2)]

        ROUNDS = [("a", h, qb) for h in range(16) for qb in range(2)] + \
                 [("b", h, qb) for h in range(8) for qb in range(2)]
        JOBS, at = [], 0
        for rd in ROUNDS:
            JOBS.append(list(range(at, at + (1 if rd[0] == "a" else 2))))
            at += len(JOBS[-1])
        NJOBS = at

        HEADS = []
        for j in range(6):
            for f in range(NF):
                t, step = NF * j + f, 8 * (j + 1) + 2 * f
                if j in (1, 4, 5):
                    HEADS.append((KV[:, t], 2 * L, None, "v", step))
                else:
                    kind = "a" if j == 0 else "b"
                    HEADS.append((KV[:, t], 2 * L, "k_norm_" + kind, kind, step))
        for j in range(6):
            for f in range(NF):
                kind = "a" if j < 4 else "b"
                HEADS.append((Q[:, NF * j + f], L, "q_norm_" + kind, kind, 8 * (j + 7) + 2 * f))
        QK_BEFORE = [sum(x[3] != "v" for x in HEADS[:i]) for i in range(len(HEADS))]
        QK_ITEM = [i for i, x in enumerate(HEADS) if x[3] != "v"]
        QK_SQ = EV[:, 0].rearrange("p (a f) n -> p a (f n)", a=2)
        QK_ST = EV[:, 1].rearrange("p (a f) n -> p a (f n)", a=2)
        QK_T = PTT.rearrange("p a b n -> p (a b) n")
        STEPS = 8 * 12

        def heads_landed(eng, i):
            j = i // NF
            eng.wait_ge(evacuated, 3 + PHASES["kv"].group0 + j)
            if j < 6:
                eng.wait_ge(S("kv_half"), 2 + j)

        def beside(stages):
            def at_step(step):
                for after, work in stages:
                    for i, x in enumerate(HEADS):
                        if x[4] + after == step:
                            work(i)

            def late(b, j, u):
                at_step((b.ph.group0 - PHASES["kv"].group0 + b.rep * len(b.ph.Us) + j) * 8 + u)

            def tail():
                for step in range(STEPS, HEADS[-1][4] + 8):
                    at_step(step)
            return late, tail

        SUBSQ, SUBST = bf(6144, 8, L), bf(20480, 8, L)
        NEGMAX, SUMS, RSUM = SM[:, 96:160], SM[:, 160:224], SM[:, 224:288]

        @block.scalar
        def _(act):
            seen = Chain(act, S("act_chain"))
            for n in range(RING):
                act.wait_ge(w_landed[n], 16)
                nc.scalar.activation(w_hi[:, n], raw[:, n], ACT.Copy).then_inc(w_rounded, 1)
            act.wait_ge(S("params_turned"), 1)
            for v, name in enumerate(("c", "c_ctx")):
                ins = nc.scalar.activation(COND[:, :, v], prm(name, 0, KT), ACT.Silu)
            ins.then_inc(S("conditions_ready"), 1)
            act.wait_ge(S("lam_sums"), 1)
            nc.scalar.activation(SM[:, 1:3], SM[:, 1:3], ACT.Exp).then_inc(S("lam_exp"), 1)
            act.wait_ge(S("x_turned"), 1)
            nc.scalar.activation(H[:, 8:16], PS[:, 4:8, :].rearrange("p b (h n) -> p (b h) n", h=2),
                                 ACT.Copy).then_inc(S("h_loaded_act"), 1)
            act.wait_ge(S("h_loaded_act"), 1)
            act.wait_ge(S("h_loaded_dve"), 1)
            squares_act(act, "mix_pre", H)
            pre_act(act, "mix_pre", XS)

            def in_evac(b, j, k):
                if j < 3:
                    group_used(act, b, k)
                    first_tap(act, lambda f: accf(b.set(j), f), lambda f: XBC[:, 4 * j + f],
                              lambda f: prm("ssd_conv_w", 24 + 4 * j + f), lambda f: prm("ssd_conv_b", 4 * j + f))
                elif j < 5:
                    group_used(act, b, k)
                    act.wait_ge(S("u_padded"), 1)
                    t = slice(4 * (j - 3), 4 * (j - 3) + 4)
                    nc.scalar.activation(UP[:, t, 8:8 + L], acc(b.set(j)), ACT.Copy).then_inc(S("u_ready"), 1)
                else:
                    group_used(act, b, k)
                    t = slice(4 * (j - 5), 4 * (j - 5) + 4)
                    nc.scalar.activation(SZ[:, t], acc(b.set(j)), ACT.Silu).then_inc(S("z_ready"), 1)
                if j == 0:
                    act.wait_ge(S("dt_biased"), 1)
                    seen.mark(nc.scalar.activation(SM[:, 384:448], SM[:, 128:192], ACT.Abs))
                    seen.wait()
                    nc.scalar.activation(SM[:, 192:256], SM[:, 384:448], ACT.Exp, scale=-1.0)
                    nc.scalar.activation(SM[:, 64:96], SM[:, 64:96], ACT.Exp).then_inc(S("dt_exp"), 1)
                if j == 1:
                    act.wait_ge(S("dt_plus_one"), 1)
                    nc.scalar.activation(SM[:, 320:384], SM[:, 256:320], ACT.Ln).then_inc(S("dt_ln"), 1)

            def in_silu(b, j, u):
                if 1 <= j <= 3 and u == 0:
                    act.wait_ge(evacuated, b.group(j) + 2)
                    t = slice(4 * (j - 1), 4 * (j - 1) + 4)
                    nc.scalar.activation(XBC[:, t], XBC[:, t], ACT.Silu).then_inc(S("xbc_ready"), 1)

            stream_act(act, "in", in_evac, in_silu)

            act.wait_ge(S("acum_done"), 1)
            nc.scalar.activation(ST[0:32, :], PS[0:32, 6, :], ACT.Copy).then_inc(S("acum_rows"), 1)
            for n in range(len(SSD_STEPS)):
                act.wait_ge(S("exponent_ready"), n + 1)
                nc.scalar.activation(ER[:, n % 4], ER[:, n % 4], ACT.Exp).then_inc(S("decay_ready"), 1)
            for g in range(2):
                act.wait_ge(S("y_gated"), 4 * g + 4)
                nc.scalar.activation(YSQ[:, 4 * g:4 * g + 4], Y[:, 4 * g:4 * g + 4],
                                     ACT.Square).then_inc(S("y_sq"), 1)
            act.wait_ge(S("y_stat"), 1)
            nc.scalar.activation(ST[:, :], PS[:, 4, :], ACT.Sqrt, bias=SM[:, 0:1],
                                 scale=1.0 / 512).then_inc(S("y_std"), 1)
            for q in (2, 3, 0, 1):
                if q < 2:
                    act.wait_ge(S("y_normed"), 4 * q + 4)
                else:
                    act.wait_ge(S("pool_scaled"), q - 1)
                nc.scalar.activation(XS[:, 4 * q:4 * q + 4, 0], Y[:, 4 * q:4 * q + 4],
                                     ACT.Copy).then_inc(S("mix_hi"), 1)

            stream_act(act, "out", out_act(act, OSQ1))
            std_act(act, "mix_post")
            squares_act(act, "ffn_pre", H, added="mix_post")
            pre_act(act, "ffn_pre", XS)

            def up_evac(b, j, k):
                if j == 0:
                    group_used(act, b, k)
                    act.wait_ge(evacuated, b.group(j) + 2)
                    first_tap(act, lambda f: accf(b.set(0), f), lambda f: evA[:, f],
                              lambda f: prm_dyn("ffn_w1", b.n(NF, f)), lambda f: prm_dyn("ffn_b", b.n(NF, f)))
                else:
                    act.wait_ge(evacuated, b.group(j) + 3)
                    nc.scalar.activation(HID[:, bass.ds(b.n(NF, 0), NF), 0], evB, ACT.Copy
                                         ).then_inc(S("hidden_hi"), 1)

            def up_gelu(b, j, u):
                if (j, u) == (1, 0):
                    act.wait_ge(evacuated, b.group(0) + 3)
                    nc.scalar.activation(evA, evA, ACT.Gelu_apprx_tanh).then_inc(S("gate_gelu"), 1)

            stream_act(act, "up", up_evac, up_gelu)
            stream_act(act, "down", down_act(act, OSQ2))
            std_act(act, "ffn_post")
            act.wait_ge(S("p_turned"), 1)
            nc.scalar.activation(PTR.rearrange("p a n -> p (a n)"), PS[:, 5, :], ACT.Copy).then_inc(S("p_copied"), 1)
            act.wait_ge(S("p_copied"), 1)
            nc.scalar.activation(PSP[:, :, 0], PTR, ACT.Copy).then_inc(S("p_hi"), 1)
            squares_act(act, "ple_pre", H, added="ffn_post")
            pre_act(act, "ple_pre", XS)
            stream_act(act, "ple", lambda b, j, k: None)

            def gate_evac(b, j, k):
                group_used(act, b, k)
                act.wait_ge(evacuated, b.group(j) + 2)
                nc.scalar.activation(evA, acc(b.set(j)), ACT.Sigmoid).then_inc(S("gate_ready"), 1)
                act.wait_ge(evacuated, b.group(j) + 3)
                at = bass.ds(b.local(j) * NF, NF)
                nc.scalar.activation(OSQ3[:, at], OUT3[:, at], ACT.Square).then_inc(norm_sq, 1)

            stream_act(act, "gate", gate_evac)
            std_act(act, "ple_post")

            squares_act(act, "norm1", H, added="ple_post")
            pre_act(act, "norm1", XS, shift=lambda t: MADA[:, t, 0:1])
            act.wait_ge(S("ctx_turned"), 1)
            nc.scalar.activation(CTX[:, 8:16], PS[:, 4:8, :].rearrange("p b (h n) -> p (b h) n", h=2),
                                 ACT.Copy).then_inc(S("ctx_loaded_act"), 1)
            act.wait_ge(S("ctx_loaded_act"), 1)
            act.wait_ge(S("ctx_loaded_dve"), 1)
            squares_act(act, "norm_c", CTX)
            pre_act(act, "norm_c", CS, shift=lambda t: MADA[:, t, 1:2])

            def kv_evac(b, j, k):
                group_used(act, b, k)
                nc.scalar.activation(KV[:, bass.ds(b.local(j) * NF + 2, 2)], PS[:, 2:4, :],
                                     ACT.Copy).then_inc(S("kv_half"), 1)

            def qk_square(i):
                x, n, _, kind, _ = HEADS[i]
                if kind == "v":
                    return
                m = QK_BEFORE[i]
                heads_landed(act, i)
                if m >= 2:
                    act.wait_ge(S("heads_pe"), QK_ITEM[m - 2] + 1)
                nc.scalar.activation(QK_SQ[:, m % 2, 0:n], x, ACT.Square).then_inc(S("qk_sq"), 1)

            def head_out(i):
                x, n, _, kind, _ = HEADS[i]
                act.wait_ge(S("heads_pe"), i + 1)
                if kind == "v":
                    nc.scalar.activation(x, PS[:, 4 + i % 2, :], ACT.Copy).then_inc(S("heads_act"), 1)
                    return
                m = QK_BEFORE[i]
                if m >= 2:
                    act.wait_ge(S("qk_normed"), m - 1)
                nc.scalar.activation(QK_ST[:, m % 2, 0:n], PS[:, 4 + i % 2, 0:n], ACT.Sqrt, bias=SM[:, 0:1],
                                     scale=1.0 / (128 if kind == "a" else 64)).then_inc(S("heads_act"), 1)

            late, tail = beside([(3, head_out), (0, qk_square)])
            stream_act(act, "kv", kv_evac, late, evac_first=True)
            stream_act(act, "q", lambda b, j, k: None, late)
            tail()

            def exps(rd):
                for n in JOBS[rd]:
                    act.wait_ge(S("max_ready"), n + 1)
                    if rd >= 2:
                        act.wait_ge(S("p_turn"), rd - 1)
                    nc.scalar.activation(PR[:, n % 4], PS[:, 2 + n % 4, :], ACT.Exp, bias=NEGMAX[:, n:n + 1],
                                         accum_out=SUMS[:, n:n + 1]).then_inc(S("exp_ready"), 1)

            exps(0)
            for rd, (_, h, qb) in enumerate(ROUNDS):
                if rd + 1 < len(ROUNDS):
                    exps(rd + 1)
                act.wait_ge(S("p_turn"), rd + 1)
                if rd >= 4:
                    act.wait_ge(S("pv_done"), rd // 2 - 1)
                nc.scalar.activation(PTT[:, (rd // 2) % 2, :, qb * P:(qb + 1) * P],
                                     PS[:, 6 + rd % 2, :].rearrange("p (c q) -> p c q", c=4),
                                     ACT.Copy).then_inc(S("pt_ready"), 1)
            act.wait_ge(S("o_ready"), 24)
            for q in range(2):
                nc.scalar.activation(SUBSQ[:, 4 * q:4 * q + 4], Q[:, 16 + 4 * q:20 + 4 * q],
                                     ACT.Square).then_inc(S("sub_sq"), 1)
            act.wait_ge(S("sub_stat"), 1)
            nc.scalar.activation(SUBST, PS[:, 2:6, :].rearrange("p b (h n) -> p (b h) n", h=2), ACT.Sqrt,
                                 bias=SM[:, 0:1], scale=1.0 / P).then_inc(S("sub_std"), 1)
            for q in range(6):
                if q == 4:
                    act.wait_ge(S("o_normed"), 8)
                nc.scalar.activation(OS[:, 4 * q:4 * q + 4, 0], Q[:, 4 * q:4 * q + 4],
                                     ACT.Copy).then_inc(S("o_hi"), 1)

            def branch_evac(b, j, k):
                if j % 2 == 0:
                    group_used(act, b, k)
                    act.wait_ge(evacuated, b.group(j) + 2)
                    nc.scalar.activation(evA, acc(b.set(j)), ACT.Sigmoid).then_inc(S("branch_gate"), 1)

            stream_act(act, "branch", branch_evac)
            act.wait_ge(S("merged"), 4)
            for q in range(4):
                nc.scalar.activation(XS[:, 4 * q:4 * q + 4, 0], MG[:, 4 * q:4 * q + 4],
                                     ACT.Copy).then_inc(S("merged_hi"), 1)

            def out2_evac(b, j, k):
                act.wait_ge(evacuated, b.group(j) + 3)
                at = bass.ds(b.local(j) * NF, NF)
                nc.scalar.activation(SQ[:, at], H[:, at], ACT.Square).then_inc(norm_sq, 1)

            stream_act(act, "out2", out2_evac)
            pre_act(act, "norm2", XS, shift=lambda t: MADA[:, 3 * KT + t, 0:1])

            def up2_evac(b, j, k):
                if j == 0:
                    group_used(act, b, k)
                    act.wait_ge(evacuated, b.group(j) + 2)
                    nc.scalar.activation(evA, acc(b.set(j)), ACT.Silu).then_inc(S("gate2_silu"), 1)
                else:
                    act.wait_ge(evacuated, b.group(j) + 3)
                    nc.scalar.activation(HID[:, bass.ds(b.n(NF, 0), NF), 0], evB, ACT.Copy
                                         ).then_inc(S("hidden2_hi"), 1)

            stream_act(act, "up2", up2_evac)
            stream_act(act, "down2", lambda b, j, k: None)
            act.wait_ge(S("out_turned"), 2)
            nc.scalar.activation(ONAT[:, 1, :], PS[:, 4:8, :].rearrange("p b n -> p (b n)"),
                                 ACT.Copy).then_inc(S("out_copied_act"), 1)

        @block.vector
        def _(dve):
            ch = Chain(dve, S("dve_chain"))
            dve.sem_inc(w_split, RING)
            dve.sem_inc(evacuated, 2)
            dve.sem_inc(ada_evacuated, 1)
            dve.sem_inc(S("kv_half"), 1)
            nc.vector.memset(SM[:, 0:1], EPS).then_inc(S("eps_ready"), 1)
            for n in range(RING):
                dve.wait_ge(w_rounded, n + 1)
                nc.vector.tensor_tensor(w_lo[:, n], raw[:, n], r(w_hi[:, n]), ALU.subtract).then_inc(w_split, 1)
            dve.wait_ge(S("params_landed"), 16 * N_PARAM_LOADS)
            nc.vector.tensor_copy(DROW[0:8].rearrange("p (e c) -> p e c", e=2),
                                  DPAIR[0:8].rearrange("p (e o) -> p e o", o=1).to_broadcast([8, 2, 64])
                                  ).then_inc(S("d_rows"), 1)
            for i in range(2):
                ch.mark(nc.vector.tensor_tensor_reduce(
                    SM[:, 320:384], EV[:, 0, 0, 128 * i:128 * i + 64], EV[:, 0, 0, 128 * i + 64:128 * i + 128],
                    1.0, 0.0, ALU.mult, ALU.add, SM[:, 1 + i:2 + i]))
                ch.wait()
            dve.sem_inc(S("lam_sums"), 1)
            dve.wait_ge(S("params_pe"), 1)
            for i, n in enumerate(PARAM_USED):
                nc.vector.tensor_copy(PRM[:, i, 0:n], PS[:, i // 4, (i % 4) * P:(i % 4) * P + n])
            nc.vector.tensor_copy(PRM[:, 1, 88:96], PS[:, 1, P:P + 8]).then_inc(S("params_turned"), 1)
            dve.wait_ge(S("params_turned"), 1)
            for i, (name, g) in enumerate((("q_norm_a", P ** -0.5), ("q_norm_b", 64 ** -0.5),
                                           ("subln", 1 - LAM_INIT))):
                nc.vector.tensor_scalar(SM[:, 4 + i:5 + i], prm(name), g, None, ALU.mult)
            dve.wait_ge(S("x_turned"), 1)
            nc.vector.tensor_copy(H[:, 0:8], PS[:, 0:4, :].rearrange("p b (h n) -> p (b h) n", h=2)
                                  ).then_inc(S("h_loaded_dve"), 1)
            dve.wait_ge(S("lam_exp"), 1)
            ch.mark(nc.vector.tensor_tensor(SM[:, 3:4], SM[:, 2:3], SM[:, 1:2], ALU.subtract))
            ch.wait()
            ch.mark(nc.vector.tensor_scalar(SM[:, 3:4], SM[:, 3:4], -LAM_INIT, None, ALU.add))
            dve.wait_ge(S("h_loaded_act"), 1)
            dve.wait_ge(S("h_loaded_dve"), 1)
            pre_dve(dve, ch, "mix_pre", H, lambda t: prm("mix_pre", t), XS)

            dx = SM[:, 128:192]
            dtv = SM[:, 448:512]
            da = SM[:, 256:320]

            def c32(ap):
                return ap.rearrange("p (c h) -> p c h", c=2)

            def over_chunks(ap):
                return ap.rearrange("p (o h) -> p o h", o=1).to_broadcast([P, 2, 32])

            def conv(x, out, taps, weight, first):
                half = taps // 2
                others = [j for j in range(taps) if j != half]
                for j in others:
                    off = j - half
                    for f in range(NF):
                        if j == others[0]:
                            dve.wait_ge(S("first_tap"), first(f | 1))
                        else:
                            ch.wait(ch.n - NF + 1 if j != others[-1] else ch.n - NF + 1 + f)
                        a, z = max(0, -off), L - max(0, off)
                        ins = nc.vector.scalar_tensor_tensor(out(f)[:, a:z], x(f)[:, a + off:z + off],
                                                             weight(j, f), out(f)[:, a:z], ALU.mult, ALU.add)
                        if j != others[-1]:
                            ch.mark(ins)
                ins.then_inc(evacuated, 1)

            def in_evac(b, j, k):
                if j == 0:
                    dve.wait_ge(S("dt_projected"), 1)
                    nc.vector.tensor_tensor(c32(dx), c32(PS[:, 5, 0:64]), over_chunks(SM[:, 32:64]),
                                            ALU.add).then_inc(S("dt_biased"), 1)
                if j == 1:
                    dve.wait_ge(S("dt_exp"), 1)
                    nc.vector.tensor_scalar(SM[:, 256:320], SM[:, 192:256], 1.0, None,
                                            ALU.add).then_inc(S("dt_plus_one"), 1)
                if j == 2:
                    dve.wait_ge(S("dt_ln"), 1)
                    dve.wait_ge(S("dt_plus_one"), 1)
                    e, ln, um1, is0, den = SM[:, 192:256], SM[:, 320:384], SM[:, 384:448], ST[:, 0:64], ST[:, 64:128]
                    for ins in (lambda: nc.vector.tensor_scalar(um1, SM[:, 256:320], -1.0, None, ALU.add),
                                lambda: nc.vector.tensor_scalar(is0, um1, 0.0, None, ALU.is_equal),
                                lambda: nc.vector.tensor_tensor(den, um1, is0, ALU.add),
                                lambda: nc.vector.reciprocal(den, den),
                                lambda: nc.vector.tensor_tensor(ln, ln, e, ALU.mult),
                                lambda: nc.vector.tensor_tensor(ln, ln, den, ALU.mult),
                                lambda: nc.vector.tensor_tensor(is0, is0, e, ALU.mult),
                                lambda: nc.vector.tensor_tensor(ln, ln, is0, ALU.add),
                                lambda: nc.vector.scalar_tensor_tensor(dtv, dx, 0.0, ln, ALU.max, ALU.add)):
                        ch.mark(ins())
                        ch.wait()
                    nc.vector.scalar_tensor_tensor(c32(da), c32(dtv), -1.0, over_chunks(SM[:, 64:96]),
                                                   ALU.mult, ALU.mult).then_inc(S("da_ready"), 1)
                if j < 3:
                    conv(lambda f: accf(b.set(j), f), lambda f: XBC[:, 4 * j + f], 5,
                         lambda tap, f: prm("ssd_conv_w", 12 * tap + 4 * j + f), lambda f: 4 * j + f + 1)
                elif j < 5:
                    dve.wait_ge(S("u_ready"), j - 2)
                    dve.sem_inc(evacuated, 1)
                else:
                    dve.wait_ge(S("z_ready"), j - 4)
                    dve.sem_inc(evacuated, 1)
                if j == 2:
                    nc.vector.memset(UP[:, :, 0:8], 0.0)
                    nc.vector.memset(UP[:, :, 8 + L:UPW], 0.0).then_inc(S("u_padded"), 1)
                if j == 4:
                    dve.wait_ge(S("u_padded"), 1)

                    def window(dst, src, t0, reach, a, z):
                        ch.mark(nc.vector.tensor_tensor(dst[:, t0:8, a:z], src[:, t0:8, a - reach[0]:z - reach[0]],
                                                        src[:, t0:8, a + reach[1]:z + reach[1]], ALU.add))
                        ch.wait()
                    window(SA, UP, 0, (1, 0), 1, UPW)
                    window(SB, SA, 2, (1, 1), 2, UPW - 1)
                    nc.vector.tensor_copy(MIXED[:, 0:2], SA[:, 0:2, 8:8 + L])
                    window(SA, SB, 4, (2, 2), 4, UPW - 3)
                    nc.vector.tensor_copy(MIXED[:, 2:4], SB[:, 2:4, 8:8 + L])
                    window(SB, SA, 6, (4, 4), 8, UPW - 7)
                    nc.vector.tensor_copy(MIXED[:, 4:6], SA[:, 4:6, 8:8 + L])
                    ch.mark(nc.vector.tensor_copy(MIXED[:, 6:8], SB[:, 6:8, 8:8 + L]))
                    ch.wait()
                    dve.wait_ge(S("inv_landed"), 64)
                    for g in range(4):
                        m = MIXED[:, 2 * g:2 * g + 2]
                        ch.mark(nc.vector.tensor_tensor(m, m, INV[:, g:g + 1].to_broadcast([P, 2, L]), ALU.mult))
                    ch.wait()
                    nc.vector.tensor_tensor(MIXED, MIXED, UP[:, :, 8:8 + L], ALU.subtract
                                            ).then_inc(S("mixed_ready"), 1)

            stream_dve(dve, "in", in_evac)

            nac = SM[:, 320:384]
            off = SM[:, 384:416]
            dve.wait_ge(S("acum_done"), 1)
            ch.mark(nc.vector.tensor_scalar(nac, PS[:, 5, 64:128], -1.0, None, ALU.mult))
            ch.wait()
            nc.vector.tensor_tensor(off[:, 0:16], PS[:, 5, 128:144], c32(nac)[:, 0, 0:16], ALU.add)
            ch.mark(nc.vector.tensor_tensor(off[:, 16:32], PS[:, 5, 144:160], c32(nac)[:, 1, 16:32], ALU.add))
            dve.wait_ge(S("pool_product"), 1)
            for t in range(8):
                ins = nc.vector.tensor_scalar(Y[:, 8 + t], PS[:, t // 2, (t % 2) * L:(t % 2) * L + L],
                                              prm("pool_scale", t), None, ALU.mult)
                if t % 4 == 3:
                    ins.then_inc(S("pool_scaled"), 1)
            dve.wait_ge(S("xs_turned"), 1)
            for d in range(2):
                for c in range(2):
                    ins = nc.vector.tensor_tensor(
                        XDT[:, d, c],
                        PS[:, 2 * c:2 * c + 2, :].rearrange("p b (h n) -> p (b h) n", n=64),
                        c32(dtv)[:, c, 16 * d:16 * d + 16].rearrange("p (h o) -> p h o", o=1
                                                                     ).to_broadcast([P, 16, 64]), ALU.mult)
            ins.then_inc(S("xdt_ready"), 1)
            dve.wait_ge(S("cb_done"), 1)
            for g in range(2):
                cb = PS[:, 4 if g == 0 else 7, :].rearrange("p (c l) -> p c l", c=2)
                for d, mask in enumerate(("upto", "from")):
                    nc.vector.tensor_tensor(CBM[:, g, d, 0], cb[:, 0, 0:P], const(mask), ALU.mult)
                    nc.vector.tensor_copy(CBM[:, g, d, 1], cb[:, 0, P:L] if d == 0 else cb[:, 1, 0:P])
                    ins = nc.vector.tensor_tensor(CBM[:, g, d, 2], cb[:, 1, P:L], const(mask), ALU.mult)
            ins.then_inc(S("cbm_ready"), 1)
            dve.wait_ge(S("cbm_ready"), 1)
            ch.wait()

            def exponents(n):
                t, e, d = SSD_STEPS[n]
                h = 16 * d + 2 * t + e
                row = PS[:, 4 + n % 2, 0:L]
                dve.wait_ge(S("row_ready"), n + 1)
                for blk, (l0, col) in enumerate(((0, nac[:, h:h + 1]),
                                                 (P if d == 0 else 0, off[:, h:h + 1]),
                                                 (P, nac[:, 32 + h:33 + h]))):
                    ins = nc.vector.tensor_scalar(ER[:, n % 4, blk * P:blk * P + P], row[:, l0:l0 + P], col, 0.0,
                                                  ALU.add, ALU.min)
                ins.then_inc(S("exponent_ready"), 1)

            def gate_y(t):
                dve.wait_ge(S("y_product"), 4 * t + 4)
                ch.mark(nc.vector.scalar_tensor_tensor(Y[:, t], XBC[:, t], prm("ssd_d", t), PS[:, 6 + t % 2, 0:L],
                                                       ALU.mult, ALU.add))
                ch.wait()
                nc.vector.tensor_tensor(Y[:, t], Y[:, t], SZ[:, t], ALU.mult).then_inc(S("y_gated"), 1)

            exponents(0)
            exponents(1)
            for n, (t, e, d) in enumerate(SSD_STEPS):
                if n + 2 < len(SSD_STEPS):
                    exponents(n + 2)
                dve.wait_ge(S("decay_ready"), n + 1)
                if n >= 4:
                    dve.wait_ge(S("y_product"), n - 3)
                nc.vector.tensor_tensor(MR[:, n % 4], ER[:, n % 4], CBM[:, t // 4, d].rearrange("p b l -> p (b l)"),
                                        ALU.mult).then_inc(S("mix_matrix"), 1)
                if n % 4 == 1 and t > 0:
                    gate_y(t - 1)
            gate_y(7)
            dve.wait_ge(S("y_std"), 1)
            ch.mark(nc.vector.reciprocal(ST[:, :], ST[:, :]))
            ch.wait()
            dve.wait_ge(S("y_gated"), 8)
            for t in range(8):
                nc.vector.scalar_tensor_tensor(Y[:, t], Y[:, t], prm("ssd_norm", t),
                                               ST[:, (t // 4) * L:(t // 4) * L + L], ALU.mult, ALU.mult
                                               ).then_inc(S("y_normed"), 1)
            for i, q in enumerate((2, 3, 0, 1)):
                dve.wait_ge(S("mix_hi"), i + 1)
                nc.vector.tensor_tensor(XS[:, 4 * q:4 * q + 4, 1], Y[:, 4 * q:4 * q + 4],
                                        r(XS[:, 4 * q:4 * q + 4, 0]), ALU.subtract).then_inc(S("mix_split"), 1)

            dve.wait_ge(S("conditions_ready"), 1)
            stream_dve(dve, "out", out_dve(dve))
            all_evacuated(dve, "out")
            post_dve(dve, ch, "mix_post", OUT1, "mix_post")
            dve.wait_ge(norm_added, so_far("mix_post", "added", 4))
            pre_dve(dve, ch, "ffn_pre", H, lambda t: prm("ffn_pre", t), XS)

            def up_evac(b, j, k):
                if j == 0:
                    ch.start(b, 4)
                    w = ["ffn_w0", "ffn_w1", "ffn_w2"]
                    conv(lambda f: accf(b.set(j), f), lambda f: evA[:, f], 3,
                         lambda tap, f: prm_dyn(w[tap], b.n(NF, f)), lambda f: b.n(NF, IN_TAPS + f + 1))
                    ch.end(b)
                else:
                    group_used(dve, b, k)
                    dve.wait_ge(S("gate_gelu"), b.n(1, 1))
                    nc.vector.tensor_tensor(evB, acc(b.set(j)), evA, ALU.mult).then_inc(evacuated, 1)
                    dve.wait_ge(S("hidden_hi"), b.n(1, 1))
                    dve.wait_ge(evacuated, b.group(j) + 3)
                    at = bass.ds(b.n(NF, 0), NF)
                    nc.vector.tensor_tensor(HID[:, at, 1], evB, r(HID[:, at, 0]), ALU.subtract
                                            ).then_inc(S("hidden_split"), 1)

            stream_dve(dve, "up", up_evac)
            stream_dve(dve, "down", down_dve(dve))
            all_evacuated(dve, "down")
            post_dve(dve, ch, "ffn_post", OUT2, "ffn_post")
            dve.wait_ge(S("p_hi"), 1)
            nc.vector.tensor_tensor(PSP[:, :, 1], PTR, r(PSP[:, :, 0]), ALU.subtract).then_inc(S("p_split"), 1)
            dve.wait_ge(norm_added, so_far("ffn_post", "added", 4))
            pre_dve(dve, ch, "ple_pre", H, lambda t: prm("ple_pre", t), XS)

            def ple_evac(b, j, k):
                group_used(dve, b, k)
                nc.vector.tensor_copy(PLE[:, NF * j:NF * j + NF], acc(b.set(j))).then_inc(evacuated, 1)

            stream_dve(dve, "ple", ple_evac)

            def gate_evac(b, j, k):
                dve.wait_ge(S("gate_ready"), b.local(j) + 1)
                at = bass.ds(b.local(j) * NF, NF)
                nc.vector.tensor_tensor(OUT3[:, at], evA, PLE[:, at], ALU.mult).then_inc(evacuated, 1)

            all_evacuated(dve, "ple")
            stream_dve(dve, "gate", gate_evac)
            all_evacuated(dve, "gate")
            post_dve(dve, ch, "ple_post", OUT3, "ple_post")

            def ada_bias(t0, t1, v):
                ch.mark(nc.vector.tensor_tensor(MADA[:, t0:t1, v], MADA[:, t0:t1, v],
                                                prm("b_ada", t0, t1 - t0), ALU.add))

            def gain_eff(i, m, v, name):
                ch.mark(nc.vector.scalar_tensor_tensor(GE[:, i], MADA[:, m * KT:(m + 1) * KT, v], 1.0,
                                                       prm(name, 0, KT), ALU.add, ALU.mult))

            def ada_done(name):
                ph = PHASES[name]
                dve.wait_ge(ada_evacuated, 1 + ph.ada0 + ph.ada * ph.times)

            ada_done("gate")
            ada_bias(0, 2 * KT, 0)
            ada_bias(0, 2 * KT, 1)
            ch.wait()
            gain_eff(0, 1, 0, "norm1")
            gain_eff(1, 1, 1, "norm1")
            ch.wait()
            dve.sem_inc(S("mod1_ready"), 1)
            dve.wait_ge(norm_added, so_far("ple_post", "added", 4))
            pre_dve(dve, ch, "norm1", H, lambda t: GE[:, 0, t:t + 1], XS, shift=lambda t: MADA[:, t, 0:1])
            dve.wait_ge(S("ctx_turned"), 1)
            nc.vector.tensor_copy(CTX[:, 0:8], PS[:, 0:4, :].rearrange("p b (h n) -> p (b h) n", h=2)
                                  ).then_inc(S("ctx_loaded_dve"), 1)
            dve.wait_ge(S("ctx_loaded_act"), 1)
            dve.wait_ge(S("ctx_loaded_dve"), 1)
            pre_dve(dve, ch, "norm_c", CTX, lambda t: GE[:, 1, t:t + 1], CS, shift=lambda t: MADA[:, t, 1:2])

            def kv_evac(b, j, k):
                group_used(dve, b, k)
                nc.vector.tensor_copy(KV[:, bass.ds(b.local(j) * NF, 2)], PS[:, 0:2, :]
                                      ).then_inc(evacuated, 1)

            def q_evac(b, j, k):
                group_used(dve, b, k)
                nc.vector.tensor_copy(Q[:, bass.ds(b.local(j) * NF, NF)], acc(b.set(j))).then_inc(evacuated, 1)

            gains = {"k_norm_a": prm("k_norm_a"), "k_norm_b": prm("k_norm_b"), "q_norm_a": SM[:, 4:5],
                     "q_norm_b": SM[:, 5:6]}

            def qk_norm(i):
                x, n, g, kind, _ = HEADS[i]
                if kind == "v":
                    return
                root = QK_ST[:, QK_BEFORE[i] % 2, 0:n]
                dve.wait_ge(S("heads_act"), i + 1)
                ch.mark(nc.vector.reciprocal(root, root))
                ch.wait()
                nc.vector.scalar_tensor_tensor(x, x, gains[g], root, ALU.mult, ALU.mult).then_inc(S("qk_normed"), 1)

            def qk_rope(i):
                x, _, _, kind, _ = HEADS[i]
                if kind == "v":
                    return
                m = QK_BEFORE[i]
                t1, t2 = QK_T[:, 2 * (m % 2)], QK_T[:, 2 * (m % 2) + 1]
                dve.wait_ge(S("qk_normed"), m + 1)
                nc.vector.tensor_tensor(t1, x[:, 0:L], const("cos_" + kind), ALU.mult)
                dve.wait_ge(S("qk_turned"), m + 1)
                ch.mark(nc.vector.tensor_tensor(t2, PS[:, 6 + m % 2, 0:L], const("sin_" + kind), ALU.mult))
                ch.wait()
                nc.vector.tensor_tensor(x[:, 0:L], t1, t2, ALU.add).then_inc(S("qk_roped"), 1)

            late, tail = beside([(7, qk_rope), (4, qk_norm)])
            stream_dve(dve, "kv", kv_evac, late, evac_first=True)
            stream_dve(dve, "q", q_evac, late)
            tail()

            def maxima(rd):
                for n in JOBS[rd]:
                    dve.wait_ge(S("scores_ready"), n + 1)
                    nc.vector.tensor_reduce(NEGMAX[:, n:n + 1], PS[:, 2 + n % 4, :], AX.X, ALU.max,
                                            negate=True).then_inc(S("max_ready"), 1)

            def probabilities(rd):
                js = JOBS[rd]
                dve.wait_ge(S("exp_ready"), js[-1] + 1)
                ch.mark(nc.vector.reciprocal(RSUM[:, js[0]:js[-1] + 1], SUMS[:, js[0]:js[-1] + 1]))
                ch.wait()
                p0 = PR[:, js[0] % 4]
                ins = nc.vector.tensor_scalar(p0, p0, RSUM[:, js[0]:js[0] + 1], None, ALU.mult)
                if len(js) == 2:
                    ch.mark(ins)
                    n = js[1]
                    ch.mark(nc.vector.tensor_tensor(RSUM[:, n:n + 1], RSUM[:, n:n + 1], SM[:, 3:4], ALU.mult))
                    ch.wait()
                    ins = nc.vector.scalar_tensor_tensor(p0, PR[:, n % 4], RSUM[:, n:n + 1], p0, ALU.mult, ALU.add)
                ins.then_inc(S("p_ready"), 1)

            def output(hd):
                dve.wait_ge(S("pv_done"), hd + 1)
                nc.vector.tensor_copy(Q[:, hd], PS[:, hd % 2, 0:L]).then_inc(S("o_ready"), 1)

            maxima(0)
            for rd in range(len(ROUNDS)):
                if rd + 1 < len(ROUNDS):
                    maxima(rd + 1)
                probabilities(rd)
                if rd % 2 == 1 and rd >= 3:
                    output(rd // 2 - 1)
            output(23)
            dve.wait_ge(S("sub_std"), 1)
            ch.mark(nc.vector.reciprocal(SUBST, SUBST))
            ch.wait()
            dve.wait_ge(S("o_ready"), 24)
            for i in range(8):
                nc.vector.scalar_tensor_tensor(Q[:, 16 + i], Q[:, 16 + i], SM[:, 6:7], SUBST[:, i], ALU.mult,
                                               ALU.mult).then_inc(S("o_normed"), 1)
            for q in range(6):
                dve.wait_ge(S("o_hi"), q + 1)
                nc.vector.tensor_tensor(OS[:, 4 * q:4 * q + 4, 1], Q[:, 4 * q:4 * q + 4],
                                        r(OS[:, 4 * q:4 * q + 4, 0]), ALU.subtract).then_inc(S("o_split"), 1)

            def branch_evac(b, j, k):
                at = bass.ds(b.n(NF, 0), NF)
                if j % 2 == 0:
                    dve.wait_ge(S("branch_gate"), b.n(2, 1 + j // 2))
                    dve.sem_inc(evacuated, 1)
                elif j == 1:
                    group_used(dve, b, k)
                    nc.vector.tensor_tensor(MG[:, at], acc(b.set(j)), evA, ALU.mult).then_inc(evacuated, 1)
                else:
                    group_used(dve, b, k)
                    nc.vector.tensor_tensor(evB, acc(b.set(j)), evA, ALU.mult).then_inc(evacuated, 1)
                    dve.wait_ge(evacuated, b.group(j) + 3)
                    nc.vector.tensor_tensor(MG[:, at], MG[:, at], evB, ALU.add).then_inc(S("merged"), 1)

            stream_dve(dve, "branch", branch_evac)
            ada_done("branch")
            ada_bias(2 * KT, 6 * KT, 0)
            ch.wait()
            gain_eff(2, 4, 0, "norm2")
            ch.wait()
            dve.wait_ge(S("merged"), 4)
            for q in range(4):
                dve.wait_ge(S("merged_hi"), q + 1)
                nc.vector.tensor_tensor(XS[:, 4 * q:4 * q + 4, 1], MG[:, 4 * q:4 * q + 4],
                                        r(XS[:, 4 * q:4 * q + 4, 0]), ALU.subtract).then_inc(S("merged_split"), 1)

            def gated_residual(m):
                def evac(b, j, k):
                    group_used(dve, b, k)
                    for f in range(NF):
                        t = bass.ds(b.local(j) * NF + f, 1)
                        h = H[:, t].rearrange("p o n -> p (o n)")
                        ins = nc.vector.scalar_tensor_tensor(
                            h, accf(b.set(j), f), MADA[:, bass.ds(b.local(j) * NF + (m * KT + f), 1), 0], h,
                            ALU.mult, ALU.add)
                    ins.then_inc(evacuated, 1)
                return evac

            stream_dve(dve, "out2", gated_residual(2))
            all_evacuated(dve, "out2")
            pre_dve(dve, ch, "norm2", H, lambda t: GE[:, 2, t:t + 1], XS, shift=lambda t: MADA[:, 3 * KT + t, 0:1])

            def up2_evac(b, j, k):
                if j == 0:
                    dve.wait_ge(S("gate2_silu"), b.n(1, 1))
                    dve.sem_inc(evacuated, 1)
                else:
                    group_used(dve, b, k)
                    nc.vector.tensor_tensor(evB, acc(b.set(j)), evA, ALU.mult).then_inc(evacuated, 1)
                    dve.wait_ge(S("hidden2_hi"), b.n(1, 1))
                    dve.wait_ge(evacuated, b.group(j) + 3)
                    at = bass.ds(b.n(NF, 0), NF)
                    nc.vector.tensor_tensor(HID[:, at, 1], evB, r(HID[:, at, 0]), ALU.subtract
                                            ).then_inc(S("hidden2_split"), 1)

            stream_dve(dve, "up2", up2_evac)
            stream_dve(dve, "down2", gated_residual(5))
            dve.wait_ge(S("out_turned"), 1)
            nc.vector.tensor_copy(ONAT[:, 0, :], PS[:, 0:4, :].rearrange("p b n -> p (b n)")
                                  ).then_inc(S("out_copied_dve"), 1)

        @block.tensor
        def _(pe):
            pe.sem_inc(w_used, RING)
            ident = const("ident")
            pe.wait_ge(S("consts_landed"), 16)
            pe.wait_ge(S("params_landed"), 16 * N_PARAM_LOADS)
            for i, n in enumerate(PARAM_USED):
                nc.tensor.transpose(PS[:, i // 4, (i % 4) * P:(i % 4) * P + n], PROW[0:n, i, :], ident[0:n, 0:n])
            pe.wait_ge(S("d_rows"), 1)
            nc.tensor.transpose(PS[:, 1, P:P + 8], DROW[0:8], ident[0:8, 0:8]).then_inc(S("params_pe"), 1)

            def turn(src, done):
                for t in range(KT):
                    for c in range(2):
                        ins = nc.tensor.transpose(PS[:, t // 2, (t % 2) * L + c * P:(t % 2) * L + c * P + P],
                                                  src[:, c, t * P:t * P + P], ident)
                ins.then_inc(S(done), 1)

            pe.wait_ge(S("params_turned"), 1)
            pe.wait_ge(S("x_landed"), 32)
            turn(XNAT, "x_turned")
            pe.wait_ge(S("h_loaded_act"), 1)
            pe.wait_ge(S("h_loaded_dve"), 1)
            stat_pe(pe, "mix_pre", SQ, 4)
            pe.wait_ge(S("wdt_landed"), 16)
            pe.wait_ge(norm_z, so_far("mix_pre", "z", 16))
            for c in range(2):
                for t in range(KT):
                    mm = nc.tensor.matmul(PS[:, 5, 32 * c:32 * c + 32], Z[:, t, c * P:c * P + P], WDT[:, t],
                                          start=c == 0 and t == 0, stop=t == KT - 1, skip_group_check=True)
            mm.then_inc(S("dt_projected"), 1)
            stream_pe(pe, "in", split_rhs(XS), of="mix_pre")

            da = SM[:, 256:320].rearrange("p (c h) -> p c h", c=2)
            pe.wait_ge(S("da_ready"), 1)
            for c in range(2):
                for d, tri in enumerate(("upto", "from")):
                    nc.tensor.matmul(PS[:, 5, 64 + 32 * c + 16 * d:80 + 32 * c + 16 * d], const(tri),
                                     da[:, c, 16 * d:16 * d + 16], start=c == 0 and d == 0, stop=True,
                                     skip_group_check=True)
            for d in range(2):
                nc.tensor.matmul(PS[:, 5, 128 + 16 * d:144 + 16 * d], const("ones"), da[:, d, 16 * d:16 * d + 16],
                                 start=False, stop=True, skip_group_check=True)
            for d, tri in enumerate(("upto", "from")):
                for c in range(2):
                    mm = nc.tensor.matmul(PS[0:32, 6, d * L + c * P:d * L + c * P + P], da[:, c], const(tri),
                                          start=c == 0 and d == 0, stop=True, skip_group_check=True)
            mm.then_inc(S("acum_done"), 1)
            all_evacuated(pe, "in")
            pe.wait_ge(S("mixed_ready"), 1)
            pe.wait_ge(S("poolw_landed"), 16)
            for g in range(4):
                for f in range(2):
                    for t in range(2):
                        mm = nc.tensor.matmul(PS[:, g, f * L:f * L + L], PW[:, g, t, f * P:f * P + P],
                                              MIXED[:, 2 * g + t], start=f == 0 and t == 0, stop=t == 1,
                                              skip_group_check=True)
            mm.then_inc(S("pool_product"), 1)
            pe.wait_ge(S("xbc_ready"), 3)
            for g in range(2):
                for c in range(2):
                    mm = nc.tensor.matmul(PS[:, 4 if g == 0 else 7, c * L:c * L + L],
                                          XBC[:, 8 + g, c * P:c * P + P], XBC[:, 10 + g], start=c == 0, stop=True,
                                          skip_group_check=True)
            mm.then_inc(S("cb_done"), 1)
            pe.wait_ge(S("pool_scaled"), 2)
            for c in range(2):
                for t in range(8):
                    ins = nc.tensor.transpose(PS[:, 2 * c + t // 4, (t % 4) * P:(t % 4) * P + P],
                                              XBC[:, t, c * P:c * P + P], ident)
            ins.then_inc(S("xs_turned"), 1)
            pe.wait_ge(S("sel_landed"), 16)
            pe.wait_ge(S("acum_rows"), 1)
            pe.wait_ge(S("cbm_ready"), 1)
            pe.wait_ge(S("xdt_ready"), 1)

            def row(n):
                t, e, d = SSD_STEPS[n]
                if n >= 2:
                    pe.wait_ge(S("exponent_ready"), n - 1)
                nc.tensor.matmul(PS[:, 4 + n % 2, 0:L], SEL[0:32, 16 * d + 2 * t + e], ST[0:32, d * L:d * L + L],
                                 start=True, stop=True, skip_group_check=True).then_inc(S("row_ready"), 1)

            row(0)
            row(1)
            for n, (t, e, d) in enumerate(SSD_STEPS):
                if n + 2 < len(SSD_STEPS):
                    row(n + 2)
                if n % 4 == 0 and t >= 2:
                    pe.wait_ge(S("y_gated"), t - 1)
                pe.wait_ge(S("mix_matrix"), n + 1)
                to = PS[64 * e:64 * e + 64, 6 + t % 2, 0:L]
                m = MR[:, n % 4]
                h = 2 * t + e
                if d == 0:
                    nc.tensor.matmul(to, XDT[:, 0, 0, h], m[:, 0:L], start=True, stop=False,
                                     skip_group_check=True)
                    mm = nc.tensor.matmul(to[:, P:L], XDT[:, 0, 1, h], m[:, L:L + P], start=False, stop=False,
                                          skip_group_check=True)
                else:
                    nc.tensor.matmul(to[:, 0:P], XDT[:, 1, 0, h], m[:, 0:P], start=False, stop=False,
                                     skip_group_check=True)
                    mm = nc.tensor.matmul(to, XDT[:, 1, 1, h], m[:, P:L + P], start=False, stop=True,
                                          skip_group_check=True)
                mm.then_inc(S("y_product"), 1)
            for t in range(8):
                pe.wait_ge(S("y_sq"), t // 4 + 1)
                mm = nc.tensor.matmul(PS[:, 4, (t // 4) * L:(t // 4) * L + L], const("ones"), YSQ[:, t],
                                      start=t == 0, stop=t % 4 == 3, skip_group_check=True)
            mm.then_inc(S("y_stat"), 1)

            pe.wait_ge(S("mix_split"), 4)
            stream_pe(pe, "out", split_rhs(XS))
            stat_pe(pe, "mix_post", OSQ1, 4)
            stat_pe(pe, "ffn_pre", SQ, 4)
            stream_pe(pe, "up", split_rhs(XS), of="ffn_pre")
            pe.wait_ge(S("hidden_split"), PHASES["up"].times)
            stream_pe(pe, "down", split_rhs(HID))
            stat_pe(pe, "ffn_post", OSQ2, 4)
            pe.wait_ge(S("p_landed"), 32)
            for t in range(2):
                for c in range(2):
                    ins = nc.tensor.transpose(PS[:, 5, t * L + c * P:t * L + c * P + P], PNAT[:, c, t * P:t * P + P],
                                              ident)
            ins.then_inc(S("p_turned"), 1)
            stat_pe(pe, "ple_pre", SQ, 4)
            pe.wait_ge(S("p_split"), 1)
            stream_pe(pe, "ple", split_rhs(PSP))
            stream_pe(pe, "gate", split_rhs(XS), of="ple_pre")
            stat_pe(pe, "ple_post", OSQ3, 4)
            stat_pe(pe, "norm1", SQ, 4)
            pe.wait_ge(norm_std, so_far("norm1", "std", 1))
            all_evacuated(pe, "gate")
            pe.wait_ge(S("ctx_landed"), 32)
            turn(CNAT, "ctx_turned")
            pe.wait_ge(S("ctx_loaded_act"), 1)
            pe.wait_ge(S("ctx_loaded_dve"), 1)
            stat_pe(pe, "norm_c", SQ, 4)

            def head_stat(i):
                x, n, _, kind, _ = HEADS[i]
                if i >= 2:
                    pe.wait_ge(S("heads_act"), i - 1)
                if kind == "v":
                    heads_landed(pe, i)
                    for c in range(4):
                        ins = nc.tensor.transpose(PS[:, 4 + i % 2, c * P:c * P + P], x[:, c * P:c * P + P], ident)
                    ins.then_inc(S("heads_pe"), 1)
                    return
                m = QK_BEFORE[i]
                pe.wait_ge(S("qk_sq"), m + 1)
                nc.tensor.matmul(PS[:, 4 + i % 2, 0:n], const("ones" if kind == "a" else "half"),
                                 QK_SQ[:, m % 2, 0:n], start=True, stop=True,
                                 skip_group_check=True).then_inc(S("heads_pe"), 1)

            def head_turn(i):
                x, _, _, kind, _ = HEADS[i]
                if kind == "v":
                    return
                m = QK_BEFORE[i]
                pe.wait_ge(S("qk_normed"), m + 1)
                if m >= 2:
                    pe.wait_ge(S("qk_roped"), m - 1)
                nc.tensor.matmul(PS[:, 6 + m % 2, 0:L], const("rot_" + kind), x[:, 0:L], start=True,
                                 stop=True, skip_group_check=True).then_inc(S("qk_turned"), 1)

            late, tail = beside([(2, head_stat), (6, head_turn)])
            kv_stream(pe, late)
            all_evacuated(pe, "kv")
            pe.wait_ge(S("kv_half"), 7)
            stream_pe(pe, "q", split_rhs(XS), late=late)
            tail()
            all_evacuated(pe, "q")
            pe.wait_ge(S("qk_roped"), len(QK_ITEM))
            pe.wait_ge(S("heads_act"), len(HEADS))

            def scores(rd):
                br, h, qb = ROUNDS[rd]
                for i, n in enumerate(JOBS[rd]):
                    if n >= 4:
                        pe.wait_ge(S("exp_ready"), n - 3)
                    if br == "a":
                        q, k = Q[:, h, qb * P:qb * P + P], KV[:, h // 4]
                    else:
                        rows = slice(64 * i, 64 * i + 64)
                        q, k = Q[rows, 16 + h, qb * P:qb * P + P], KV[rows, 8 + h]
                    nc.tensor.matmul(PS[:, 2 + n % 4, :], q, k, start=True, stop=True,
                                     skip_group_check=True).then_inc(S("scores_ready"), 1)

            def values(hd):
                j = 4 + hd // 4 if hd < 16 else hd
                pe.wait_ge(S("pt_ready"), 2 * hd + 2)
                if hd >= 2:
                    pe.wait_ge(S("o_ready"), hd - 1)
                for c in range(4):
                    mm = nc.tensor.matmul(PS[:, hd % 2, 0:L], KV[:, j, c * P:c * P + P], PTT[:, hd % 2, c],
                                          start=c == 0, stop=c == 3, skip_group_check=True)
                mm.then_inc(S("pv_done"), 1)

            scores(0)
            scores(1)
            for rd in range(len(ROUNDS)):
                if rd + 2 < len(ROUNDS):
                    scores(rd + 2)
                pe.wait_ge(S("p_ready"), rd + 1)
                if rd >= 2:
                    pe.wait_ge(S("pt_ready"), rd - 1)
                for c in range(4):
                    ins = nc.tensor.transpose(PS[:, 6 + rd % 2, c * P:c * P + P],
                                              PR[:, JOBS[rd][0] % 4, c * P:c * P + P], ident)
                ins.then_inc(S("p_turn"), 1)
                if rd % 2 == 0 and rd >= 2:
                    values(rd // 2 - 1)
            values(23)
            for i in range(8):
                pe.wait_ge(S("sub_sq"), i // 4 + 1)
                mm = nc.tensor.matmul(PS[:, 2 + i // 2, (i % 2) * L:(i % 2) * L + L], const("ones"), SUBSQ[:, i],
                                      start=i % 2 == 0, stop=True, skip_group_check=True)
            mm.then_inc(S("sub_stat"), 1)
            pe.wait_ge(S("sub_std"), 1)
            branch_rhs = [split_rhs(XS), split_rhs(OS), split_rhs(XS), split_rhs(OS, KT)]
            stream_pe(pe, "branch", lambda j, k: branch_rhs[j](j, k),
                      first=lambda j: pe.wait_ge(S("o_split"), 6) if j == 1 else None)
            pe.wait_ge(S("merged_split"), 4)
            stream_pe(pe, "out2", split_rhs(XS))
            stat_pe(pe, "norm2", SQ, 4)
            stream_pe(pe, "up2", split_rhs(XS), of="norm2")
            pe.wait_ge(S("hidden2_split"), PHASES["up2"].times)
            stream_pe(pe, "down2", split_rhs(HID))
            all_evacuated(pe, "down2")
            for c in range(2):
                for t in range(KT):
                    ins = nc.tensor.transpose(PS[:, 4 * c + t // 4, (t % 4) * P:(t % 4) * P + P],
                                              H[:, t, c * P:c * P + P], ident)
                ins.then_inc(S("out_turned"), 1)


NAMES = [
    "x", "p", "mix_norm_pre", "mix_norm_post", "w_in", "ssd_conv_w", "ssd_conv_b", "ssd_dt_bias",
    "ssd_a_log", "ssd_d", "ssd_norm", "pool_w", "pool_scale", "w_out", "ffn_norm_pre",
    "ffn_norm_post", "w_ffn_up", "ffn_conv_w", "ffn_conv_b", "w_ffn_down", "ple_norm_pre",
    "w_ple_gate", "w_ple", "ple_norm_post", "c_2", "ctx_2", "c_ctx_2", "w_ada_2", "b_ada_2",
    "norm1_g_2", "w_in_2", "q_norm_a_2", "k_norm_a_2", "q_norm_b_2", "k_norm_b_2", "lam_q1_2",
    "lam_k1_2", "lam_q2_2", "lam_k2_2", "subln_g_2", "w_br_a_2", "w_br_b_2", "w_out_2",
    "norm2_g_2", "w_ff_gate_2", "w_ff_up_2", "w_ff_down_2",
]


def kernel(**inputs):
    import concourse.bacc as bacc
    from concourse.bass_utils import run_bass_kernel_spmd

    nc = bacc.Bacc("TRN2", target_bir_lowering=False, num_devices=1)
    arrays, aps = {}, {}
    for name in NAMES:
        a = np.ascontiguousarray(inputs[name])
        arrays[f"in_{name}"] = a
        aps[name] = nc.dram_tensor(f"in_{name}", a.shape, F32, kind="ExternalInput").ap()
    tables = []
    for name, a in zip(("constants", "selectors", "inverse_counts"), constant_tables()):
        arrays[f"in_{name}"] = a
        tables.append(nc.dram_tensor(f"in_{name}", a.shape, F32, kind="ExternalInput").ap())
    out = nc.dram_tensor("out", (1, L, D), F32, kind="ExternalOutput").ap()
    build(nc, aps, out, tables)
    got = run_bass_kernel_spmd(nc, [arrays], core_ids=[0])
    return got.results[0]["out"]
```

```python
from contextlib import ExitStack

import numpy as np

import concourse.bass as bass
from concourse import mybir

F32 = mybir.dt.float32
F32R = mybir.dt.float32r
ALU = mybir.AluOpType
ACT = mybir.ActivationFunctionType
AX = mybir.AxisListType

P = 128
L = 256
D = 2048
KT = D // P
DFF = 5632
FT = DFF // P
RING = 4
GC = 512
NF = GC // P
EPS = 1e-6
SSD_H = 16
LAM_INIT = 0.2

PARAM_ROWS = {
    "mix_pre": 0, "mix_post": 16, "ffn_pre": 32, "ffn_post": 48, "ple_pre": 64, "ple_post": 80,
    "norm1": 96, "norm2": 112,
    "ssd_conv_w": 128, "ssd_conv_b": 188, "ssd_norm": 200, "pool_scale": 208, "ssd_d": 216,
    "b_ada": 256, "q_norm_a": 352, "k_norm_a": 353, "q_norm_b": 354, "k_norm_b": 355, "subln": 356,
    "ffn_w0": 384, "ffn_w1": 428, "c": 472, "c_ctx": 488,
    "ffn_w2": 512, "ffn_b": 556,
}
PARAM_USED = [128, 88, 101, 120, 88]

CONST = {}
_at = 0
for _name, _n in (("ident", 128), ("ones", 128), ("half", 128), ("rot_a", 128), ("rot_b", 128),
                  ("upto", 128), ("from", 128), ("cos_a", 256), ("sin_a", 256), ("cos_b", 256),
                  ("sin_b", 256)):
    CONST[_name] = (_at, _n)
    _at += _n
NCONST = _at


def constant_tables():
    c = np.zeros((P, NCONST), np.float32)
    i, j = np.arange(P)[:, None], np.arange(P)[None, :]

    def put(name, a):
        at, n = CONST[name]
        c[:, at:at + n] = a

    put("ident", i == j)
    put("ones", 1.0)
    put("half", i // 64 == j // 64)
    for name, sub in (("rot_a", 128), ("rot_b", 64)):
        half = sub // 2
        put(name, np.where((j % sub < half) & (i == j + half), -1.0, 0.0)
            + np.where((j % sub >= half) & (i == j - half), 1.0, 0.0))
    put("upto", i <= j)
    put("from", i >= j)
    t = np.arange(L)
    for name, hd in (("a", 128), ("b", 64)):
        n = hd // 4
        freqs = (np.float32(10000.0) ** (-np.arange(n, dtype=np.float32) / np.float32(n))).astype(np.float32)
        row, col = (t // 64).astype(np.float32), (t % 64).astype(np.float32)
        ang = np.concatenate([row[:, None] * freqs, col[:, None] * freqs], axis=1).T
        rows = np.arange(P) % (hd // 2)
        put("cos_" + name, np.cos(ang)[rows])
        put("sin_" + name, np.sin(ang)[rows])
    inv = np.zeros((4, L), np.float32)
    for g, k in enumerate((2, 4, 8, 16)):
        lo, hi = np.clip(t - k // 2, 0, L), np.clip(t + k - k // 2, 0, L)
        inv[g] = 1.0 / (hi - lo).astype(np.float32)
    return c, inv


IN_COLS = [2048, 1024, 1536, 2592, 3104, 0, 512]
X_TILE = [8, 0, 4]


class Phase:

    def __init__(self, Us, times, ada_cols=(0,)):
        self.Us, self.times, self.ada_cols = Us, times, ada_cols
        ada = self.ada = len(ada_cols) if times == 1 else ada_cols[1]
        self.units = [(j, u) for j, n in enumerate(Us) for u in range(n)]
        n = len(self.units)
        self.body, self.at, self.after = [], [], [[] for _ in range(n)]
        a = 0
        for i, x in enumerate(self.units):
            self.at.append(len(self.body))
            self.body.append(("g",) + x)
            while a < 8 * ada and (i - RING + 1) * 8 * ada >= (a + 1) * (n - RING):
                self.after[i].append((len(self.body), a // 8, a % 8))
                self.body.append(("a", a // 8, a % 8))
                a += 1
        self.done = [max(n - RING for n, xs in enumerate(self.after) for x in xs if x[1:] == (i, 7))
                     for i in range(ada)]
        assert times == 1 or (n % RING == 0 and len(self.body) % RING == 0 and len(Us) % 2 == 0)


PHASES = {
    "in": Phase([8] * 7, 1, ()),
    "out": Phase([8] * 4, 1, (0, 1, 23)),
    "up": Phase([8, 8], 11, (8, 1)),
    "down": Phase([22, 22], 2, (2, 2)),
    "ple": Phase([1] * 4, 1, ()),
    "gate": Phase([8, 8], 2, (6, 1)),
    "kv": Phase([8, 8], 3, (0, 0)),
    "q": Phase([8, 8], 3, (0, 0)),
    "branch": Phase([8, 8, 8, 4], 4, (19, 1)),
    "out2": Phase([8, 8], 2, (0, 0)),
    "up2": Phase([8, 8], 11, (0, 0)),
    "down2": Phase([22] * 4, 1, ()),
}
_u = _n = _g = _a = 0
for _p in PHASES.values():
    _p.load0, _p.unit0, _p.group0, _p.ada0 = _u, _n, _g, _a
    _u += len(_p.body) * _p.times
    _n += len(_p.units) * _p.times
    _g += len(_p.Us) * _p.times
    _a += _p.ada * _p.times
UNITS, ADA_GROUPS = _n, _a
assert ADA_GROUPS == 6 * D // GC


class Body:

    def __init__(self, ph, i, rep):
        self.ph, self.i, self.rep = ph, i, rep

    def _of(self, base, per, k):
        if self.i is None:
            return base + self.rep * per + k
        return self.i * per + (base + k)

    def load(self, k):
        return self._of(self.ph.load0, len(self.ph.body), k)

    def unit(self, n):
        return self._of(self.ph.unit0, len(self.ph.units), n)

    def is_last(self, n):
        return self.ph.unit0 + self.rep * len(self.ph.units) + n + RING >= UNITS

    def ahead(self, n):
        n += RING
        return self.ph.at[n] if n < len(self.ph.units) else len(self.ph.body) + n - len(self.ph.units)

    def static_load(self, k):
        return self.ph.load0 + self.rep * len(self.ph.body) + k

    def raw_slot(self, k):
        return self.static_load(k) % RING

    def slot(self, n):
        return (self.ph.unit0 + self.rep * len(self.ph.units) + n) % RING

    def landed(self, k):
        n = self.static_load(k) // RING + 1
        return 16 * n if self.i is None else self.i * (16 * len(self.ph.body) // RING) + 16 * n

    def group(self, j):
        return self._of(self.ph.group0, len(self.ph.Us), j)

    def local(self, j):
        return self._of(0, len(self.ph.Us), j)

    def set(self, j):
        return (self.ph.group0 + self.rep * len(self.ph.Us) + j) % 2

    def ada(self, a):
        return self._of(self.ph.ada0, self.ph.ada, a)

    def ada_col(self, a):
        if self.ph.times == 1:
            return self.ph.ada_cols[a]
        return self._of(self.ph.ada_cols[0], self.ph.ada, a)

    def n(self, per=1, k=0):
        return self._of(0, per, k)


def bodies(eng, name, straight=False):
    ph = PHASES[name]
    if ph.times == 1 or straight or name in ("kv", "q"):
        for rep in range(ph.times):
            yield Body(ph, None, rep)
    else:
        with eng.Fori(0, ph.times) as i:
            yield Body(ph, i, 0)


class Chain:

    def __init__(self, eng, sem):
        self.eng, self.sem, self.n, self.i, self.per = eng, sem, 0, None, 0

    def mark(self, ins):
        ins.then_inc(self.sem, 1)
        self.n += 1
        return self.n

    def wait(self, n=None):
        n = self.n if n is None else n
        self.eng.wait_ge(self.sem, n if self.i is None else self.i * self.per + n)

    def start(self, b, per):
        self.i, self.per, self.n0 = b.i, per, self.n

    def end(self, b):
        assert self.n - self.n0 == self.per, self.n - self.n0
        if b.i is not None:
            self.n = self.n0 + self.per * b.ph.times
        self.i = None


def build(nc, A, out, tables):
    consts_d, inv_d = tables

    def ktiles(w):
        return w[0].rearrange("(t p) n -> p t n", p=P)

    W_IN, W_OUT, W_UP, W_DOWN = (ktiles(A[n]) for n in ("w_in", "w_out", "w_ffn_up", "w_ffn_down"))
    W_GATE, W_PLE, W_ADA, W_IN2 = (ktiles(A[n]) for n in ("w_ple_gate", "w_ple", "w_ada_2", "w_in_2"))
    W_BR_A, W_BR_B, W_OUT2 = (ktiles(A[n]) for n in ("w_br_a_2", "w_br_b_2", "w_out_2"))
    W_G2, W_U2, W_D2 = (ktiles(A[n]) for n in ("w_ff_gate_2", "w_ff_up_2", "w_ff_down_2"))

    with ExitStack() as ctx:
        def sb(name, shape, dt=F32):
            return ctx.enter_context(nc.sbuf_tensor(name, shape, dt))

        def freed(name, shape, dt):
            with nc.sbuf_tensor(name, shape, dt) as t:
                return t

        sems = {}

        def S(name):
            if name not in sems:
                sems[name] = ctx.enter_context(nc.semaphore(name))
            return sems[name]

        raw = sb("w_raw", [P, RING, 2, GC])
        w_hi = sb("w_hi", [P, RING, 2, GC], F32R)
        w_lo = sb("w_lo", [P, RING, 2, GC], F32R)
        H = sb("residual", [P, KT, L])
        XS = freed("x_split", [P, KT, 2, L], F32R)
        XF = sb("region_x", [P, 2 * KT * L])
        NB = FT * 2 * L
        HID = freed("hidden_split", [P, FT, 2, L], F32R)
        CS = freed("ctx_split", [P, KT, 2, L], F32R)
        with nc.sbuf_tensor("pad_o", [P, 8192], F32):
            OS = freed("attn_split", [P, 24, 2, L], F32R)
        BF = sb("region_b", [P, NB])
        with nc.sbuf_tensor("pad_e", [P, NF * L], F32):
            PSP = freed("p_split", [P, 2, 2, L], F32R)
        EV = sb("evac", [P, 2, NF, L])
        EVF = EV.rearrange("p a f n -> p (a f n)")
        C = sb("constants", [P, NCONST])
        PRM = sb("params", [P, 5, P])
        MADA = sb("ada", [P, 6 * KT, 2])
        COND = sb("conditions", [P, KT, 2])
        GE = sb("gain_eff", [P, 3, KT])
        SM = sb("small", [P, 608])
        ST = sb("stat", [P, 512])
        PS = ctx.enter_context(nc.psum_tensor("psum", [P, 8, 512], F32))

        def const(name):
            at, n = CONST[name]
            return C[:, at:at + n]

        def prm(name, i=0, n=1):
            at = PARAM_ROWS[name] + i
            return PRM[:, at // P, at % P:at % P + n]

        def prm_dyn(name, i):
            at = PARAM_ROWS[name]
            return PRM[:, at // P, bass.ds(i + at % P, 1)]

        def bf(at, *shape):
            n = int(np.prod(shape))
            v = BF[:, at:at + n]
            if len(shape) == 1:
                return v
            names = "abcd"[:len(shape)]
            return v.rearrange(f"p ({' '.join(names)}) -> p {' '.join(names)}",
                               **{k: s for k, s in zip(names[1:], shape[1:])})

        def xf(at, *shape):
            n = int(np.prod(shape))
            v = XF[:, at:at + n]
            if len(shape) == 1:
                return v
            names = "abcd"[:len(shape)]
            return v.rearrange(f"p ({' '.join(names)}) -> p {' '.join(names)}",
                               **{k: s for k, s in zip(names[1:], shape[1:])})

        def r(ap):
            return ap.bitcast(F32)

        SQ = bf(14336, KT, L)
        Z = bf(18432, KT, L)
        XNAT = bf(0, 2, D)
        PROW = bf(4096, 5, P)
        WDT = bf(4736, KT, 32)
        DROW = bf(5248, P)
        DPAIR = bf(5376, 2)
        XBC = bf(0, 12, L)
        SZ = bf(3072, 8, L)
        UPW = L + 16
        UP = bf(5120, 8, UPW)
        ER = bf(7296, 2, 2, 3, P)
        PW = bf(9344, 4, 2, L)
        XDT = bf(11392, 2, 2, SSD_H, 64)
        CBM = bf(15488, 2, 2, 3, P)
        Y = bf(17024, KT, L)
        MIXED = Y[:, 8:16]
        YSQ = bf(5120, 8, L)
        SA, SB = (EVF[:, i * 2 * UPW:(i + 1) * 2 * UPW].rearrange("p (t n) -> p t n", t=2) for i in range(2))
        INV = bf(21120, 4, L)
        MR = [bf(8832, 3 * P)] + [EVF[:, at:at + 3 * P] for at in (4 * UPW, 4 * UPW + 3 * P)]
        OUT1 = bf(0, KT, L)
        OSQ1 = bf(4096, KT, L)
        OUT2 = xf(0, KT, L)
        OSQ2 = xf(4096, KT, L)
        PLE = bf(0, KT, L)
        OUT3 = bf(5120, KT, L)
        OSQ3 = bf(9216, KT, L)
        PNAT, PTR = (EVF[:, at:at + 2 * L].rearrange("p (t n) -> p t n", t=2) for at in (0, 2 * L))
        CNAT = bf(0, 2, D)
        CTX = bf(9216, KT, L)
        CTX_SQ = bf(5120, KT, L)
        KV = bf(8192, 24, 2 * L)
        Q = bf(0, 24, L)
        PR = bf(6144, 4, 512)
        PTT = bf(20480, 2, 4, L)
        MG = bf(0, KT, L)
        ONAT = bf(0, 2, D)
        evA, evB = EV[:, 0], EV[:, 1]

        def acc(s):
            return PS[:, 2 * s:2 * s + 2, :].rearrange("p b (h n) -> p (b h) n", h=2)

        def accf(s, f):
            return PS[:, 2 * s + f // 2, (f % 2) * L:(f % 2) * L + L]

        ADA = PS[:, 5, 0:2 * NF].rearrange("p (f v) -> p f v", v=2)
        ADA_SUM = ST[:, 0:GC], SM[:, 96:96 + GC]

        w_landed = [S(f"w_landed{i}") for i in range(RING)]
        w_rounded, w_split, w_used = S("w_rounded"), S("w_split"), S("w_used")
        evacuated, ada_evacuated = S("evacuated"), S("ada_evacuated")
        ada_half, ada_copied, ada_reduced = S("ada_half"), S("ada_copied"), S("ada_reduced")
        norm_sq, norm_stat, norm_std, norm_z, norm_hi, norm_ready, norm_added = (
            S("norm_" + kind) for kind in ("sq", "stat", "std", "z", "hi", "ready", "added"))
        norms = ("mix_pre", "mix_post", "ffn_pre", "ffn_post", "ple_pre", "ple_post", "norm1", "norm_c", "norm2")

        def so_far(tag, kind, n):
            before = norms[:norms.index(tag)]
            posts = sum(t.endswith("_post") for t in before)
            per, times = {"sq": (4, len(before)), "stat": (1, len(before)), "std": (1, len(before)),
                          "z": (16, len(before) - posts), "hi": (4, len(before) - posts),
                          "ready": (4, len(before) - posts), "added": (4, posts)}[kind]
            return per * times + n

        prev_ada = {}
        for name, ph in PHASES.items():
            at = [k for k, x in enumerate(ph.body) if x[0] == "a"]
            prev_ada[name] = dict(zip(at[1:], at[:-1]))

        def source(name, b, x):
            kind, j, u = x
            k = slice(2 * u, 2 * u + 2)
            if kind == "a":
                return W_ADA[:, k, bass.ds(b.ada_col(j) * GC, GC)]
            if name == "in":
                col = IN_COLS[j]
                return W_IN[:, k, col:col + GC]
            if name == "out":
                k = slice((2 * u + 8) % KT, (2 * u + 8) % KT + 2)
            if name == "up":
                return W_UP[:, k, bass.ds(b.n(GC, j * DFF), GC)]
            if name == "branch":
                w, c0 = [(W_IN2, 6144), (W_BR_A, 0), (W_IN2, 8192), (W_BR_B, 0)][j]
                return w[:, k, bass.ds(b.n(GC, c0), GC)]
            if name == "up2":
                return (W_G2, W_U2)[j][:, k, bass.ds(b.n(GC, 0), GC)]
            w, c0 = {"out": (W_OUT, 0), "down": (W_DOWN, 0), "ple": (W_PLE, 0), "gate": (W_GATE, 0),
                     "kv": (W_IN2, 0), "q": (W_IN2, 3072), "out2": (W_OUT2, 0),
                     "down2": (W_D2, 0)}[name]
            return w[:, k, bass.ds(b.local(j) * GC + c0, GC)]

        def stream_pe(pe, name, rhs, ready=None, first=None, late=None):
            for b in bodies(pe, name):
                for n, (j, u) in enumerate(b.ph.units):
                    slot = b.slot(n)
                    if u == 0:
                        pe.wait_ge(evacuated, b.group(j) + 1)
                        if first is not None:
                            first(j)
                    if ready is not None and j == 0 and u % 2 == 0:
                        ready(u // 2)
                    pe.wait_ge(w_split, b.load(b.ph.at[n]) + RING + 1)
                    for t in range(2):
                        kt = 2 * u + t
                        last = kt == 2 * b.ph.Us[j] - 1
                        for f in range(NF):
                            hi = w_hi[:, slot, t, f * P:f * P + P]
                            lo = w_lo[:, slot, t, f * P:f * P + P]
                            to = accf(b.set(j), f)
                            x_hi, x_lo = rhs(j, kt)
                            nc.tensor.matmul(to, hi, x_hi, start=kt == 0 and f % 2 == 0, stop=False,
                                             skip_group_check=True)
                            nc.tensor.matmul(to, hi, x_lo, start=False, stop=False, skip_group_check=True)
                            mm = nc.tensor.matmul(to, lo, x_hi, start=False, stop=last, skip_group_check=True)
                    mm.then_inc(w_used, 1)
                    for i, at in enumerate(b.ph.done):
                        if n == at + 3:
                            pe.wait_ge(ada_copied, b.ada(i) + 1)
                            pe.wait_ge(ada_evacuated, b.ada(i) + 1)
                            for v in range(ada_conditions(name, i)):
                                for f in range(NF):
                                    mm = nc.tensor.matmul(ADA[:, f, v:v + 1], ADA_SUM[v][:, f * P:f * P + P],
                                                          const("ones")[:, 0:1], start=f == 0 and v == 0,
                                                          stop=True, skip_group_check=True)
                            mm.then_inc(ada_reduced, 1)
                    if late is not None:
                        late(b, j, u)

        def kv_stream(pe, late):
            for b in bodies(pe, "kv"):
                for n, (j, u) in enumerate(b.ph.units):
                    slot = b.slot(n)
                    if u % 2 == 0 and j == 0:
                        pe.wait_ge(norm_ready, so_far("norm1", "ready", u + 2))
                    if u == 0:
                        pe.wait_ge(evacuated, b.group(j) + 2)
                    pe.wait_ge(w_split, b.load(b.ph.at[n]) + RING + 1)
                    for t in range(2):
                        kt = 2 * u + t
                        for f in range(NF):
                            if kt == 0 and f == 2:
                                pe.wait_ge(S("kv_half"), b.local(j) + 1)
                            hi = w_hi[:, slot, t, f * P:f * P + P]
                            lo = w_lo[:, slot, t, f * P:f * P + P]
                            for i, x in enumerate((XS, CS)):
                                to = PS[:, f, i * L:i * L + L]
                                nc.tensor.matmul(to, hi, x[:, kt, 0], start=kt == 0 and i == 0, stop=False,
                                                 skip_group_check=True)
                                nc.tensor.matmul(to, hi, x[:, kt, 1], start=False, stop=False,
                                                 skip_group_check=True)
                                mm = nc.tensor.matmul(to, lo, x[:, kt, 0], start=False, stop=kt == KT - 1,
                                                      skip_group_check=True)
                    mm.then_inc(w_used, 1)
                    late(b, j, u)

        def stream_act(act, name, evac, late=None, evac_first=False):
            for b in bodies(act, name):
                for n, (j, u) in enumerate(b.ph.units):
                    if evac_first and u == b.ph.Us[j] - 1:
                        evac(b, j, n)
                    if not b.is_last(n):
                        k = b.ahead(n)
                        act.wait_ge(w_landed[b.raw_slot(k)], b.landed(k))
                        act.wait_ge(w_used, b.unit(n) + RING + 1)
                        nc.scalar.activation(w_hi[:, b.slot(n)], raw[:, b.raw_slot(k)],
                                             ACT.Copy).then_inc(w_rounded, 1)
                    if not evac_first and u == b.ph.Us[j] - 1:
                        evac(b, j, n)
                    if late is not None:
                        late(b, j, u)

        def ada_conditions(name, i):
            cols = PHASES[name].ada_cols
            return 2 if cols[i if PHASES[name].times == 1 else 0] < 2 * D // GC else 1

        def ada_unit(dve, b, name, k, i, u):
            slot, nv = b.raw_slot(k), ada_conditions(name, i)
            dve.wait_ge(w_landed[slot], b.landed(k))
            for t in range(2):
                if u == 0 and t == 0:
                    if b.i is not None or b.ada(i) > 0:
                        dve.wait_ge(ada_copied, b.ada(i))
                elif t == 0:
                    dve.wait_ge(w_split, b.load(prev_ada[name][k]) + RING + 1)
                else:
                    dve.wait_ge(ada_half, b.ada(i) * 8 + (u + 1))
                for v in range(nv):
                    acc_v, c = PS[:, 6 + v, :], COND[:, 2 * u + t, v:v + 1]
                    if u == 0 and t == 0:
                        ins = nc.vector.tensor_scalar(acc_v, raw[:, slot, t], c, None, ALU.mult)
                    else:
                        ins = nc.vector.scalar_tensor_tensor(acc_v, raw[:, slot, t], c, acc_v, ALU.mult, ALU.add)
                ins.then_inc(ada_half if t == 0 else w_split, 1)
            if u == 7:
                dve.wait_ge(w_split, b.load(k) + RING + 1)
                for v in range(nv):
                    ins = nc.vector.tensor_copy(ADA_SUM[v], PS[:, 6 + v, :])
                ins.then_inc(ada_copied, 1)

        def stream_dve(dve, name, evac, late=None, evac_first=False):
            for b in bodies(dve, name):
                for n, (j, u) in enumerate(b.ph.units):
                    if evac_first and u == b.ph.Us[j] - 1:
                        evac(b, j, n)
                    if not b.is_last(n):
                        slot, k = b.slot(n), b.ahead(n)
                        dve.wait_ge(w_rounded, b.unit(n) + RING + 1)
                        nc.vector.tensor_tensor(w_lo[:, slot], raw[:, b.raw_slot(k)], r(w_hi[:, slot]),
                                                ALU.subtract).then_inc(w_split, 1)
                    if n + RING < len(b.ph.units):
                        for k, i, au in b.ph.after[n + RING]:
                            ada_unit(dve, b, name, k, i, au)
                    if not evac_first and u == b.ph.Us[j] - 1:
                        evac(b, j, n)
                    for i, at in enumerate(b.ph.done):
                        if n == at + 4:
                            nv = ada_conditions(name, i)
                            dve.wait_ge(ada_reduced, b.ada(i) + 1)
                            nc.vector.tensor_copy(MADA[:, bass.ds(b.ada_col(i) * NF, NF), 0:nv],
                                                  ADA[:, :, 0:nv]).then_inc(ada_evacuated, 1)
                    if late is not None:
                        late(b, j, u)

        def first_tap(act, x, out, weight, bias):
            for f in range(NF):
                nc.scalar.activation(out(f), x(f), ACT.Identity, bias=bias(f), scale=weight(f)
                                     ).then_inc(S("first_tap"), 1)

        def group_used(eng, b, k):
            eng.wait_ge(w_used, b.unit(k) + RING + 1)

        def all_evacuated(eng, name):
            ph = PHASES[name]
            eng.wait_ge(ada_evacuated, 1 + ph.ada0 + ph.ada * ph.times)
            eng.wait_ge(evacuated, 2 + ph.group0 + len(ph.Us) * ph.times)

        def squares_act(act, tag, src, added=None, sq=SQ, quarters=range(4)):
            for q in quarters:
                if added is not None:
                    act.wait_ge(norm_added, so_far(added, "added", q + 1))
                nc.scalar.activation(sq[:, 4 * q:4 * q + 4], src[:, 4 * q:4 * q + 4],
                                     ACT.Square).then_inc(norm_sq, 1)

        def stat_pe(pe, tag, sq, per, bank=4, between=None):
            for t in range(KT):
                if t == 3 * KT // 4 and between is not None:
                    between()
                pe.wait_ge(norm_sq, so_far(tag, "sq", t // (KT // per) + 1))
                mm = nc.tensor.matmul(PS[:, bank, 0:L], const("ones"), sq[:, t], start=t == 0, stop=t == KT - 1,
                                      skip_group_check=True)
            mm.then_inc(norm_stat, 1)

        def std_act(act, tag, bank=4, at=0):
            act.wait_ge(norm_stat, so_far(tag, "stat", 1))
            nc.scalar.activation(ST[:, at:at + L], PS[:, bank, 0:L], ACT.Sqrt, bias=SM[:, 0:1],
                                 scale=1.0 / D).then_inc(norm_std, 1)

        def rstd_dve(dve, ch, tag, at=0):
            dve.wait_ge(norm_std, so_far(tag, "std", 1))
            ch.mark(nc.vector.reciprocal(ST[:, at:at + L], ST[:, at:at + L]))
            ch.wait()

        def pre_act(act, tag, dst, shift=None):
            std_act(act, tag)
            hi_act(act, tag, dst, shift)

        def hi_act(act, tag, dst, shift=None):
            for q in range(4):
                act.wait_ge(norm_z, so_far(tag, "z", 4 * q + 4))
                if shift is None:
                    nc.scalar.activation(dst[:, 4 * q:4 * q + 4, 0], Z[:, 4 * q:4 * q + 4],
                                         ACT.Copy).then_inc(norm_hi, 1)
                else:
                    for t in range(4 * q, 4 * q + 4):
                        ins = nc.scalar.activation(dst[:, t, 0], Z[:, t], ACT.Identity, bias=shift(t))
                    ins.then_inc(norm_hi, 1)

        def pre_dve(dve, ch, tag, src, gain, dst, shift=None):
            rstd_dve(dve, ch, tag)

            def scaled(q):
                for t in range(4 * q, 4 * q + 4):
                    nc.vector.scalar_tensor_tensor(Z[:, t], src[:, t], gain(t), ST[:, 0:L], ALU.mult,
                                                   ALU.mult).then_inc(norm_z, 1)

            def rest(q):
                dve.wait_ge(norm_hi, so_far(tag, "hi", q + 1))
                dve.wait_ge(norm_z, so_far(tag, "z", 4 * q + 4))
                if shift is None:
                    ins = nc.vector.tensor_tensor(dst[:, 4 * q:4 * q + 4, 1], Z[:, 4 * q:4 * q + 4],
                                                  r(dst[:, 4 * q:4 * q + 4, 0]), ALU.subtract)
                else:
                    for t in range(4 * q, 4 * q + 4):
                        ins = nc.vector.scalar_tensor_tensor(dst[:, t, 1], Z[:, t], shift(t), r(dst[:, t, 0]),
                                                             ALU.add, ALU.subtract)
                ins.then_inc(norm_ready, 1)

            scaled(0)
            for q in range(4):
                if q < 3:
                    scaled(q + 1)
                rest(q)

        def post_dve(dve, ch, tag, o, gain):
            rstd_dve(dve, ch, tag)

            def scaled(q):
                for t in range(4 * q, 4 * q + 4):
                    ch.mark(nc.vector.scalar_tensor_tensor(Z[:, t], o[:, t], prm(gain, t), ST[:, 0:L], ALU.mult,
                                                           ALU.mult))

            scaled(0)
            for q in range(4):
                if q < 3:
                    scaled(q + 1)
                ch.wait(ch.n - (4 if q < 3 else 0))
                nc.vector.tensor_tensor(H[:, 4 * q:4 * q + 4], H[:, 4 * q:4 * q + 4], Z[:, 4 * q:4 * q + 4],
                                        ALU.add).then_inc(norm_added, 1)

        PAIRED = [(q, v) for q in range(4) for v in range(2)]

        def split_rhs(xs, at=0):
            return lambda j, k: (xs[:, at + k, 0], xs[:, at + k, 1])

        copied = S("copied")
        COPIED_BEFORE, n = {}, 0
        for name in ("out", "down", "ple", "q"):
            COPIED_BEFORE[name] = n
            n += len(PHASES[name].Us) * PHASES[name].times

        def copy_act(act, name, o, sq=None):
            def evac(b, j, k):
                at = bass.ds(b.local(j) * NF, NF)
                group_used(act, b, k)
                nc.scalar.activation(o[:, at], acc(b.set(j)), ACT.Copy).then_inc(copied, 1)
                if sq is not None:
                    act.wait_ge(copied, b.local(j) + (COPIED_BEFORE[name] + 1))
                    nc.scalar.activation(sq[:, at], o[:, at], ACT.Square).then_inc(norm_sq, 1)
            return evac

        def copied_dve(dve, name):
            def evac(b, j, k):
                dve.wait_ge(copied, b.local(j) + (COPIED_BEFORE[name] + 1))
                dve.sem_inc(evacuated, 1)
            return evac

        IN_TAPS = 3 * NF

        block = ctx.enter_context(nc.Block())

        def columns(a):
            if len(a.shape) == 2:
                return a.rearrange("k (r c) -> (k r) c", c=P)
            return a.rearrange("(r c) -> r c", c=P)

        def param_rows(name, src, c0=0):
            at, (k, width) = PARAM_ROWS[name], src.shape
            return PROW[at % P:at % P + k, at // P, c0:c0 + width], src

        params = [param_rows(name, columns(A[key][0])) for name, key in (
            ("mix_pre", "mix_norm_pre"), ("mix_post", "mix_norm_post"), ("ffn_pre", "ffn_norm_pre"),
            ("ffn_post", "ffn_norm_post"), ("ple_pre", "ple_norm_pre"), ("ple_post", "ple_norm_post"),
            ("norm1", "norm1_g_2"), ("norm2", "norm2_g_2"), ("ssd_conv_w", "ssd_conv_w"),
            ("ssd_conv_b", "ssd_conv_b"), ("ssd_norm", "ssd_norm"), ("pool_scale", "pool_scale"),
            ("b_ada", "b_ada_2"), ("q_norm_a", "q_norm_a_2"), ("k_norm_a", "k_norm_a_2"),
            ("subln", "subln_g_2"), ("ffn_b", "ffn_conv_b"), ("c", "c_2"))]
        params.append(param_rows("c_ctx", columns(A["c_ctx_2"])))
        params += [param_rows(f"ffn_w{i}", columns(A["ffn_conv_w"][0, i])) for i in range(3)]
        params += [param_rows(name, A[name + "_2"][0:1, :], c0) for name in ("q_norm_b", "k_norm_b") for c0 in (0, 64)]
        params.append((DPAIR[0:8], A["ssd_d"][0].rearrange("(t e) -> t e", e=2)))
        for at, key in ((32, "ssd_dt_bias"), (64, "ssd_a_log")):
            params.append((SM[:, at:at + 32], A[key][0].rearrange("a b -> (a b)").partition_broadcast(P)))
        for i, key in enumerate(("lam_q1_2", "lam_k1_2", "lam_q2_2", "lam_k2_2")):
            params.append((EV[:, 0, 0, 64 * i:64 * i + 64], A[key][0].partition_broadcast(P)))

        def all_params(eng):
            eng.wait_ge(S("params_landed"), 16 * len(params[0::2]))
            eng.wait_ge(S("params_by_pool"), 16 * len(params[1::2]))

        @block.sync
        def _(sp):
            sp.dma_start(C[:, :], consts_d).then_inc(S("consts_landed"), 16)
            for t in range(2):
                sp.dma_start(XNAT[:, t, :], A["x"][0, t * P:(t + 1) * P, :]).then_inc(S("x_landed"), 16)
            for to, src in params[0::2]:
                sp.dma_start(to, src).then_inc(S("params_landed"), 16)

            def stream(name):
                for b in bodies(sp, name, straight=name == "branch"):
                    for k, x in enumerate(b.ph.body):
                        if name == "in" and k == RING:
                            sp.dma_start(WDT, W_IN[:, :, 2560:2592]).then_inc(S("wdt_landed"), 16)
                        slot = b.raw_slot(k)
                        sp.wait_ge(w_split, b.load(k) + 1)
                        sp.dma_start(raw[:, slot], source(name, b, x)).then_inc(w_landed[slot], 16)

            stream("in")
            stream("out")
            stream("up")
            stream("down")
            stream("ple")
            stream("gate")
            for name in ("kv", "q", "branch", "out2", "up2", "down2"):
                stream(name)
            for t, by in enumerate(("out_copied_dve", "out_copied_act")):
                sp.wait_ge(S(by), 1)
                sp.dma_start(out[0, t * P:(t + 1) * P, :], ONAT[:, t, :]).then_inc(S("stored"), 16)
            sp.wait_ge(S("stored"), 32)

        @block.gpsimd
        def _(pool):
            for to, src in params[1::2]:
                pool.dma_start(to, src).then_inc(S("params_by_pool"), 16)
            pool.dma_start(PW, A["pool_w"][0].rearrange("g (t p) n -> p g t n", p=P)).then_inc(S("poolw_landed"), 16)
            pool.wait_ge(norm_ready, so_far("mix_pre", "ready", 4))
            pool.wait_ge(S("dt_projected"), 1)
            for g in range(4):
                pool.dma_start(INV[:, g, :], inv_d[g].partition_broadcast(P)).then_inc(S("inv_landed"), 16)
            pool.wait_ge(evacuated, 2 + PHASES["down"].group0)
            for t in range(2):
                pool.dma_start(PNAT[:, t, :], A["p"][0, 0, t * P:(t + 1) * P, :]).then_inc(S("p_landed"), 16)
            pool.wait_ge(evacuated, 2 + PHASES["kv"].group0)
            for t in range(2):
                pool.dma_start(CNAT[:, t, :], A["ctx_2"][0, t * P:(t + 1) * P, :]).then_inc(S("ctx_landed"), 16)

        def beside(entries, first, end):
            def at_step(step):
                for at, work, arg in entries:
                    if at == step:
                        work(arg)

            def late(b, j, u):
                at_step(8 * (b.ph.group0 - PHASES[first].group0 + b.rep * len(b.ph.Us) + j) + u)

            def tail():
                for step in range(end, max(x[0] for x in entries) + 1):
                    at_step(step)
            return late, tail

        SSD_STEPS = [(t, e, d) for t in range(8) for e in range(2) for d in range(2)]
        IN_END = 8 * 7
        PAIR_AT = [18, 21, 23, 25, 27, 29] + [21 + 2 * m for m in range(6, 16)]
        STEP_AT = [PAIR_AT[n // 2] + n % 2 for n in range(32)]
        TURN_AT = {(0, 0): 19, (0, 1): 21, (1, 0): 31, (1, 1): 33}
        POOL_AT = [49, 50, 52, 53]

        def turn_bank(half, c):
            return 5 - c if half == 0 else 4 + c

        ROUNDS = [("a", h, qb) for h in range(16) for qb in range(2)] + \
                 [("b", h, qb) for h in range(8) for qb in range(2)]
        JOBS, at = [], 0
        for rd in ROUNDS:
            JOBS.append(list(range(at, at + (1 if rd[0] == "a" else 2))))
            at += len(JOBS[-1])

        HEADS = []
        for j in range(6):
            for f in range(NF):
                t, step = NF * j + f, 8 * (j + 1) + 2 * f
                if j in (1, 4, 5):
                    HEADS.append((KV[:, t], 2 * L, None, "v", step))
                else:
                    kind = "a" if j == 0 else "b"
                    HEADS.append((KV[:, t], 2 * L, "k_norm_" + kind, kind, step))
        for j in range(6):
            for f in range(NF):
                kind = "a" if j < 4 else "b"
                HEADS.append((Q[:, NF * j + f], L, "q_norm_" + kind, kind, 8 * (j + 7) + (2 if j < 4 else 1) * f))
        QK_BEFORE = [sum(x[3] != "v" for x in HEADS[:i]) for i in range(len(HEADS))]
        QK_ITEM = [i for i, x in enumerate(HEADS) if x[3] != "v"]
        QK_SQ = EV[:, 0].rearrange("p (a f) n -> p a (f n)", a=2)
        QK_ST = EV[:, 1].rearrange("p (a f) n -> p a (f n)", a=2)
        QK_T = PTT.rearrange("p a b n -> p (a b) n")
        HEADS_END = 8 * 12

        def per_head(stages):
            return [(x[4] + after, work, i) for after, work in stages for i, x in enumerate(HEADS)]

        def heads_landed(eng, i):
            j = i // NF
            eng.wait_ge(evacuated, 3 + PHASES["kv"].group0 + j)
            if j < 6:
                eng.wait_ge(S("kv_half"), 2 + j)

        SUBSQ, SUB_ROOT = bf(6144, 8, L), SM[:, 288:304]
        NEGMAX, SUMS, RSUM = SM[:, 96:160], SM[:, 160:224], SM[:, 224:288]

        @block.scalar
        def _(act):
            seen = Chain(act, S("act_chain"))
            act.wait_ge(S("eps_ready"), 1)
            act.wait_ge(S("x_turned"), 2)
            nc.scalar.activation(H[:, 8:16], PS[:, 4:8, :].rearrange("p b (h n) -> p (b h) n", h=2),
                                 ACT.Copy).then_inc(S("h_loaded_act"), 1)
            act.wait_ge(S("h_loaded_act"), 1)
            act.wait_ge(S("h_loaded_dve"), 1)
            squares_act(act, "mix_pre", H)
            for n in range(RING):
                act.wait_ge(w_landed[n], 16)
                nc.scalar.activation(w_hi[:, n], raw[:, n], ACT.Copy).then_inc(w_rounded, 1)
            std_act(act, "mix_pre")
            hi_act(act, "mix_pre", XS)

            def conditions(_):
                act.wait_ge(S("params_turned"), 1)
                for v, name in enumerate(("c", "c_ctx")):
                    ins = nc.scalar.activation(COND[:, :, v], prm(name, 0, KT), ACT.Silu)
                ins.then_inc(S("conditions_ready"), 1)
                act.wait_ge(S("lam_sums"), 1)
                nc.scalar.activation(SM[:, 1:3], SM[:, 1:3], ACT.Exp).then_inc(S("lam_exp"), 1)

            def in_evac(b, j, k):
                group_used(act, b, k)
                if j < 3:
                    t0 = X_TILE[j]
                    first_tap(act, lambda f: accf(b.set(j), f), lambda f: XBC[:, t0 + f],
                              lambda f: prm("ssd_conv_w", 24 + t0 + f), lambda f: prm("ssd_conv_b", t0 + f))
                elif j < 5:
                    act.wait_ge(S("u_padded"), 1)
                    t = slice(4 * (j - 3), 4 * (j - 3) + 4)
                    nc.scalar.activation(UP[:, t, 8:8 + L], acc(b.set(j)), ACT.Copy).then_inc(S("u_ready"), 1)
                else:
                    t = slice(4 * (j - 5), 4 * (j - 5) + 4)
                    nc.scalar.activation(SZ[:, t], acc(b.set(j)), ACT.Silu).then_inc(S("z_ready"), 1)

            def conv_silu(j):
                act.wait_ge(evacuated, 3 + j)
                t = slice(X_TILE[j], X_TILE[j] + 4)
                nc.scalar.activation(XBC[:, t], XBC[:, t], ACT.Silu).then_inc(S("xbc_ready"), 1)

            def dt_exp(_):
                act.wait_ge(S("dt_biased"), 1)
                seen.mark(nc.scalar.activation(SM[:, 384:448], SM[:, 128:192], ACT.Abs))
                seen.wait()
                nc.scalar.activation(SM[:, 192:256], SM[:, 384:448], ACT.Exp, scale=-1.0)
                nc.scalar.activation(SM[:, 64:96], SM[:, 64:96], ACT.Exp).then_inc(S("dt_exp"), 1)

            def dt_ln(_):
                act.wait_ge(S("dt_plus_one"), 1)
                nc.scalar.activation(SM[:, 320:384], SM[:, 256:320], ACT.Ln).then_inc(S("dt_ln"), 1)

            def acum_rows(_):
                act.wait_ge(S("acum_done"), 1)
                nc.scalar.activation(ST[0:32, :], PS[0:32, 6, :], ACT.Copy).then_inc(S("acum_rows"), 1)

            def pair(m):
                return m // 2, m % 2

            def decays_between(m):
                t, e = pair(m)
                act.wait_ge(S("row_ready"), m + 1)
                act.wait_ge(S("acum_columns"), 1)
                if m >= 2:
                    act.wait_ge(S("mix_matrix"), 2 * m - 2)
                for d in range(2):
                    h, l0 = 16 * d + 2 * t + e, P if d == 0 else L
                    ins = nc.scalar.activation(ER[:, m % 2, d, 1], PS[:, 4 + m % 2, l0:l0 + P], ACT.Exp,
                                               bias=SM[:, 384 + h:385 + h])
                ins.then_inc(S("between_ready"), 1)

            def decays(m):
                act.wait_ge(S("exponent_ready"), m + 1)
                er = ER[:, m % 2, :, 0:3:2]
                nc.scalar.activation(er, er, ACT.Exp).then_inc(S("decay_ready"), 1)

            def pool_out(g):
                act.wait_ge(S("pool_product"), g + 1)
                for f in range(2):
                    ins = nc.scalar.activation(Y[:, 8 + 2 * g + f], PS[:, 2 + g % 2, f * L:f * L + L], ACT.Identity,
                                               scale=prm("pool_scale", 2 * g + f))
                ins.then_inc(S("pool_scaled"), 1)

            def y_square(g):
                act.wait_ge(S("y_gated"), g + 1)
                nc.scalar.activation(YSQ[:, 4 * g:4 * g + 4], Y[:, 4 * g:4 * g + 4],
                                     ACT.Square).then_inc(S("y_sq"), 1)

            def y_root(g):
                act.wait_ge(S("y_stat"), g + 1)
                nc.scalar.activation(ST[:, g * L:g * L + L], PS[:, 2 + g, 0:L], ACT.Sqrt, bias=SM[:, 0:1],
                                     scale=1.0 / 512).then_inc(S("y_std"), 1)

            def mix_hi(q):
                if q < 2:
                    act.wait_ge(S("y_normed"), 4 * q + 4)
                else:
                    act.wait_ge(S("pool_scaled"), 2 * q - 2)
                nc.scalar.activation(XS[:, 4 * q:4 * q + 4, 0], Y[:, 4 * q:4 * q + 4],
                                     ACT.Copy).then_inc(S("mix_hi"), 1)

            late, tail = beside(
                [(2, conditions, None), (5, dt_exp, None), (8, dt_ln, None), (14, acum_rows, None)] +
                [(8 * j + 10, conv_silu, j) for j in range(3)] +
                [(at + 3, decays, m) for m, at in enumerate(PAIR_AT)] +
                [(at + 1, decays_between, m) for m, at in enumerate(PAIR_AT)] +
                [(at + 1, pool_out, g) for g, at in enumerate(POOL_AT)] +
                [(52, y_square, 0), (56, mix_hi, 2), (56, mix_hi, 3), (57, y_root, 0), (58, y_square, 1),
                 (59, mix_hi, 0), (60, y_root, 1), (61, mix_hi, 1)], "in", IN_END)
            stream_act(act, "in", in_evac, late)
            tail()

            stream_act(act, "out", copy_act(act, "out", OUT1, OSQ1))
            std_act(act, "mix_post")
            squares_act(act, "ffn_pre", H, added="mix_post")
            pre_act(act, "ffn_pre", XS)

            def up_evac(b, j, k):
                if j == 0:
                    group_used(act, b, k)
                    act.wait_ge(evacuated, b.group(j) + 2)
                    first_tap(act, lambda f: accf(b.set(0), f), lambda f: evA[:, f],
                              lambda f: prm_dyn("ffn_w1", b.n(NF, f)), lambda f: prm_dyn("ffn_b", b.n(NF, f)))
                else:
                    act.wait_ge(evacuated, b.group(j) + 3)
                    nc.scalar.activation(HID[:, bass.ds(b.n(NF, 0), NF), 0], evB, ACT.Copy
                                         ).then_inc(S("hidden_hi"), 1)

            def up_gelu(b, j, u):
                if (j, u) == (1, 0):
                    act.wait_ge(evacuated, b.group(0) + 3)
                    nc.scalar.activation(evA, evA, ACT.Gelu_apprx_tanh).then_inc(S("gate_gelu"), 1)

            stream_act(act, "up", up_evac, up_gelu)
            stream_act(act, "down", copy_act(act, "down", OUT2, OSQ2))
            act.wait_ge(S("p_turned"), 1)
            nc.scalar.activation(PTR.rearrange("p a n -> p (a n)"), PS[:, 5, :], ACT.Copy).then_inc(S("p_copied"), 1)
            act.wait_ge(S("p_copied"), 1)
            nc.scalar.activation(PSP[:, :, 0], PTR, ACT.Copy).then_inc(S("p_hi"), 1)
            std_act(act, "ffn_post")
            stream_act(act, "ple", copy_act(act, "ple", PLE),
                       lambda b, j, u: squares_act(act, "ple_pre", H, added="ffn_post", quarters=[j]))
            pre_act(act, "ple_pre", XS)

            def gate_evac(b, j, k):
                group_used(act, b, k)
                act.wait_ge(evacuated, b.group(j) + 2)
                nc.scalar.activation(evA, acc(b.set(j)), ACT.Sigmoid).then_inc(S("gate_ready"), 1)
                act.wait_ge(evacuated, b.group(j) + 3)
                at = bass.ds(b.local(j) * NF, NF)
                nc.scalar.activation(OSQ3[:, at], OUT3[:, at], ACT.Square).then_inc(norm_sq, 1)

            stream_act(act, "gate", gate_evac)
            std_act(act, "ple_post")

            for half in range(2):
                act.wait_ge(S("ctx_turned"), half + 1)
                nc.scalar.activation(CTX[:, 8 * half:8 * half + 8],
                                     PS[:, 4 * half:4 * half + 4, :].rearrange("p b (h n) -> p (b h) n", h=2),
                                     ACT.Copy).then_inc(S("ctx_loaded"), 1)
            squares_act(act, "norm1", H, added="ple_post")
            act.wait_ge(S("ctx_loaded"), 2)
            squares_act(act, "norm_c", CTX, sq=CTX_SQ, quarters=(0, 1))
            std_act(act, "norm1")
            squares_act(act, "norm_c", CTX, sq=CTX_SQ, quarters=(2, 3))
            std_act(act, "norm_c", 5, L)
            for i, (q, v) in enumerate(PAIRED):
                act.wait_ge(norm_z, so_far("norm1", "z", 4 * i + 4))
                for t in range(4 * q, 4 * q + 4):
                    ins = nc.scalar.activation((XS, CS)[v][:, t, 0], (Z, CTX)[v][:, t], ACT.Identity,
                                               bias=MADA[:, t, v:v + 1])
                ins.then_inc(norm_hi, 1)

            def kv_evac(b, j, k):
                group_used(act, b, k)
                nc.scalar.activation(KV[:, bass.ds(b.local(j) * NF + 2, 2)], PS[:, 2:4, :],
                                     ACT.Copy).then_inc(S("kv_half"), 1)

            def qk_square(i):
                x, n, _, kind, _ = HEADS[i]
                if kind == "v":
                    return
                m = QK_BEFORE[i]
                heads_landed(act, i)
                if m >= 2:
                    act.wait_ge(S("heads_pe"), QK_ITEM[m - 2] + 1)
                nc.scalar.activation(QK_SQ[:, m % 2, 0:n], x, ACT.Square).then_inc(S("qk_sq"), 1)

            def head_out(i):
                x, n, _, kind, _ = HEADS[i]
                act.wait_ge(S("heads_pe"), i + 1)
                if kind == "v":
                    nc.scalar.activation(x, PS[:, 4 + i % 2, :], ACT.Copy).then_inc(S("heads_act"), 1)
                    return
                m = QK_BEFORE[i]
                if m >= 2:
                    act.wait_ge(S("qk_normed"), m - 1)
                nc.scalar.activation(QK_ST[:, m % 2, 0:n], PS[:, 4 + i % 2, 0:n], ACT.Sqrt, bias=SM[:, 0:1],
                                     scale=1.0 / (128 if kind == "a" else 64)).then_inc(S("heads_act"), 1)

            late, tail = beside(per_head([(3, head_out), (0, qk_square)]), "kv", HEADS_END)
            stream_act(act, "kv", kv_evac, late, evac_first=True)
            stream_act(act, "q", copy_act(act, "q", Q), late)
            tail()

            def exps(rd):
                for n in JOBS[rd]:
                    act.wait_ge(S("max_ready"), n + 1)
                    if rd >= 2:
                        act.wait_ge(S("p_turn"), rd - 1)
                    nc.scalar.activation(PR[:, n % 4], PS[:, 2 + n % 4, :], ACT.Exp, bias=NEGMAX[:, n:n + 1],
                                         accum_out=SUMS[:, n:n + 1]).then_inc(S("exp_ready"), 1)

            exps(0)
            for rd, (_, h, qb) in enumerate(ROUNDS):
                if rd + 1 < len(ROUNDS):
                    exps(rd + 1)
                act.wait_ge(S("p_turn"), rd + 1)
                if rd >= 4:
                    act.wait_ge(S("pv_done"), rd // 2 - 1)
                nc.scalar.activation(PTT[:, (rd // 2) % 2, :, qb * P:(qb + 1) * P],
                                     PS[:, 6 + rd % 2, :].rearrange("p (c q) -> p c q", c=4),
                                     ACT.Copy).then_inc(S("pt_ready"), 1)
            act.wait_ge(S("o_ready"), 24)
            for q in range(2):
                nc.scalar.activation(SUBSQ[:, 4 * q:4 * q + 4], Q[:, 16 + 4 * q:20 + 4 * q],
                                     ACT.Square).then_inc(S("sub_sq"), 1)
            act.wait_ge(S("sub_stat"), 1)
            nc.scalar.activation(SUB_ROOT, PS[:, 2, 0:16], ACT.Sqrt, bias=SM[:, 0:1],
                                 scale=1.0 / P).then_inc(S("sub_std"), 1)
            for q in range(6):
                if q == 4:
                    act.wait_ge(S("o_normed"), 8)
                nc.scalar.activation(OS[:, 4 * q:4 * q + 4, 0], Q[:, 4 * q:4 * q + 4],
                                     ACT.Copy).then_inc(S("o_hi"), 1)

            def branch_evac(b, j, k):
                if j % 2 == 0:
                    group_used(act, b, k)
                    act.wait_ge(evacuated, b.group(j) + 2)
                    nc.scalar.activation(evA, acc(b.set(j)), ACT.Sigmoid).then_inc(S("branch_gate"), 1)

            stream_act(act, "branch", branch_evac)
            act.wait_ge(S("merged"), 4)
            for q in range(4):
                nc.scalar.activation(XS[:, 4 * q:4 * q + 4, 0], MG[:, 4 * q:4 * q + 4],
                                     ACT.Copy).then_inc(S("merged_hi"), 1)

            def out2_evac(b, j, k):
                act.wait_ge(evacuated, b.group(j) + 3)
                at = bass.ds(b.local(j) * NF, NF)
                nc.scalar.activation(SQ[:, at], H[:, at], ACT.Square).then_inc(norm_sq, 1)

            stream_act(act, "out2", out2_evac)
            pre_act(act, "norm2", XS, shift=lambda t: MADA[:, 3 * KT + t, 0:1])

            def up2_evac(b, j, k):
                if j == 0:
                    group_used(act, b, k)
                    act.wait_ge(evacuated, b.group(j) + 2)
                    nc.scalar.activation(evA, acc(b.set(j)), ACT.Silu).then_inc(S("gate2_silu"), 1)
                else:
                    act.wait_ge(evacuated, b.group(j) + 3)
                    nc.scalar.activation(HID[:, bass.ds(b.n(NF, 0), NF), 0], evB, ACT.Copy
                                         ).then_inc(S("hidden2_hi"), 1)

            stream_act(act, "up2", up2_evac)
            stream_act(act, "down2", lambda b, j, k: None)
            act.wait_ge(S("out_turned"), 2)
            nc.scalar.activation(ONAT[:, 1, :], PS[:, 4:8, :].rearrange("p b n -> p (b n)"),
                                 ACT.Copy).then_inc(S("out_copied_act"), 1)

        @block.vector
        def _(dve):
            ch = Chain(dve, S("dve_chain"))
            dve.sem_inc(w_split, RING)
            dve.sem_inc(evacuated, 2)
            dve.sem_inc(ada_evacuated, 1)
            dve.sem_inc(S("kv_half"), 1)
            nc.vector.memset(SM[:, 0:1], EPS).then_inc(S("eps_ready"), 1)
            dve.wait_ge(S("x_turned"), 1)
            nc.vector.tensor_copy(H[:, 0:8], PS[:, 0:4, :].rearrange("p b (h n) -> p (b h) n", h=2)
                                  ).then_inc(S("h_loaded_dve"), 1)
            all_params(dve)
            nc.vector.tensor_copy(DROW[0:8].rearrange("p (e c) -> p e c", e=2),
                                  DPAIR[0:8].rearrange("p (e o) -> p e o", o=1).to_broadcast([8, 2, 64])
                                  ).then_inc(S("d_rows"), 1)
            for n in range(RING):
                dve.wait_ge(w_rounded, n + 1)
                nc.vector.tensor_tensor(w_lo[:, n], raw[:, n], r(w_hi[:, n]), ALU.subtract).then_inc(w_split, 1)
            dve.wait_ge(S("params_pe"), 1)
            for i, n in enumerate(PARAM_USED):
                nc.vector.tensor_copy(PRM[:, i, 0:n], PS[:, i // 4, (i % 4) * P:(i % 4) * P + n])
            nc.vector.tensor_copy(PRM[:, 1, 88:96], PS[:, 1, P:P + 8]).then_inc(S("params_turned"), 1)
            dve.wait_ge(S("params_turned"), 1)
            dve.wait_ge(S("h_loaded_act"), 1)
            dve.wait_ge(S("h_loaded_dve"), 1)
            pre_dve(dve, ch, "mix_pre", H, lambda t: prm("mix_pre", t), XS)

            def lambda_sums(_):
                for i in range(2):
                    ch.mark(nc.vector.tensor_tensor_reduce(
                        SM[:, 320:384], EV[:, 0, 0, 128 * i:128 * i + 64], EV[:, 0, 0, 128 * i + 64:128 * i + 128],
                        1.0, 0.0, ALU.mult, ALU.add, SM[:, 1 + i:2 + i]))
                    ch.wait()
                dve.sem_inc(S("lam_sums"), 1)
                for i, (name, g) in enumerate((("q_norm_a", P ** -0.5), ("q_norm_b", 64 ** -0.5),
                                               ("subln", 1 - LAM_INIT))):
                    nc.vector.tensor_scalar(SM[:, 4 + i:5 + i], prm(name), g, None, ALU.mult)

            def minus_lambda(_):
                dve.wait_ge(S("lam_exp"), 1)
                ch.mark(nc.vector.tensor_tensor(SM[:, 3:4], SM[:, 2:3], SM[:, 1:2], ALU.subtract))
                ch.wait()
                ch.mark(nc.vector.tensor_scalar(SM[:, 3:4], SM[:, 3:4], -LAM_INIT, None, ALU.add))

            dx = SM[:, 128:192]
            dtv = SM[:, 448:512]
            da = SM[:, 256:320]

            def c32(ap):
                return ap.rearrange("p (c h) -> p c h", c=2)

            def over_chunks(ap):
                return ap.rearrange("p (o h) -> p o h", o=1).to_broadcast([P, 2, 32])

            def conv(x, out, taps, weight, first):
                half = taps // 2
                others = [j for j in range(taps) if j != half]
                for j in others:
                    off = j - half
                    for f in range(NF):
                        if j == others[0]:
                            dve.wait_ge(S("first_tap"), first(f | 1))
                        else:
                            ch.wait(ch.n - NF + 1 if j != others[-1] else ch.n - NF + 1 + f)
                        a, z = max(0, -off), L - max(0, off)
                        ins = nc.vector.scalar_tensor_tensor(out(f)[:, a:z], x(f)[:, a + off:z + off],
                                                             weight(j, f), out(f)[:, a:z], ALU.mult, ALU.add)
                        if j != others[-1]:
                            ch.mark(ins)
                ins.then_inc(evacuated, 1)

            nac = SM[:, 320:384]
            off = SM[:, 384:416]

            def in_evac(b, j, k):
                if j < 3:
                    t0 = X_TILE[j]
                    conv(lambda f: accf(b.set(j), f), lambda f: XBC[:, t0 + f], 5,
                         lambda tap, f: prm("ssd_conv_w", 12 * tap + t0 + f), lambda f: 4 * j + f + 1)
                elif j < 5:
                    dve.wait_ge(S("u_ready"), j - 2)
                    dve.sem_inc(evacuated, 1)
                else:
                    dve.wait_ge(S("z_ready"), j - 4)
                    dve.sem_inc(evacuated, 1)

            def dt_bias(_):
                dve.wait_ge(S("dt_projected"), 1)
                nc.vector.tensor_tensor(c32(dx), c32(PS[:, 5, 0:64]), over_chunks(SM[:, 32:64]),
                                        ALU.add).then_inc(S("dt_biased"), 1)
                nc.vector.memset(UP[:, :, 0:8], 0.0)
                nc.vector.memset(UP[:, :, 8 + L:UPW], 0.0).then_inc(S("u_padded"), 1)

            def dt_plus_one(_):
                dve.wait_ge(S("dt_exp"), 1)
                nc.vector.tensor_scalar(SM[:, 256:320], SM[:, 192:256], 1.0, None,
                                        ALU.add).then_inc(S("dt_plus_one"), 1)

            def dt_done(_):
                dve.wait_ge(S("dt_ln"), 1)
                dve.wait_ge(S("dt_plus_one"), 1)
                e, ln, um1, is0, den = SM[:, 192:256], SM[:, 320:384], SM[:, 384:448], ST[:, 0:64], ST[:, 64:128]
                for ins in (lambda: nc.vector.tensor_scalar(um1, SM[:, 256:320], -1.0, None, ALU.add),
                            lambda: nc.vector.tensor_scalar(is0, um1, 0.0, None, ALU.is_equal),
                            lambda: nc.vector.tensor_tensor(den, um1, is0, ALU.add),
                            lambda: nc.vector.reciprocal(den, den),
                            lambda: nc.vector.tensor_tensor(ln, ln, e, ALU.mult),
                            lambda: nc.vector.tensor_tensor(ln, ln, den, ALU.mult),
                            lambda: nc.vector.tensor_tensor(is0, is0, e, ALU.mult),
                            lambda: nc.vector.tensor_tensor(ln, ln, is0, ALU.add),
                            lambda: nc.vector.scalar_tensor_tensor(dtv, dx, 0.0, ln, ALU.max, ALU.add)):
                    ch.mark(ins())
                    ch.wait()
                nc.vector.scalar_tensor_tensor(c32(da), c32(dtv), -1.0, over_chunks(SM[:, 64:96]),
                                               ALU.mult, ALU.mult).then_inc(S("da_ready"), 1)

            def masked_cb(g):
                dve.wait_ge(S("cb_done"), 1)
                cb = PS[:, 4 if g == 0 else 7, :].rearrange("p (c l) -> p c l", c=2)
                for d, mask in enumerate(("upto", "from")):
                    nc.vector.tensor_tensor(CBM[:, g, d, 0], cb[:, 0, 0:P], const(mask), ALU.mult)
                    nc.vector.tensor_copy(CBM[:, g, d, 1], cb[:, 0, P:L] if d == 0 else cb[:, 1, 0:P])
                    ins = nc.vector.tensor_tensor(CBM[:, g, d, 2], cb[:, 1, P:L], const(mask), ALU.mult)
                ins.then_inc(S("cbm_ready"), 1)

            def acum_columns(_):
                dve.wait_ge(S("acum_done"), 1)
                ch.mark(nc.vector.tensor_scalar(nac, PS[:, 5, 64:128], -1.0, None, ALU.mult))
                ch.wait()
                nc.vector.tensor_tensor(off[:, 0:16], PS[:, 5, 128:144], c32(nac)[:, 0, 0:16], ALU.add)
                nc.vector.tensor_tensor(off[:, 16:32], PS[:, 5, 144:160], c32(nac)[:, 1, 16:32],
                                        ALU.add).then_inc(S("acum_columns"), 1)

            def times_dt(arg):
                half, c = arg
                dve.wait_ge(S("xs_turned"), 2 * half + c + 1)
                for d in range(2):
                    h = 16 * d + 8 * half
                    ins = nc.vector.tensor_tensor(
                        XDT[:, d, c, 8 * half:8 * half + 8],
                        PS[:, turn_bank(half, c), :].rearrange("p (h n) -> p h n", n=64),
                        c32(dtv)[:, c, h:h + 8].rearrange("p (h o) -> p h o", o=1).to_broadcast([P, 8, 64]),
                        ALU.mult)
                ins.then_inc(S("xdt_ready"), 1)

            def exponents(m):
                t, e = m // 2, m % 2
                dve.wait_ge(S("between_ready"), m + 1)
                for d in range(2):
                    h = 16 * d + 2 * t + e
                    row = PS[:, 4 + m % 2, d * L:d * L + L]
                    for c in range(2):
                        ins = nc.vector.tensor_scalar(ER[:, m % 2, d, 2 * c], row[:, c * P:c * P + P],
                                                      nac[:, 32 * c + h:32 * c + h + 1], 0.0, ALU.add, ALU.min)
                ins.then_inc(S("exponent_ready"), 1)

            def mix_matrix(m):
                dve.wait_ge(S("decay_ready"), m + 1)
                dve.wait_ge(S("cbm_ready"), 2)
                for n in (2 * m, 2 * m + 1):
                    t, e, d = SSD_STEPS[n]
                    if n >= 3:
                        dve.wait_ge(S("y_product"), n - 2)
                    nc.vector.tensor_tensor(MR[n % 3], ER[:, m % 2, d].rearrange("p b l -> p (b l)"),
                                            CBM[:, t // 4, d].rearrange("p b l -> p (b l)"),
                                            ALU.mult).then_inc(S("mix_matrix"), 1)

            def y_out(t):
                dve.wait_ge(S("y_product"), 4 * t + 4)
                nc.vector.scalar_tensor_tensor(Y[:, t], XBC[:, t], prm("ssd_d", t), PS[:, 6 + t % 2, 0:L],
                                               ALU.mult, ALU.add).then_inc(S("y_out"), 1)

            def gate_y(g):
                dve.wait_ge(S("y_out"), 4 * g + 4)
                dve.wait_ge(S("z_ready"), g + 1)
                nc.vector.tensor_tensor(Y[:, 4 * g:4 * g + 4], Y[:, 4 * g:4 * g + 4], SZ[:, 4 * g:4 * g + 4],
                                        ALU.mult).then_inc(S("y_gated"), 1)

            def pooled(g):
                u = UP[:, 2 * g:2 * g + 2]
                dve.wait_ge(S("u_ready"), g // 2 + 1)
                dve.wait_ge(S("u_padded"), 1)

                def window(dst, src, reach, a, z):
                    ch.mark(nc.vector.tensor_tensor(dst[:, :, a:z], src[:, :, a - reach[0]:z - reach[0]],
                                                    src[:, :, a + reach[1]:z + reach[1]], ALU.add))
                    ch.wait()
                    return dst

                w = window(SA, u, (1, 0), 1, UPW)
                if g >= 1:
                    w = window(SB, SA, (1, 1), 2, UPW - 1)
                if g >= 2:
                    w = window(SA, SB, (2, 2), 4, UPW - 3)
                if g >= 3:
                    w = window(SB, SA, (4, 4), 8, UPW - 7)
                if g == 0:
                    dve.wait_ge(S("inv_landed"), 64)
                m = MIXED[:, 2 * g:2 * g + 2]
                ch.mark(nc.vector.tensor_tensor(m, w[:, :, 8:8 + L], INV[:, g:g + 1].to_broadcast([P, 2, L]),
                                                ALU.mult))
                ch.wait()
                nc.vector.tensor_tensor(m, m, u[:, :, 8:8 + L], ALU.subtract).then_inc(S("mixed_ready"), 1)

            def y_recip(g):
                dve.wait_ge(S("y_std"), g + 1)
                ch.mark(nc.vector.reciprocal(ST[:, g * L:g * L + L], ST[:, g * L:g * L + L]))

            def y_norm(g):
                ch.wait()
                for t in range(4 * g, 4 * g + 4):
                    nc.vector.scalar_tensor_tensor(Y[:, t], Y[:, t], prm("ssd_norm", t), ST[:, g * L:g * L + L],
                                                   ALU.mult, ALU.mult).then_inc(S("y_normed"), 1)

            def mix_lo(arg):
                i, q = arg
                dve.wait_ge(S("mix_hi"), i + 1)
                nc.vector.tensor_tensor(XS[:, 4 * q:4 * q + 4, 1], Y[:, 4 * q:4 * q + 4],
                                        r(XS[:, 4 * q:4 * q + 4, 0]), ALU.subtract).then_inc(S("mix_split"), 1)

            late, tail = beside(
                [(1, lambda_sums, None), (3, minus_lambda, None), (4, dt_bias, None), (6, dt_plus_one, None),
                 (10, dt_done, None), (13, masked_cb, 0),
                 (14, masked_cb, 1), (14, acum_columns, None)] +
                [(at + 1, times_dt, x) for x, at in TURN_AT.items()] +
                [(at + 4, mix_matrix, m) for m, at in enumerate(PAIR_AT)] +
                [(at + 2, exponents, m) for m, at in enumerate(PAIR_AT)] +
                [(STEP_AT[4 * t + 3] + 6, y_out, t) for t in range(8)] +
                [(at, pooled, g) for g, at in enumerate((33, 35, 41, 43))] +
                [(51, gate_y, 0), (57, mix_lo, (0, 2)), (58, gate_y, 1), (58, mix_lo, (1, 3)), (59, y_recip, 0),
                 (59, y_norm, 0), (60, mix_lo, (2, 0)), (61, y_recip, 1), (61, y_norm, 1), (62, mix_lo, (3, 1))],
                "in", IN_END)
            stream_dve(dve, "in", in_evac, late)
            tail()

            dve.wait_ge(S("conditions_ready"), 1)
            stream_dve(dve, "out", copied_dve(dve, "out"))
            all_evacuated(dve, "out")
            post_dve(dve, ch, "mix_post", OUT1, "mix_post")
            dve.wait_ge(norm_added, so_far("mix_post", "added", 4))
            pre_dve(dve, ch, "ffn_pre", H, lambda t: prm("ffn_pre", t), XS)

            def up_evac(b, j, k):
                if j == 0:
                    ch.start(b, 4)
                    w = ["ffn_w0", "ffn_w1", "ffn_w2"]
                    conv(lambda f: accf(b.set(j), f), lambda f: evA[:, f], 3,
                         lambda tap, f: prm_dyn(w[tap], b.n(NF, f)), lambda f: b.n(NF, IN_TAPS + f + 1))
                    ch.end(b)
                else:
                    group_used(dve, b, k)
                    dve.wait_ge(S("gate_gelu"), b.n(1, 1))
                    nc.vector.tensor_tensor(evB, acc(b.set(j)), evA, ALU.mult).then_inc(evacuated, 1)
                    dve.wait_ge(S("hidden_hi"), b.n(1, 1))
                    dve.wait_ge(evacuated, b.group(j) + 3)
                    at = bass.ds(b.n(NF, 0), NF)
                    nc.vector.tensor_tensor(HID[:, at, 1], evB, r(HID[:, at, 0]), ALU.subtract
                                            ).then_inc(S("hidden_split"), 1)

            stream_dve(dve, "up", up_evac)
            stream_dve(dve, "down", copied_dve(dve, "down"))
            all_evacuated(dve, "down")
            dve.wait_ge(S("p_hi"), 1)
            nc.vector.tensor_tensor(PSP[:, :, 1], PTR, r(PSP[:, :, 0]), ALU.subtract).then_inc(S("p_split"), 1)
            post_dve(dve, ch, "ffn_post", OUT2, "ffn_post")
            stream_dve(dve, "ple", copied_dve(dve, "ple"))
            dve.wait_ge(norm_added, so_far("ffn_post", "added", 4))
            pre_dve(dve, ch, "ple_pre", H, lambda t: prm("ple_pre", t), XS)

            def gate_evac(b, j, k):
                dve.wait_ge(S("gate_ready"), b.local(j) + 1)
                at = bass.ds(b.local(j) * NF, NF)
                nc.vector.tensor_tensor(OUT3[:, at], evA, PLE[:, at], ALU.mult).then_inc(evacuated, 1)

            all_evacuated(dve, "ple")
            stream_dve(dve, "gate", gate_evac)
            all_evacuated(dve, "gate")
            post_dve(dve, ch, "ple_post", OUT3, "ple_post")

            def ada_bias(t0, t1, v):
                ch.mark(nc.vector.tensor_tensor(MADA[:, t0:t1, v], MADA[:, t0:t1, v],
                                                prm("b_ada", t0, t1 - t0), ALU.add))

            def gain_eff(i, m, v, name):
                ch.mark(nc.vector.scalar_tensor_tensor(GE[:, i], MADA[:, m * KT:(m + 1) * KT, v], 1.0,
                                                       prm(name, 0, KT), ALU.add, ALU.mult))

            def ada_done(name):
                ph = PHASES[name]
                dve.wait_ge(ada_evacuated, 1 + ph.ada0 + ph.ada * ph.times)

            ada_done("gate")
            ada_bias(0, 2 * KT, 0)
            ada_bias(0, 2 * KT, 1)
            ch.wait()
            gain_eff(0, 1, 0, "norm1")
            gain_eff(1, 1, 1, "norm1")
            ch.wait()

            def paired_scaled(i):
                q, v = PAIRED[i]
                for t in range(4 * q, 4 * q + 4):
                    nc.vector.scalar_tensor_tensor((Z, CTX)[v][:, t], (H, CTX)[v][:, t], GE[:, v, t:t + 1],
                                                   ST[:, v * L:v * L + L], ALU.mult, ALU.mult).then_inc(norm_z, 1)

            def paired_rest(i):
                q, v = PAIRED[i]
                dve.wait_ge(norm_hi, so_far("norm1", "hi", i + 1))
                dve.wait_ge(norm_z, so_far("norm1", "z", 4 * i + 4))
                for t in range(4 * q, 4 * q + 4):
                    ins = nc.vector.scalar_tensor_tensor((XS, CS)[v][:, t, 1], (Z, CTX)[v][:, t], MADA[:, t, v:v + 1],
                                                         r((XS, CS)[v][:, t, 0]), ALU.add, ALU.subtract)
                ins.then_inc(norm_ready, 1)

            dve.wait_ge(norm_added, so_far("ple_post", "added", 4))
            rstd_dve(dve, ch, "norm1")
            paired_scaled(0)
            rstd_dve(dve, ch, "norm_c", L)
            for i in range(len(PAIRED)):
                if i + 1 < len(PAIRED):
                    paired_scaled(i + 1)
                paired_rest(i)

            def kv_evac(b, j, k):
                group_used(dve, b, k)
                nc.vector.tensor_copy(KV[:, bass.ds(b.local(j) * NF, 2)], PS[:, 0:2, :]
                                      ).then_inc(evacuated, 1)

            gains = {"k_norm_a": prm("k_norm_a"), "k_norm_b": prm("k_norm_b"), "q_norm_a": SM[:, 4:5],
                     "q_norm_b": SM[:, 5:6]}

            def qk_norm(i):
                x, n, g, kind, _ = HEADS[i]
                if kind == "v":
                    return
                root = QK_ST[:, QK_BEFORE[i] % 2, 0:n]
                dve.wait_ge(S("heads_act"), i + 1)
                ch.mark(nc.vector.reciprocal(root, root))
                ch.wait()
                nc.vector.scalar_tensor_tensor(x, x, gains[g], root, ALU.mult, ALU.mult).then_inc(S("qk_normed"), 1)

            def qk_rope(i):
                x, _, _, kind, _ = HEADS[i]
                if kind == "v":
                    return
                m = QK_BEFORE[i]
                t1, t2 = QK_T[:, 2 * (m % 2)], QK_T[:, 2 * (m % 2) + 1]
                dve.wait_ge(S("qk_normed"), m + 1)
                nc.vector.tensor_tensor(t1, x[:, 0:L], const("cos_" + kind), ALU.mult)
                dve.wait_ge(S("qk_turned"), m + 1)
                ch.mark(nc.vector.tensor_tensor(t2, PS[:, 6 + m % 2, 0:L], const("sin_" + kind), ALU.mult))
                ch.wait()
                nc.vector.tensor_tensor(x[:, 0:L], t1, t2, ALU.add).then_inc(S("qk_roped"), 1)

            late, tail = beside(per_head([(7, qk_rope), (4, qk_norm)]), "kv", HEADS_END)
            stream_dve(dve, "kv", kv_evac, late, evac_first=True)
            stream_dve(dve, "q", copied_dve(dve, "q"), late)
            tail()

            def maxima(rd):
                for n in JOBS[rd]:
                    dve.wait_ge(S("scores_ready"), n + 1)
                    nc.vector.tensor_reduce(NEGMAX[:, n:n + 1], PS[:, 2 + n % 4, :], AX.X, ALU.max,
                                            negate=True).then_inc(S("max_ready"), 1)

            def probabilities(rd):
                js = JOBS[rd]
                dve.wait_ge(S("exp_ready"), js[-1] + 1)
                ch.mark(nc.vector.reciprocal(RSUM[:, js[0]:js[-1] + 1], SUMS[:, js[0]:js[-1] + 1]))
                ch.wait()
                p0 = PR[:, js[0] % 4]
                ins = nc.vector.tensor_scalar(p0, p0, RSUM[:, js[0]:js[0] + 1], None, ALU.mult)
                if len(js) == 2:
                    ch.mark(ins)
                    n = js[1]
                    ch.mark(nc.vector.tensor_tensor(RSUM[:, n:n + 1], RSUM[:, n:n + 1], SM[:, 3:4], ALU.mult))
                    ch.wait()
                    ins = nc.vector.scalar_tensor_tensor(p0, PR[:, n % 4], RSUM[:, n:n + 1], p0, ALU.mult, ALU.add)
                ins.then_inc(S("p_ready"), 1)

            def output(hd):
                dve.wait_ge(S("pv_done"), hd + 1)
                nc.vector.tensor_copy(Q[:, hd], PS[:, hd % 2, 0:L]).then_inc(S("o_ready"), 1)

            maxima(0)
            for rd in range(len(ROUNDS)):
                if rd + 1 < len(ROUNDS):
                    maxima(rd + 1)
                probabilities(rd)
                if rd % 2 == 1 and rd >= 3:
                    output(rd // 2 - 1)
            output(23)
            dve.wait_ge(S("sub_std"), 1)
            nc.vector.reciprocal(SUB_ROOT, SUB_ROOT).then_inc(S("sub_recip"), 1)
            dve.wait_ge(S("o_ready"), 24)
            dve.wait_ge(S("sub_spread"), 1)
            for i in range(8):
                nc.vector.scalar_tensor_tensor(Q[:, 16 + i], Q[:, 16 + i], SM[:, 6:7],
                                               PS[:, 4 + i // 2, (i % 2) * L:(i % 2) * L + L], ALU.mult,
                                               ALU.mult).then_inc(S("o_normed"), 1)
            for q in range(6):
                dve.wait_ge(S("o_hi"), q + 1)
                nc.vector.tensor_tensor(OS[:, 4 * q:4 * q + 4, 1], Q[:, 4 * q:4 * q + 4],
                                        r(OS[:, 4 * q:4 * q + 4, 0]), ALU.subtract).then_inc(S("o_split"), 1)

            def branch_evac(b, j, k):
                at = bass.ds(b.n(NF, 0), NF)
                if j % 2 == 0:
                    dve.wait_ge(S("branch_gate"), b.n(2, 1 + j // 2))
                    dve.sem_inc(evacuated, 1)
                elif j == 1:
                    group_used(dve, b, k)
                    nc.vector.tensor_tensor(MG[:, at], acc(b.set(j)), evA, ALU.mult).then_inc(evacuated, 1)
                else:
                    group_used(dve, b, k)
                    nc.vector.tensor_tensor(evB, acc(b.set(j)), evA, ALU.mult).then_inc(evacuated, 1)
                    dve.wait_ge(evacuated, b.group(j) + 3)
                    nc.vector.tensor_tensor(MG[:, at], MG[:, at], evB, ALU.add).then_inc(S("merged"), 1)

            stream_dve(dve, "branch", branch_evac)
            ada_done("branch")
            ada_bias(2 * KT, 6 * KT, 0)
            ch.wait()
            gain_eff(2, 4, 0, "norm2")
            ch.wait()
            dve.wait_ge(S("merged"), 4)
            for q in range(4):
                dve.wait_ge(S("merged_hi"), q + 1)
                nc.vector.tensor_tensor(XS[:, 4 * q:4 * q + 4, 1], MG[:, 4 * q:4 * q + 4],
                                        r(XS[:, 4 * q:4 * q + 4, 0]), ALU.subtract).then_inc(S("merged_split"), 1)

            def gated_residual(m):
                def evac(b, j, k):
                    group_used(dve, b, k)
                    for f in range(NF):
                        t = bass.ds(b.local(j) * NF + f, 1)
                        h = H[:, t].rearrange("p o n -> p (o n)")
                        ins = nc.vector.scalar_tensor_tensor(
                            h, accf(b.set(j), f), MADA[:, bass.ds(b.local(j) * NF + (m * KT + f), 1), 0], h,
                            ALU.mult, ALU.add)
                    ins.then_inc(evacuated, 1)
                return evac

            stream_dve(dve, "out2", gated_residual(2))
            all_evacuated(dve, "out2")
            pre_dve(dve, ch, "norm2", H, lambda t: GE[:, 2, t:t + 1], XS, shift=lambda t: MADA[:, 3 * KT + t, 0:1])

            def up2_evac(b, j, k):
                if j == 0:
                    dve.wait_ge(S("gate2_silu"), b.n(1, 1))
                    dve.sem_inc(evacuated, 1)
                else:
                    group_used(dve, b, k)
                    nc.vector.tensor_tensor(evB, acc(b.set(j)), evA, ALU.mult).then_inc(evacuated, 1)
                    dve.wait_ge(S("hidden2_hi"), b.n(1, 1))
                    dve.wait_ge(evacuated, b.group(j) + 3)
                    at = bass.ds(b.n(NF, 0), NF)
                    nc.vector.tensor_tensor(HID[:, at, 1], evB, r(HID[:, at, 0]), ALU.subtract
                                            ).then_inc(S("hidden2_split"), 1)

            stream_dve(dve, "up2", up2_evac)
            stream_dve(dve, "down2", gated_residual(5))
            dve.wait_ge(S("out_turned"), 1)
            nc.vector.tensor_copy(ONAT[:, 0, :], PS[:, 0:4, :].rearrange("p b n -> p (b n)")
                                  ).then_inc(S("out_copied_dve"), 1)

        @block.tensor
        def _(pe):
            pe.sem_inc(w_used, RING)
            ident = const("ident")
            pe.wait_ge(S("consts_landed"), 16)
            def normed(tag):
                return lambda q: pe.wait_ge(norm_ready, so_far(tag, "ready", q + 1))

            def turn(src, done):
                for t in range(KT):
                    for c in range(2):
                        ins = nc.tensor.transpose(PS[:, t // 2, (t % 2) * L + c * P:(t % 2) * L + c * P + P],
                                                  src[:, c, t * P:t * P + P], ident)
                    if t % 8 == 7:
                        ins.then_inc(S(done), 1)

            pe.wait_ge(S("x_landed"), 32)
            turn(XNAT, "x_turned")
            pe.wait_ge(S("h_loaded_act"), 1)
            pe.wait_ge(S("h_loaded_dve"), 1)
            stat_pe(pe, "mix_pre", SQ, 4)
            all_params(pe)
            for i, n in enumerate(PARAM_USED):
                nc.tensor.transpose(PS[:, i // 4, (i % 4) * P:(i % 4) * P + n], PROW[0:n, i, :], ident[0:n, 0:n])
            pe.wait_ge(S("d_rows"), 1)
            nc.tensor.transpose(PS[:, 1, P:P + 8], DROW[0:8], ident[0:8, 0:8]).then_inc(S("params_pe"), 1)
            pe.wait_ge(S("params_turned"), 1)
            def dt_product(_):
                pe.wait_ge(S("wdt_landed"), 16)
                pe.wait_ge(norm_z, so_far("mix_pre", "z", 16))
                for c in range(2):
                    for t in range(KT):
                        mm = nc.tensor.matmul(PS[:, 5, 32 * c:32 * c + 32], Z[:, t, c * P:c * P + P], WDT[:, t],
                                              start=c == 0 and t == 0, stop=t == KT - 1, skip_group_check=True)
                mm.then_inc(S("dt_projected"), 1)

            def cb_product(_):
                pe.wait_ge(S("xbc_ready"), 1)
                for g in range(2):
                    for c in range(2):
                        mm = nc.tensor.matmul(PS[:, 4 if g == 0 else 7, c * L:c * L + L],
                                              XBC[:, 8 + g, c * P:c * P + P], XBC[:, 10 + g], start=c == 0, stop=True,
                                              skip_group_check=True)
                mm.then_inc(S("cb_done"), 1)

            def cumulate(_):
                da = SM[:, 256:320].rearrange("p (c h) -> p c h", c=2)
                pe.wait_ge(S("da_ready"), 1)
                for c in range(2):
                    for d, tri in enumerate(("upto", "from")):
                        nc.tensor.matmul(PS[:, 5, 64 + 32 * c + 16 * d:80 + 32 * c + 16 * d], const(tri),
                                         da[:, c, 16 * d:16 * d + 16], start=c == 0 and d == 0, stop=True,
                                         skip_group_check=True)
                for d in range(2):
                    nc.tensor.matmul(PS[:, 5, 128 + 16 * d:144 + 16 * d], const("ones"), da[:, d, 16 * d:16 * d + 16],
                                     start=False, stop=True, skip_group_check=True)
                for d, tri in enumerate(("upto", "from")):
                    for c in range(2):
                        mm = nc.tensor.matmul(PS[0:32, 6, d * L + c * P:d * L + c * P + P], da[:, c], const(tri),
                                              start=c == 0 and d == 0, stop=True, skip_group_check=True)
                mm.then_inc(S("acum_done"), 1)

            def x_turn(arg):
                half, c = arg
                pe.wait_ge(S("xbc_ready"), 2 + half)
                if half == 0 and c == 0:
                    pe.wait_ge(S("acum_columns"), 1)
                else:
                    pe.wait_ge(S("exponent_ready"), 1 if half == 0 else 5 + c)
                for t in range(4):
                    ins = nc.tensor.transpose(PS[:, turn_bank(half, c), t * P:t * P + P],
                                              XBC[:, 4 * half + t, c * P:c * P + P], ident)
                ins.then_inc(S("xs_turned"), 1)

            def rows(m):
                t, e = m // 2, m % 2
                pe.wait_ge(S("acum_rows"), 1)
                if m == 0:
                    pe.wait_ge(S("cbm_ready"), 1)
                elif m in (1, 2):
                    pe.wait_ge(S("xdt_ready"), m)
                elif m in (6, 7):
                    pe.wait_ge(S("xdt_ready"), m - 3)
                else:
                    pe.wait_ge(S("exponent_ready"), m - 1)
                for d in range(2):
                    h = 16 * d + 2 * t + e
                    mm = nc.tensor.matmul(PS[:, 4 + m % 2, d * L:d * L + L], ident[0:32, h:h + 1].to_broadcast([32, P]),
                                          ST[0:32, d * L:d * L + L], start=d == 0, stop=True, skip_group_check=True)
                mm.then_inc(S("row_ready"), 1)

            def y_product(n):
                t, e, d = SSD_STEPS[n]
                if n % 4 == 0 and t >= 2:
                    pe.wait_ge(S("y_out"), t - 1)
                if n % 4 == 0 and t % 4 == 0:
                    pe.wait_ge(S("xdt_ready"), 2 + t // 2)
                pe.wait_ge(S("mix_matrix"), n + 1)
                to = PS[64 * e:64 * e + 64, 6 + t % 2, 0:L]
                m = MR[n % 3]
                h = 2 * t + e
                if d == 0:
                    nc.tensor.matmul(to, XDT[:, 0, 0, h], m[:, 0:L], start=True, stop=False,
                                     skip_group_check=True)
                    mm = nc.tensor.matmul(to[:, P:L], XDT[:, 0, 1, h], m[:, L:L + P], start=False, stop=False,
                                          skip_group_check=True)
                else:
                    nc.tensor.matmul(to[:, 0:P], XDT[:, 1, 0, h], m[:, 0:P], start=False, stop=False,
                                     skip_group_check=True)
                    mm = nc.tensor.matmul(to, XDT[:, 1, 1, h], m[:, P:L + P], start=False, stop=True,
                                          skip_group_check=True)
                mm.then_inc(S("y_product"), 1)

            def pool_product(g):
                pe.wait_ge(evacuated, 2 + 6)
                pe.wait_ge(S("mixed_ready"), g + 1)
                pe.wait_ge(S("poolw_landed"), 16)
                if g >= 2:
                    pe.wait_ge(S("pool_scaled"), g - 1)
                for f in range(2):
                    for t in range(2):
                        mm = nc.tensor.matmul(PS[:, 2 + g % 2, f * L:f * L + L], PW[:, g, t, f * P:f * P + P],
                                              MIXED[:, 2 * g + t], start=f == 0 and t == 0, stop=t == 1,
                                              skip_group_check=True)
                mm.then_inc(S("pool_product"), 1)

            def y_stat(g):
                pe.wait_ge(S("pool_scaled"), 3 + g)
                pe.wait_ge(S("y_sq"), g + 1)
                for t in range(4 * g, 4 * g + 4):
                    mm = nc.tensor.matmul(PS[:, 2 + g, 0:L], const("ones"), YSQ[:, t], start=t % 4 == 0,
                                          stop=t % 4 == 3, skip_group_check=True)
                mm.then_inc(S("y_stat"), 1)

            late, tail = beside(
                [(2, dt_product, None), (12, cb_product, None), (13, cumulate, None)] +
                [(at + 5, y_product, n) for n, at in enumerate(STEP_AT)] +
                [(at, x_turn, x) for x, at in TURN_AT.items()] +
                [(at, rows, m) for m, at in enumerate(PAIR_AT)] +
                [(at, pool_product, g) for g, at in enumerate(POOL_AT)] +
                [(56, y_stat, 0), (59, y_stat, 1)], "in", IN_END)
            stream_pe(pe, "in", split_rhs(XS), normed("mix_pre"), late=late)
            tail()
            all_evacuated(pe, "in")
            pe.wait_ge(S("y_std"), 2)
            stream_pe(pe, "out", lambda j, k: (XS[:, (k + 8) % KT, 0], XS[:, (k + 8) % KT, 1]),
                      lambda q: pe.wait_ge(S("mix_split"), q + 1))
            stat_pe(pe, "mix_post", OSQ1, 4)
            stat_pe(pe, "ffn_pre", SQ, 4)
            stream_pe(pe, "up", split_rhs(XS), normed("ffn_pre"))
            stream_pe(pe, "down", split_rhs(HID), lambda q: pe.wait_ge(S("hidden_split"), q + 1))

            def p_turn():
                all_evacuated(pe, "down")
                pe.wait_ge(S("p_landed"), 32)
                for t in range(2):
                    for c in range(2):
                        ins = nc.tensor.transpose(PS[:, 5, t * L + c * P:t * L + c * P + P],
                                                  PNAT[:, c, t * P:t * P + P], ident)
                ins.then_inc(S("p_turned"), 1)

            stat_pe(pe, "ffn_post", OSQ2, 4, between=p_turn)
            pe.wait_ge(S("p_split"), 1)
            stream_pe(pe, "ple", split_rhs(PSP))
            stat_pe(pe, "ple_pre", SQ, 4)
            stream_pe(pe, "gate", split_rhs(XS), normed("ple_pre"))
            stat_pe(pe, "ple_post", OSQ3, 4)
            pe.wait_ge(norm_std, so_far("ple_post", "std", 1))
            all_evacuated(pe, "gate")
            pe.wait_ge(S("ctx_landed"), 32)
            turn(CNAT, "ctx_turned")
            pe.wait_ge(S("ctx_loaded"), 2)
            stat_pe(pe, "norm1", SQ, 4)
            stat_pe(pe, "norm_c", CTX_SQ, 4, bank=5)

            def head_stat(i):
                x, n, _, kind, _ = HEADS[i]
                if i >= 2:
                    pe.wait_ge(S("heads_act"), i - 1)
                if kind == "v":
                    heads_landed(pe, i)
                    for c in range(4):
                        ins = nc.tensor.transpose(PS[:, 4 + i % 2, c * P:c * P + P], x[:, c * P:c * P + P], ident)
                    ins.then_inc(S("heads_pe"), 1)
                    return
                m = QK_BEFORE[i]
                pe.wait_ge(S("qk_sq"), m + 1)
                nc.tensor.matmul(PS[:, 4 + i % 2, 0:n], const("ones" if kind == "a" else "half"),
                                 QK_SQ[:, m % 2, 0:n], start=True, stop=True,
                                 skip_group_check=True).then_inc(S("heads_pe"), 1)

            def head_turn(i):
                x, _, _, kind, _ = HEADS[i]
                if kind == "v":
                    return
                m = QK_BEFORE[i]
                pe.wait_ge(S("qk_normed"), m + 1)
                if m >= 2:
                    pe.wait_ge(S("qk_roped"), m - 1)
                nc.tensor.matmul(PS[:, 6 + m % 2, 0:L], const("rot_" + kind), x[:, 0:L], start=True,
                                 stop=True, skip_group_check=True).then_inc(S("qk_turned"), 1)

            late, tail = beside(per_head([(2, head_stat), (6, head_turn)]), "kv", HEADS_END)
            kv_stream(pe, late)
            all_evacuated(pe, "kv")
            pe.wait_ge(S("kv_half"), 7)
            stream_pe(pe, "q", split_rhs(XS), late=late)
            tail()
            all_evacuated(pe, "q")
            pe.wait_ge(S("qk_roped"), len(QK_ITEM))
            pe.wait_ge(S("heads_act"), len(HEADS))

            def scores(rd):
                br, h, qb = ROUNDS[rd]
                for i, n in enumerate(JOBS[rd]):
                    if n >= 4:
                        pe.wait_ge(S("exp_ready"), n - 3)
                    if br == "a":
                        q, k = Q[:, h, qb * P:qb * P + P], KV[:, h // 4]
                    else:
                        rows = slice(64 * i, 64 * i + 64)
                        q, k = Q[rows, 16 + h, qb * P:qb * P + P], KV[rows, 8 + h]
                    nc.tensor.matmul(PS[:, 2 + n % 4, :], q, k, start=True, stop=True,
                                     skip_group_check=True).then_inc(S("scores_ready"), 1)

            def values(hd):
                j = 4 + hd // 4 if hd < 16 else hd
                pe.wait_ge(S("pt_ready"), 2 * hd + 2)
                if hd >= 2:
                    pe.wait_ge(S("o_ready"), hd - 1)
                for c in range(4):
                    mm = nc.tensor.matmul(PS[:, hd % 2, 0:L], KV[:, j, c * P:c * P + P], PTT[:, hd % 2, c],
                                          start=c == 0, stop=c == 3, skip_group_check=True)
                mm.then_inc(S("pv_done"), 1)

            scores(0)
            scores(1)
            for rd in range(len(ROUNDS)):
                if rd + 2 < len(ROUNDS):
                    scores(rd + 2)
                pe.wait_ge(S("p_ready"), rd + 1)
                if rd >= 2:
                    pe.wait_ge(S("pt_ready"), rd - 1)
                for c in range(4):
                    ins = nc.tensor.transpose(PS[:, 6 + rd % 2, c * P:c * P + P],
                                              PR[:, JOBS[rd][0] % 4, c * P:c * P + P], ident)
                ins.then_inc(S("p_turn"), 1)
                if rd % 2 == 0 and rd >= 2:
                    values(rd // 2 - 1)
            values(23)
            for i in range(8):
                pe.wait_ge(S("sub_sq"), i // 4 + 1)
                for c in range(2):
                    mm = nc.tensor.matmul(PS[:, 2, 2 * i + c:2 * i + c + 1], SUBSQ[:, i, c * P:c * P + P],
                                          const("ones")[:, 0:1], start=i == 0 and c == 0, stop=True,
                                          skip_group_check=True)
            mm.then_inc(S("sub_stat"), 1)
            pe.wait_ge(S("sub_recip"), 1)
            for i in range(8):
                for c in range(2):
                    at = (i % 2) * L + c * P
                    mm = nc.tensor.matmul(PS[:, 4 + i // 2, at:at + P],
                                          SUB_ROOT[:, 2 * i + c:2 * i + c + 1].to_broadcast([P, P]), ident,
                                          start=at == 0, stop=True, skip_group_check=True)
            mm.then_inc(S("sub_spread"), 1)
            branch_rhs = [split_rhs(XS), split_rhs(OS), split_rhs(XS), split_rhs(OS, KT)]
            stream_pe(pe, "branch", lambda j, k: branch_rhs[j](j, k),
                      first=lambda j: pe.wait_ge(S("o_split"), 6) if j == 1 else None)
            stream_pe(pe, "out2", split_rhs(XS), lambda q: pe.wait_ge(S("merged_split"), q + 1))
            stat_pe(pe, "norm2", SQ, 4)
            stream_pe(pe, "up2", split_rhs(XS), normed("norm2"))
            stream_pe(pe, "down2", split_rhs(HID), lambda q: pe.wait_ge(S("hidden2_split"), q + 1))
            all_evacuated(pe, "down2")
            for c in range(2):
                for t in range(KT):
                    ins = nc.tensor.transpose(PS[:, 4 * c + t // 4, (t % 4) * P:(t % 4) * P + P],
                                              H[:, t, c * P:c * P + P], ident)
                ins.then_inc(S("out_turned"), 1)


NAMES = [
    "x", "p", "mix_norm_pre", "mix_norm_post", "w_in", "ssd_conv_w", "ssd_conv_b", "ssd_dt_bias",
    "ssd_a_log", "ssd_d", "ssd_norm", "pool_w", "pool_scale", "w_out", "ffn_norm_pre",
    "ffn_norm_post", "w_ffn_up", "ffn_conv_w", "ffn_conv_b", "w_ffn_down", "ple_norm_pre",
    "w_ple_gate", "w_ple", "ple_norm_post", "c_2", "ctx_2", "c_ctx_2", "w_ada_2", "b_ada_2",
    "norm1_g_2", "w_in_2", "q_norm_a_2", "k_norm_a_2", "q_norm_b_2", "k_norm_b_2", "lam_q1_2",
    "lam_k1_2", "lam_q2_2", "lam_k2_2", "subln_g_2", "w_br_a_2", "w_br_b_2", "w_out_2",
    "norm2_g_2", "w_ff_gate_2", "w_ff_up_2", "w_ff_down_2",
]


def kernel(**inputs):
    import concourse.bacc as bacc
    from concourse.bass_utils import run_bass_kernel_spmd

    nc = bacc.Bacc("TRN2", target_bir_lowering=False, num_devices=1)
    arrays, aps = {}, {}
    for name in NAMES:
        a = np.ascontiguousarray(inputs[name])
        arrays[f"in_{name}"] = a
        aps[name] = nc.dram_tensor(f"in_{name}", a.shape, F32, kind="ExternalInput").ap()
    tables = []
    for name, a in zip(("constants", "inverse_counts"), constant_tables()):
        arrays[f"in_{name}"] = a
        tables.append(nc.dram_tensor(f"in_{name}", a.shape, F32, kind="ExternalInput").ap())
    out = nc.dram_tensor("out", (1, L, D), F32, kind="ExternalOutput").ap()
    build(nc, aps, out, tables)
    got = run_bass_kernel_spmd(nc, [arrays], core_ids=[0])
    return got.results[0]["out"]
```
